# Optimizing a Trainium2 kernel written in Bass

```python
import math
import jax, jax.numpy as jnp
from jax import lax
import numpy as np

D_MODEL = 1024
BATCH = 1
SEQ = 512
DEPTH = 2

GDN_HEADS = 4
GDN_DK = 128
GDN_DV = 128
GDN_CONV = 4
GDN_CHUNK = 64
DSWA_GROUPS = ((128, 1), (512, 4), (2048, 16))
DSWA_HEADS_PER_GROUP = 3
DSWA_HEADS = 9
DSWA_DH = 64
DSWA_BLOCK = 128
ROPE_THETA = 500000.0
ROPE_DIM = DSWA_DH // 4
SB_HEADS = 8
SB_DH = 64
SB_BLOCK = 128
RET_HEADS = 4
RET_DK = 64
RET_DV = 128
RET_CHUNK = 64
RET_THETA = 10000.0
N_BRANCH = 4
D_FF = 4 * D_MODEL
NORM_EPS = 1e-6

COL_SIZES = (
    2 * GDN_HEADS * GDN_DK + GDN_HEADS * GDN_DV,
    GDN_HEADS * GDN_DV,
    GDN_HEADS,
    GDN_HEADS,
    3 * DSWA_HEADS * DSWA_DH,
    3 * SB_HEADS * SB_DH,
    2 * RET_HEADS * RET_DK,
    RET_HEADS * RET_DV,
    RET_HEADS * RET_DV,
    N_BRANCH * D_MODEL,
)
N_IN_COLS = sum(COL_SIZES)

kernel_name = 'hybrid_gated_four_mixer_block'

def rmsnorm(x, w, eps=NORM_EPS):
    xf = x.astype(jnp.float32)
    y = xf * lax.rsqrt(jnp.mean(xf * xf, axis=-1, keepdims=True) + eps)
    return (y * w.astype(jnp.float32)).astype(x.dtype)

def l2norm(x, eps=1e-6):
    xf = x.astype(jnp.float32)
    return xf * lax.rsqrt(jnp.sum(xf * xf, axis=-1, keepdims=True) + eps)

def split_cols(t, sizes):
    return jnp.split(t, list(np.cumsum(sizes)[:-1]), axis=-1)

def rope_tables(positions, inv_freq):
    ang = positions.astype(jnp.float32)[:, None] * inv_freq[None, :]
    return jnp.cos(ang), jnp.sin(ang)

def apply_rope(x, cos, sin):
    half = cos.shape[-1]
    r = 2 * half
    c = cos[:, None, :].astype(x.dtype)
    s = sin[:, None, :].astype(x.dtype)
    x1, x2, rest = x[..., :half], x[..., half:r], x[..., r:]
    return jnp.concatenate([x1 * c - x2 * s, x2 * c + x1 * s, rest], axis=-1)

def causal_dwconv(x, w):
    K, C = w.shape
    return lax.conv_general_dilated(
        x, w[:, None, :].astype(x.dtype), window_strides=(1,), padding=((K - 1, 0),),
        dimension_numbers=('NWC', 'WIO', 'NWC'), feature_group_count=C)

def gated_delta_chunked(q, k, v, beta, g):
    f32 = jnp.float32
    B, H, S, DK = q.shape
    DV = v.shape[-1]
    C = GDN_CHUNK
    N = S // C
    q = q.reshape(B, H, N, C, DK).astype(f32)
    k = k.reshape(B, H, N, C, DK).astype(f32)
    v = v.reshape(B, H, N, C, DV).astype(f32)
    beta = beta.reshape(B, H, N, C).astype(f32)
    gc = jnp.cumsum(g.reshape(B, H, N, C).astype(f32), axis=-1)
    idx = jnp.arange(C)
    incl = idx[:, None] >= idx[None, :]
    strict = idx[:, None] > idx[None, :]
    decay = jnp.exp(jnp.where(incl, gc[..., :, None] - gc[..., None, :], -jnp.inf))
    k_beta = k * beta[..., None]
    v_beta = v * beta[..., None]
    lower = jnp.where(strict, jnp.einsum('bhncd,bhnsd->bhncs', k_beta, k) * decay, 0.0)
    eye = jnp.eye(C, dtype=f32)
    t_inv = lax.linalg.triangular_solve(eye + lower, jnp.broadcast_to(eye, lower.shape),
                                        left_side=True, lower=True, unit_diagonal=True)
    u = jnp.einsum('bhncs,bhnsd->bhncd', t_inv, v_beta)
    w = jnp.einsum('bhncs,bhnsd->bhncd', t_inv, k_beta * jnp.exp(gc)[..., None])
    attn = jnp.einsum('bhncd,bhnsd->bhncs', q, k) * decay
    q_dec = q * jnp.exp(gc)[..., None]
    g_last = gc[..., -1]
    k_dec = k * jnp.exp(g_last[..., None] - gc)[..., None]

    def step(state, inp):
        q_c, k_c, u_c, w_c, a_c, gl = inp
        v_new = u_c - jnp.einsum('bhcd,bhde->bhce', w_c, state)
        o = jnp.einsum('bhcd,bhde->bhce', q_c, state) + jnp.einsum('bhcs,bhse->bhce', a_c, v_new)
        state = state * jnp.exp(gl)[..., None, None] + jnp.einsum('bhcd,bhce->bhde', k_c, v_new)
        return state, o

    xs = tuple(jnp.moveaxis(t, 2, 0) for t in (q_dec, k_dec, u, w, attn, g_last))
    _, o = lax.scan(step, jnp.zeros((B, H, DK, DV), f32), xs)
    return jnp.moveaxis(o, 0, 2).reshape(B, H, S, DV)

def dilated_window_attn(q, k, v, dilation, lookback):
    B, S, H, D = q.shape
    L = S // dilation
    BL = DSWA_BLOCK
    nb = -(-L // BL)
    Lp = nb * BL

    def strided(t):
        t = t.reshape(B, L, dilation, H, D).transpose(0, 2, 3, 1, 4)
        t = jnp.pad(t, ((0, 0), (0, 0), (0, 0), (0, Lp - L), (0, 0)))
        return t.reshape(B, dilation, H, nb, BL, D)

    def with_prev(t):
        prev = jnp.pad(t, ((0, 0), (0, 0), (0, 0), (1, 0), (0, 0), (0, 0)))[:, :, :, :-1]
        return jnp.concatenate([prev, t], axis=4)

    qb = strided(q)
    kk = with_prev(strided(k))
    vv = with_prev(strided(v))
    s = jnp.einsum('bghnqd,bghnkd->bghnqk', qb, kk).astype(jnp.float32)
    blk = jnp.arange(nb)[:, None]
    qi = blk * BL + jnp.arange(BL)[None, :]
    kj = (blk - 1) * BL + jnp.arange(2 * BL)[None, :]
    rel = qi[:, :, None] - kj[:, None, :]
    mask = (rel >= 0) & (rel <= lookback) & (kj[:, None, :] >= 0)
    s = jnp.where(mask, s, -jnp.inf)
    lse = jax.nn.logsumexp(s, axis=-1)
    p = jnp.exp(s - lse[..., None])
    o = jnp.einsum('bghnqk,bghnkd->bghnqd', p.astype(v.dtype), vv)
    o = o.reshape(B, dilation, H, Lp, D)[:, :, :, :L].transpose(0, 3, 1, 2, 4).reshape(B, S, H, D)
    lse = lse.reshape(B, dilation, H, Lp)[..., :L].transpose(0, 3, 1, 2).reshape(B, S, H)
    return o, lse

def stick_breaking_attn(q, k, v):
    B, H, S, D = q.shape
    nb = S // SB_BLOCK
    qb = q.reshape(B, H, nb, SB_BLOCK, D).transpose(2, 0, 1, 3, 4)
    kpos = jnp.arange(S)

    def block(args):
        q_blk, n = args
        z = jnp.einsum('bhqd,bhkd->bhqk', q_blk, k).astype(jnp.float32)
        qpos = n * SB_BLOCK + jnp.arange(SB_BLOCK)
        mask = kpos[None, :] < qpos[:, None]
        log_one_minus = jnp.where(mask, jax.nn.log_sigmoid(-z), 0.0)
        suffix = lax.cumsum(log_one_minus, axis=3, reverse=True) - log_one_minus
        a = jnp.where(mask, jnp.exp(jax.nn.log_sigmoid(z) + suffix), 0.0)
        return jnp.einsum('bhqk,bhkd->bhqd', a.astype(v.dtype), v)

    o = lax.map(block, (qb, jnp.arange(nb)))
    return o.transpose(1, 2, 0, 3, 4).reshape(B, H, S, D)

def retention_chunked(q, k, v, log_gamma):
    f32 = jnp.float32
    B, H, S, DK = q.shape
    DV = v.shape[-1]
    C = RET_CHUNK
    N = S // C
    q = q.reshape(B, H, N, C, DK).astype(f32)
    k = k.reshape(B, H, N, C, DK).astype(f32)
    v = v.reshape(B, H, N, C, DV).astype(f32)
    idx = jnp.arange(C, dtype=f32)
    diff = idx[:, None] - idx[None, :]
    lg = log_gamma[:, None, None]
    dmat = jnp.exp(jnp.where(diff[None] >= 0, diff[None] * lg, -jnp.inf))
    intra = jnp.einsum('bhncd,bhnsd->bhncs', q, k) * dmat[:, None]
    intra_o = jnp.einsum('bhncs,bhnse->bhnce', intra, v)
    xi = jnp.exp((idx + 1.0)[None, :] * log_gamma[:, None])
    zeta = jnp.exp((C - 1.0 - idx)[None, :] * log_gamma[:, None])
    chunk_decay = jnp.exp(C * log_gamma)
    kz = k * zeta[None, :, None, :, None]

    def step(r, inp):
        q_c, kz_c, v_c = inp
        cross = jnp.einsum('bhcd,bhde->bhce', q_c, r)
        r = r * chunk_decay[None, :, None, None] + jnp.einsum('bhcd,bhce->bhde', kz_c, v_c)
        return r, cross

    xs = tuple(jnp.moveaxis(t, 2, 0) for t in (q, kz, v))
    _, cross = lax.scan(step, jnp.zeros((B, H, DK, DV), f32), xs)
    o = intra_o + jnp.moveaxis(cross, 0, 2) * xi[None, :, None, :, None]
    return o.reshape(B, H, S, DV)

def hybrid_layer(x, rope_cs, ret_cs, n_pre_mix, n_post_mix, n_pre_mlp, n_post_mlp, w_in, conv_w,
                 a_log, dt_bias, gdn_norm, ret_norm, w_br_a, w_br_b, w_br_c, w_br_d, w_o,
                 w_mlp_in, w_mlp_out):
    f32 = jnp.float32
    B, S, _ = x.shape

    def to_heads(t, n_heads):
        return t.reshape(B, S, n_heads, -1).transpose(0, 2, 1, 3)

    h = rmsnorm(x, n_pre_mix)
    proj = h @ w_in
    (gdn_qkv, gdn_z, gdn_a, gdn_b, dswa_qkv, sb_qkv, ret_qk, ret_v, ret_g, gates) = split_cols(proj, COL_SIZES)

    qkv = jax.nn.silu(causal_dwconv(gdn_qkv, conv_w))
    qa, ka, va = jnp.split(qkv, [GDN_HEADS * GDN_DK, 2 * GDN_HEADS * GDN_DK], axis=-1)
    qa = l2norm(to_heads(qa, GDN_HEADS)) * GDN_DK ** -0.5
    ka = l2norm(to_heads(ka, GDN_HEADS))
    va = to_heads(va, GDN_HEADS)
    beta = jax.nn.sigmoid(gdn_b.astype(f32)).transpose(0, 2, 1)
    g = (-jnp.exp(a_log.astype(f32)) * jax.nn.softplus(gdn_a.astype(f32) + dt_bias.astype(f32))).transpose(0, 2, 1)
    oa = gated_delta_chunked(qa, ka, va, beta, g).transpose(0, 2, 1, 3)
    oa = rmsnorm(oa, gdn_norm) * jax.nn.silu(gdn_z.reshape(B, S, GDN_HEADS, GDN_DV).astype(f32))
    y_a = oa.reshape(B, S, -1).astype(x.dtype) @ w_br_a

    qb, kb, vb = [t.reshape(B, S, DSWA_HEADS, DSWA_DH) for t in jnp.split(dswa_qkv, 3, axis=-1)]
    cos_p, sin_p = rope_cs
    qb = apply_rope(qb, cos_p, sin_p) * DSWA_DH ** -0.5
    kb = apply_rope(kb, cos_p, sin_p)
    outs, lses = [], []
    for gi, (window, dil) in enumerate(DSWA_GROUPS):
        hs = slice(gi * DSWA_HEADS_PER_GROUP, (gi + 1) * DSWA_HEADS_PER_GROUP)
        o_g, lse_g = dilated_window_attn(qb[:, :, hs], kb[:, :, hs], vb[:, :, hs], dil, window // dil)
        outs.append(o_g)
        lses.append(lse_g)
    alpha = jax.nn.softmax(jnp.stack(lses, axis=2), axis=2)
    ob = (jnp.stack(outs, axis=2) * alpha[..., None]).reshape(B, S, -1).astype(x.dtype)
    y_b = ob @ w_br_b

    qc, kc, vc = [to_heads(t, SB_HEADS) for t in jnp.split(sb_qkv, 3, axis=-1)]
    oc = stick_breaking_attn(qc * SB_DH ** -0.5, kc, vc).transpose(0, 2, 1, 3).reshape(B, S, -1)
    y_c = oc @ w_br_c

    cos_r, sin_r = ret_cs
    qd, kd = jnp.split(ret_qk, 2, axis=-1)
    qd = apply_rope(qd.reshape(B, S, RET_HEADS, RET_DK), cos_r, sin_r)
    kd = apply_rope(kd.reshape(B, S, RET_HEADS, RET_DK), cos_r, sin_r) * RET_DK ** -0.5
    vd = ret_v.reshape(B, S, RET_HEADS, RET_DV)
    log_gamma = jnp.log1p(-jnp.exp2(-5.0 - jnp.arange(RET_HEADS, dtype=f32)))
    od = retention_chunked(qd.transpose(0, 2, 1, 3), kd.transpose(0, 2, 1, 3),
                           vd.transpose(0, 2, 1, 3), log_gamma).transpose(0, 2, 1, 3)
    od = rmsnorm(od, ret_norm) * jax.nn.silu(ret_g.reshape(B, S, RET_HEADS, RET_DV).astype(f32))
    y_d = od.reshape(B, S, -1).astype(x.dtype) @ w_br_d

    g_a, g_b, g_c, g_d = jnp.split(jax.nn.sigmoid(gates), N_BRANCH, axis=-1)
    mixed = (g_a * y_a + g_b * y_b + g_c * y_c + g_d * y_d) @ w_o
    x = x + rmsnorm(mixed, n_post_mix)

    h2 = rmsnorm(x, n_pre_mlp)
    f = jnp.square(jax.nn.relu(h2 @ w_mlp_in)) @ w_mlp_out
    return x + rmsnorm(f, n_post_mlp)

def setup_inputs(seed: int = 0) -> dict:
    key = jax.random.key(seed)
    ks = jax.random.split(key, 20)
    f32 = jnp.float32

    def dense(k, shape, fan_in):
        return jax.random.normal(k, shape, f32) * fan_in ** -0.5

    def gain(k, shape):
        return 1.0 + 0.05 * jax.random.normal(k, shape, f32)

    dt = jnp.exp(jax.random.uniform(ks[8], (DEPTH, GDN_HEADS), f32, math.log(1e-3), math.log(1e-1)))
    return {
        'x': jax.random.normal(ks[0], (BATCH, SEQ, D_MODEL), f32),
        'norm_pre_mix': gain(ks[1], (DEPTH, D_MODEL)),
        'norm_post_mix': gain(ks[2], (DEPTH, D_MODEL)),
        'norm_pre_mlp': gain(ks[3], (DEPTH, D_MODEL)),
        'norm_post_mlp': gain(ks[4], (DEPTH, D_MODEL)),
        'w_in': dense(ks[5], (DEPTH, D_MODEL, N_IN_COLS), D_MODEL),
        'conv_w': dense(ks[6], (DEPTH, GDN_CONV, COL_SIZES[0]), GDN_CONV),
        'a_log': jnp.log(jax.random.uniform(ks[7], (DEPTH, GDN_HEADS), f32, 1.0, 16.0)),
        'dt_bias': dt + jnp.log(-jnp.expm1(-dt)),
        'gdn_norm': gain(ks[9], (DEPTH, GDN_DV)),
        'ret_norm': gain(ks[10], (DEPTH, RET_DV)),
        'w_br_a': dense(ks[11], (DEPTH, GDN_HEADS * GDN_DV, D_MODEL), GDN_HEADS * GDN_DV),
        'w_br_b': dense(ks[12], (DEPTH, DSWA_HEADS * DSWA_DH, D_MODEL), DSWA_HEADS * DSWA_DH),
        'w_br_c': dense(ks[13], (DEPTH, SB_HEADS * SB_DH, D_MODEL), SB_HEADS * SB_DH),
        'w_br_d': dense(ks[14], (DEPTH, RET_HEADS * RET_DV, D_MODEL), RET_HEADS * RET_DV),
        'w_o': dense(ks[15], (DEPTH, D_MODEL, D_MODEL), D_MODEL),
        'w_mlp_in': dense(ks[16], (DEPTH, D_MODEL, D_FF), D_MODEL),
        'w_mlp_out': dense(ks[17], (DEPTH, D_FF, D_MODEL), D_FF),
    }

def reference(x, norm_pre_mix, norm_post_mix, norm_pre_mlp, norm_post_mlp, w_in, conv_w, a_log,
              dt_bias, gdn_norm, ret_norm, w_br_a, w_br_b, w_br_c, w_br_d, w_o, w_mlp_in, w_mlp_out):
    f32 = jnp.float32
    pos = jnp.arange(x.shape[1], dtype=jnp.int32)
    rope_cs = rope_tables(pos, ROPE_THETA ** (-jnp.arange(0, ROPE_DIM, 2, dtype=f32) / ROPE_DIM))
    ret_cs = rope_tables(pos, RET_THETA ** (-jnp.linspace(0.0, 1.0, RET_DK // 2, dtype=f32)))
    for l in range(DEPTH):
        x = hybrid_layer(x, rope_cs, ret_cs, norm_pre_mix[l], norm_post_mix[l], norm_pre_mlp[l],
                         norm_post_mlp[l], w_in[l], conv_w[l], a_log[l], dt_bias[l], gdn_norm[l],
                         ret_norm[l], w_br_a[l], w_br_b[l], w_br_c[l], w_br_d[l], w_o[l],
                         w_mlp_in[l], w_mlp_out[l])
    return x


_drawn_inputs = setup_inputs


def setup_inputs(seed=0):
    import zlib

    import numpy as np

    out = dict(_drawn_inputs(seed))
    spreads = {}
    factors = {}
    for name, (base, spread) in spreads.items():
        noise = np.random.default_rng([zlib.crc32(name.encode()), seed]).standard_normal(out[name].shape)
        drawn = base * np.exp(spread * noise) if base else spread * noise
        out[name] = __import__('jax').numpy.asarray(drawn.astype(out[name].dtype))
    for name, factor in factors.items():
        out[name] = (out[name] * factor).astype(out[name].dtype)
    return out
```

```python
import math
from contextlib import ExitStack

import numpy as np
import concourse.bass as bass
from concourse import mybir

F32 = mybir.dt.float32
F32R = mybir.dt.float32r
BF16 = mybir.dt.bfloat16
ALU = mybir.AluOpType
ACT = mybir.ActivationFunctionType
AX_X = mybir.AxisListType.X

P = 128
S = 512
NT = S // P
DM = 1024
KT = DM // P
DEPTH = 2
FF = 4 * DM
EPS = 1e-6
NEG = -1e30

C_GDN, C_Z, C_AB, C_DSWA, C_SB, C_RET, C_RV, C_RG, C_GATE = np.cumsum(
    [0, 1536, 512, 8, 1728, 1536, 512, 512, 512]).tolist()
GH, DK = 4, 128
DH = 64
SBH = 8
DIL = (1, 4, 4)
UK = 2
STAGES = 4
RING = 4

CI, CTU, CST, CLV, CNTL, CNON, CMG0, CMG1, CMG2, CSEL, CRD, CRR, CEND = np.cumsum(
    [0, P, P, P, 7 * P, P, P, 768, P, P, 3 * DH, P, P]).tolist()
TD, TRC, TRS, TWC, TWS, TEND = np.cumsum([0, 4 * S, S, S, S, S]).tolist()
LN1, LN2, LGN, LRN, LCW, LAL, LDT, LEND = np.cumsum([0, KT, KT, 1, 1, 48, GH, GH]).tolist()


def shape_constants():
    p = np.arange(P)[:, None]
    c = np.arange(P)[None, :]
    one = lambda m: m.astype(np.float32)
    neg = lambda m: np.where(m, 0.0, NEG).astype(np.float32)
    levels = []
    for n in range(7):
        z = 1 << n
        levels.append(one((c // (2 * z) == p // (2 * z)) & (c % (2 * z) >= z) & (p % (2 * z) < z)))
    k = np.arange(2 * P)[None, :]
    near = (k <= p + P) & (k >= p)
    first = (k <= p + P) & (k >= P)
    sel = np.zeros((P, 3 * DH), np.float32)
    for h in range(3):
        sel[h, h * DH:(h + 1) * DH] = 1.0

    def rotation(half):
        r = np.zeros((P, P), np.float32)
        for b in range(0, P, DH):
            for i in range(half):
                r[b + i + half, b + i] = -1.0
                r[b + i, b + i + half] = 1.0
        return r

    consts = np.concatenate(
        [one(p == c), one(c >= p), one(c > p), *levels, -one(c <= p), -np.ones((P, P), np.float32),
         neg(np.concatenate([first, near, near], 1)), neg(c <= p),
         neg((c <= p) & ((p - c) % 4 == 0)), sel, rotation(8), rotation(32)], 1)
    return np.ascontiguousarray(consts.astype(np.float32))


def shape_tables():
    p = np.arange(P)[:, None].astype(np.float64)
    c = np.arange(S)[None, :].astype(np.float64)
    out = []
    for h in range(4):
        lg = math.log1p(-2.0 ** (-5.0 - h))
        out.append(np.where(c >= p, np.exp((c - p) * lg), 0.0) * DH ** -0.5)
    pos = np.arange(S, dtype=np.float32)[None, :]
    lin = np.linspace(0.0, 1.0, 32, dtype=np.float32)
    fr = (np.float64(10000.0) ** -lin.astype(np.float64)).astype(np.float32)
    fw = (np.float64(500000.0) ** (-np.arange(0, 16, 2, dtype=np.float32).astype(np.float64) / 16)).astype(np.float32)
    for f, half in ((fr, 32), (fw, 8)):
        ang = (pos * f[:, None]).astype(np.float32)
        cos, sin = np.ones((DH, S)), np.zeros((DH, S))
        for b in (0, half):
            cos[b:b + half] = np.cos(ang.astype(np.float64))
            sin[b:b + half] = np.sin(ang.astype(np.float64))
        out += [np.tile(cos, (2, 1)), np.tile(sin, (2, 1))]
    return np.ascontiguousarray(np.concatenate(out, 1).astype(np.float32))


class Job:

    def __init__(self, name, w, c0, n, rows, kind, src, tiles=None, perm=0):
        self.name, self.w, self.c0, self.n, self.kind, self.src, self.perm = name, w, c0, n, kind, src, perm
        self.tiles = tiles or (n // P if kind == "T" else NT)
        self.units = []
        r = 0
        while r < rows:
            k = min(UK * P, rows - r)
            self.units.append((r, k))
            r += k


def make_jobs():
    jobs = []

    def add(*a, **k):
        jobs.append(Job(*a, **k))

    def gates(b):
        for hf in range(2):
            add(f"gate{b}{hf}", "w_in", C_GATE + "abcd".index(b) * DM + hf * 512, 512, DM, "T", "h")

    def branch(b, rows):
        for hf in range(2):
            add(f"y{b}{hf}", f"w_br_{b}", hf * 512, 512, rows, "T", "o")

    for n, c in (("aq", 0), ("ak", 512), ("av", 1024)):
        add(n, "w_in", C_GDN + c, 512, DM, "T", "h")
    add("aab", "w_in", C_AB, P, DM, "T", "h")
    gates("a")
    add("az", "w_in", C_Z, 512, DM, "T", "h")
    branch("a", 512)
    add("cq", "w_in", C_SB, 512, DM, "T", "h")
    add("ck", "w_in", C_SB + 512, 512, DM, "T", "h")
    add("cv", "w_in", C_SB + 1024, 512, DM, "N", "h")
    gates("c")
    branch("c", 512)
    add("dqk", "w_in", C_RET, 512, DM, "T", "h")
    add("dv", "w_in", C_RV, 512, DM, "N", "h")
    add("dg", "w_in", C_RG, 512, DM, "T", "h")
    gates("d")
    branch("d", 512)
    for i, n in enumerate("qk"):
        add(f"b{n}0", "w_in", C_DSWA + 576 * i, 512, DM, "T", "h")
        add(f"b{n}1", "w_in", C_DSWA + 576 * i + 512, P, DM, "T", "h")
    for g in range(3):
        add(f"bv{g}", "w_in", C_DSWA + 1152 + 192 * g, 192, DM, "N", "h", perm=g)
    gates("b")
    branch("b", 576)
    for hf in range(2):
        add(f"o{hf}", "w_o", hf * 512, 512, DM, "N", "h")
    for g in range(FF // 512):
        add(f"up{g}", "w_mlp_in", g * 512, 512, DM, "T", "h")
    for hf in range(2):
        add(f"dn{hf}", "w_mlp_out", hf * 512, 512, FF, "N", "f")
    return jobs


JOBS = make_jobs()
JOB = {j.name: j for j in JOBS}
UNITS = [(j, i) for j in JOBS for i in range(len(j.units))]


def number(keys, banks):
    return {k: (i % banks, i // banks + 1) for i, k in enumerate(keys)}


DN0 = next(i for i, (j, _) in enumerate(UNITS) if j.name == "dn0")
BIG = number([(j.name, t) for j in JOBS for t in range(j.tiles)], 4)


def window_units():
    out = []
    for g in range(3):
        for h in range(3):
            if g == 0:
                out += [(g, h, 0, 2, 2 * P), (g, h, 2, 2, 2 * P)]
            else:
                out.append((g, h, 0, 4, P))
    return out


WU = window_units()
LEVELS = 7


def mixer_keys():
    k = [("pre1", i) for i in range(KT)]
    k += [("l2", i) for i in range(8)]
    k += ["ab", "gc"]
    for b in range(NT):
        k += [("R", b), ("B", b), ("LT", b), ("att", b), ("T0", b), ("kn", b), ("vn", b)]
        for n in range(1, LEVELS):
            k += [("Y", b, n)] + ([("X", b, n)] if n < LEVELS - 1 else []) + [("XT", b, n)]
        k += [("ks", b), ("new", b), ("o", b), ("dS", b)]
    k += [("an", h) for h in range(4)]
    for h in range(SBH + 1):
        for j in reversed(range(NT)):
            if h < SBH:
                k.append(("z", h, j))
        if h >= 1:
            k += [("cs", h - 1, j) for j in range(NT)]
            if h % 2 == 0:
                k.append(("cpv", h // 2 - 1))
    k += [("drot", i) for i in range(4)]
    for h in range(4):
        k += [("dz", h, j) for j in range(NT)] + [("dpv", h), ("dn", h)]
    k += [("brot", i) for i in range(10)]
    for i in range(len(WU) + 2):
        if i < len(WU):
            k.append(("sc", i))
        if 1 <= i <= len(WU):
            k.append(("pt", i - 1))
        if i >= 2:
            k.append(("wpv", i - 2))
    k += [("st", n, g) for n in range(2) for g in range(3)]
    k += [("bf", t) for t in range(5)]
    k += [("pre2", i) for i in range(KT)]
    return k


MIX = number(mixer_keys(), 4)


def hybrid_kernel(nc, ins, out):
    ctx = ExitStack()
    with ctx:
        def sb(name, n, dt=F32):
            return ctx.enter_context(nc.sbuf_tensor(name, [P, n], dt))

        x_sb = sb("x_sb", NT * DM)
        h_hi, h_lo = sb("h_hi", KT * S, F32R), sb("h_lo", KT * S, F32R)
        o_hi, o_lo = sb("o_hi", 5 * S, F32R), sb("o_lo", 5 * S, F32R)
        stage = sb("stage", STAGES * UK * S)
        ring_hi, ring_lo = sb("ring_hi", RING * UK * S, F32R), sb("ring_lo", RING * UK * S, F32R)
        consts = sb("consts", CEND)
        ones = sb("ones", P)
        idb, strictb = sb("idb", P, BF16), sb("strictb", P, BF16)
        lw = sb("lw", LEND)
        st = sb("st", 320)
        scr = sb("scr", 19712)
        big = [ctx.enter_context(nc.psum_tensor(f"big{i}", [P, S], F32)) for i in range(4)]
        mxb = [ctx.enter_context(nc.psum_tensor(f"mix{i}", [P, S], F32)) for i in range(4)]

        def at(t, base, k, n, w=S):
            return t[:, base + k * w:base + k * w + n]

        xv = x_sb[:, :].rearrange("p (t d) -> p t d", t=NT)
        hH, hL = (t[:, :].rearrange("p (k s) -> p k s", s=S) for t in (h_hi, h_lo))
        oH, oL = (t[:, :].rearrange("p (k s) -> p k s", s=S) for t in (o_hi, o_lo))
        rH, rL = (t[:, :].rearrange("p (r k s) -> p r k s", r=RING, s=S) for t in (ring_hi, ring_lo))
        stg = stage[:, :].rearrange("p (r k s) -> p r k s", r=STAGES, s=S)
        ident = consts[:, CI:CI + P]
        triu = consts[:, CTU:CTU + P]
        strict = consts[:, CST:CST + P]

        def sview(base, k, w=S):
            return scr[:, base:base + k * w].rearrange("p (k w) -> p k w", w=w)

        mixed, sg = sview(0, KT), sview(4096, KT)
        MB = 8192
        fT = sview(0, FF // P)
        hn = scr[:, MB:MB + 4096].rearrange("p (t d) -> p t d", t=NT)
        yhalf = (sview(FF // P * S, NT), sview(0, NT))
        junk = scr[:, FF // P * S + 2048:FF // P * S + 2048 + DM]
        postw = scr[:, 4096:4096 + DM]
        ytmp = sview(4096 + DM, 2)
        aQ, aK, aV = sview(MB, 4), sview(MB + 2048, 4), sview(MB + 4096, 4)
        (g_eR, g_dec, g_kb, g_LT, g_att, g_LTm, g_T, g_U, g_Y, g_kd) = (
            scr[:, MB + 6144 + i * S:MB + 6144 + (i + 1) * S].rearrange("p (h c) -> p h c", h=GH) for i in range(10))
        g_S = scr[:, 0:S].rearrange("p (h c) -> p h c", h=GH)
        g_sq, g_rs = sview(S, 2), sview(3 * S, 2)
        g_ab = scr[0:8, 5 * S:6 * S]
        g_cv = sview(6 * S, 2)
        g_vb = scr[:, 6 * S:7 * S].rearrange("p (h c) -> p h c", h=GH)
        cQ, cK = sview(MB, 4), sview(MB + 2048, 4)
        cV = sview(MB + 4096, 4)
        OFF = [0, 512, 896, 1152]
        c_sp = [scr[:, MB + 6144 + i * 1280:MB + 6144 + (i + 1) * 1280] for i in range(2)]
        c_A = [scr[:, MB + 8704 + i * 1280:MB + 8704 + (i + 1) * 1280] for i in range(2)]
        dQK, dV, dG = sview(MB, 4), sview(MB + 2048, 4), sview(MB + 4096, 4)
        dTab = scr[:, MB + 6144:MB + 6144 + 3072]
        dX, dY = sview(MB + 9216, 2), sview(MB + 10240, 2)
        dP = sview(MB + 9216, 4)
        dO, dSq = scr[:, MB + 8192:MB + 8704], scr[:, MB + 8704:MB + 9216]
        bQ, bK = sview(MB, 5), sview(MB + 2560, 5)
        bV = scr[:, MB + 5120:MB + 5120 + 2304].rearrange("p (g b c) -> p g b c", g=3, b=4)
        bP, bPT = sview(MB + 7424, 2), sview(MB + 8448, 2)
        bX = sview(MB + 9472, 2)
        bTab = scr[:, MB + 10496:MB + 11520]
        bFM = scr[0:3, MB + 2560:MB + 2560 + 1536].rearrange("p (g s) -> p g s", g=3)
        bFZ = scr[0:3, MB + 5120:MB + 5120 + 1536].rearrange("p (g s) -> p g s", g=3)
        bFS = scr[0:3, MB + 7424:MB + 7424 + 512]
        n_v, n_y, n_t = (st[:, 4 * i:4 * i + 4] for i in range(3))
        n_ss = st[:, 296:304]
        s16 = [st[:, 16 + 16 * i:32 + 16 * i].rearrange("p (b h) -> p b h", b=4) for i in range(10)]
        s_a, s_e, s_l, s_g, s_be, s_gc, s_ed, s_b1, s_gl, s_ea = s16
        w_m, w_nm, w_z = (st[:, 176 + 36 * i:212 + 36 * i].rearrange("p (g b h) -> p g b h", g=3, b=4) for i in range(3))

        sems = {}

        def sem(name):
            if name not in sems:
                sems[name] = ctx.enter_context(nc.semaphore(name))
            return sems[name]

        once = ctx.enter_context(nc.semaphore("once"))
        idready = ctx.enter_context(nc.semaphore("idready"))

        def big_wait(eng, key):
            b, k = BIG[key]
            eng.wait_ge(sem(f"big_done{b}"), k)
            return big[b]

        def mix_wait(eng, key):
            b, k = MIX[key]
            eng.wait_ge(sem(f"mix_done{b}"), k)
            return mxb[b]

        def big_free(ins_, key):
            return ins_.then_inc(sem(f"big_free{BIG[key][0]}"), 1)

        def mix_free(ins_, key):
            return ins_.then_inc(sem(f"mix_free{MIX[key][0]}"), 1)

        def mix_freed(eng, key):
            b, k = MIX[key]
            eng.wait_ge(sem(f"mix_free{b}"), k)

        def big_freed(eng, key):
            b, k = BIG[key]
            eng.wait_ge(sem(f"big_free{b}"), k)

        def heads(t):
            return t[:, 0:S].rearrange("p (h c) -> p h c", h=GH)

        def f32(ap):
            return ap.bitcast(F32)

        with nc.Block() as block:
            @block.sync
            def _(sp):
                sp.dma_start(xv, ins["x"].rearrange("a (t p) d -> p (a t) d", p=P)).then_inc(once, 16)
                sp.dma_start(consts[:, :], ins["consts"]).then_inc(once, 16)

            @block.vector
            def _(dve):
                nc.vector.memset(ones[:, :], 1.0).then_inc(idready, 1)
                dve.wait_ge(once, 32)
                nc.vector.tensor_copy(idb[:, :], ident).then_inc(idready, 1)
                nc.vector.tensor_scalar(strictb[:, :], strict, -NEG, NEG, ALU.mult, ALU.add).then_inc(idready, 1)

        def build_layer(l, block):
            @block.sync
            def _(sp):
                sp.dma_start(lw[:, :], ins["small"][bass.ds(l, 1), :, :].rearrange("a p n -> p (a n)")).then_inc(sem("small_loaded"), 16)
                for u, (job, i) in enumerate(UNITS):
                    if u >= STAGES:
                        sp.wait_ge(sem("w_ready"), u - STAGES + 1)
                    r0, rows = job.units[i]
                    w = ins[job.w]
                    src = w[bass.ds(l, 1), r0:r0 + rows, job.c0:job.c0 + job.n]
                    s = u % STAGES
                    if rows >= P:
                        sp.dma_start(stg[:, s, 0:rows // P, 0:job.n],
                                     src.rearrange("a (t p) n -> p (a t) n", p=P)).then_inc(sem(f"w_loaded{s}"), 16)
                    else:
                        sp.dma_start(stg[0:rows, s, 0, 0:job.n],
                                     src.rearrange("a p n -> p (a n)")).then_inc(sem(f"w_loaded{s}"), 16)

            @block.gpsimd
            def _(pool):
                for u, (job, i) in enumerate(UNITS):
                    r0, rows = job.units[i]
                    s, r = u % STAGES, u % RING
                    pp, kk = min(rows, P), max(rows // P, 1)
                    pool.wait_ge(sem(f"w_loaded{s}"), 16 * (u // STAGES + 1))
                    if u >= RING:
                        pool.wait_ge(sem("w_used"), u - RING + 1)
                    w = stg[0:pp, s, 0:kk, 0:job.n]
                    nc.gpsimd.tensor_scalar(rH[0:pp, r, 0:kk, 0:job.n], w, 1.0, 0.0, ALU.mult, ALU.add).then_inc(sem("w_hi"), 1)
                    pool.wait_ge(sem("w_hi"), u + 1)
                    nc.gpsimd.tensor_tensor(rL[0:pp, r, 0:kk, 0:job.n], w, f32(rH[0:pp, r, 0:kk, 0:job.n]),
                                            ALU.subtract).then_inc(sem("w_ready"), 1)

            @block.scalar
            def _(act):
                A = nc.scalar.activation

                def norm_stats(parts, ready, tag):
                    for q, src in enumerate(parts):
                        for t in range(NT):
                            ready(q, t)
                            if NT * q + t:
                                act.wait_ge(sem(f"{tag}_ss"), NT * q + t)
                            A(junk[:, 0:DM // len(parts)], src[:, t, :], ACT.Square, scale=DM ** -0.5,
                              accum_out=n_ss[:, NT * q + t:NT * q + t + 1]).then_inc(sem(f"{tag}_ss"), 1)
                    act.wait_ge(sem(f"{tag}_v"), 1)
                    A(n_t, n_v, ACT.Ln).then_inc(sem(f"{tag}_ln"), 1)
                    act.wait_ge(sem(f"{tag}_ln"), 1)
                    A(n_y, n_t, ACT.Exp, scale=-0.5).then_inc(sem(f"{tag}_y"), 1)

                def split_hi(tag, nw, kk=KT):
                    for k in range(kk):
                        ps = mix_wait(act, (tag, k))
                        A(hH[:, k, :], ps[:, :], ACT.Copy, scale=lw[:, nw + k:nw + k + 1]).then_inc(sem(f"{tag}_hi"), 1)

                def gate_copy(b, hf):
                    if hf == 0 and b != "a":
                        prev = {"c": "a", "d": "c", "b": "d"}[b]
                        big_freed(act, (f"y{prev}1", 3))
                    for i in range(4):
                        ps = big_wait(act, (f"gate{b}{hf}", i))
                        big_free(A(sg[:, 4 * hf + i, :], ps[:, :], ACT.Copy), (f"gate{b}{hf}", i))

                def gate_sigmoid(b):
                    for hf in range(2):
                        big_freed(act, (f"gate{b}{hf}", 3))
                        A(sg[:, 4 * hf:4 * hf + 4, :], sg[:, 4 * hf:4 * hf + 4, :], ACT.Sigmoid).then_inc(sem(f"sig{b}"), 1)

                act.wait_ge(sem("small_loaded"), 16)
                norm_stats([xv], lambda q, t: None, "n1")
                split_hi("pre1", LN1)
                for i in range(12):
                    big_freed(act, (("aq", "ak", "av")[i // 4], i % 4))
                    dst = (aQ, aK, aV)[i // 4][:, i % 4, :]
                    A(dst, g_cv[:, i % 2, :], ACT.Silu).then_inc(sem("a_silu"), 1)
                for i in range(8):
                    if i >= 2:
                        mix_freed(act, ("l2", i - 2))
                        act.wait_ge(sem("a_l2"), i - 1)
                    else:
                        act.wait_ge(sem("a_silu"), i + 1)
                    A(g_sq[:, i % 2, :], (aQ, aK)[i // 4][:, i % 4, :], ACT.Square).then_inc(sem("a_sq"), 1)
                    ps = mix_wait(act, ("l2", i))
                    mix_free(A(g_rs[:, i % 2, :], ps[:, :], ACT.Ln, bias=EPS), ("l2", i))
                    mix_freed(act, ("l2", i))
                    A(g_rs[:, i % 2, :], g_rs[:, i % 2, :], ACT.Exp, scale=-0.5).then_inc(sem("a_rs"), 1)
                big_freed(act, ("av", 3))
                ps = big_wait(act, ("aab", 0))
                big_free(A(g_ab, ps[0:8, :], ACT.Copy), ("aab", 0))
                act.wait_ge(sem("a_small"), 2)
                A(s_e, s_e, ACT.Exp, scale=-1.0).then_inc(sem("a_smallact"), 1)
                A(s_be, s_be, ACT.Exp, scale=-1.0).then_inc(sem("a_smallact"), 1)
                A(s_ea[:, 0, :], lw[:, LAL:LAL + GH], ACT.Exp).then_inc(sem("a_smallact"), 1)
                act.wait_ge(sem("a_smallact"), 1)
                A(s_l, s_e, ACT.Ln, bias=1.0).then_inc(sem("a_smallact"), 1)
                for b in range(NT):
                    ps = mix_wait(act, ("R", b))
                    if b:
                        mix_freed(act, ("dS", b - 1))
                    A(g_eR, heads(ps), ACT.Exp).then_inc(sem("a_eR"), 1)
                    act.wait_ge(sem("a_min"), b + 1)
                    A(g_dec, g_dec, ACT.Exp).then_inc(sem("a_dec"), 1)
                    act.wait_ge(sem("a_edarg"), b + 1)
                    A(s_ed[:, b, :], s_ed[:, b, :], ACT.Exp).then_inc(sem("a_ed"), 1)
                    ps = mix_wait(act, ("T0", b))
                    mix_free(A(g_T, heads(ps), ACT.Copy), ("T0", b))
                    for n in range(1, LEVELS):
                        ps = mix_wait(act, ("Y", b, n))
                        mix_free(A(g_Y, heads(ps), ACT.Copy), ("Y", b, n))
                    if b == 0:
                        gate_copy("a", 0)
                    if b == 2:
                        gate_copy("a", 1)
                    ps = mix_wait(act, ("new", b))
                    mix_free(A(g_Y, heads(ps), ACT.Copy), ("new", b))
                    ps = mix_wait(act, ("o", b))
                    mix_free(A(aQ[:, :, b * P:(b + 1) * P], heads(ps), ACT.Copy), ("o", b))
                mix_wait(act, ("dS", NT - 1))
                for i in range(4):
                    ps = big_wait(act, ("az", i))
                    big_free(A(aK[:, i, :], ps[:, :], ACT.Silu), ("az", i))

                def head_norm(h, key, o, sq, rs, tag, prior):
                    prior()
                    A(sq, o, ACT.Square, scale=P ** -0.5).then_inc(sem(f"{tag}_sq"), 1)
                    ps = mix_wait(act, key)
                    mix_free(A(rs, ps[:, :], ACT.Ln, bias=EPS), key)
                    mix_freed(act, key)
                    A(rs, rs, ACT.Exp, scale=-0.5).then_inc(sem(f"{tag}_rs"), 1)

                def o_split(tag, i, src, rows=P):
                    if tag == "b":
                        mix_freed(act, ("bf", i))
                    else:
                        act.wait_ge(sem(f"{tag}_out"), i + 1)
                    if i == 0 and tag != "a":
                        big_freed(act, ({"d": "yc1", "b": "yd1"}[tag], 3))
                    A(oH[0:rows, i, :], src, ACT.Copy).then_inc(sem(f"{tag}_ohi"), 1)

                for h in range(4):
                    def prior():
                        mix_freed(act, ("o", NT - 1))
                        if h >= 2:
                            act.wait_ge(sem("a_out"), h - 1)
                    head_norm(h, ("an", h), aQ[:, h, :], g_sq[:, h % 2, :], g_rs[:, h % 2, :], "an", prior)
                    if h >= 1:
                        o_split("a", h - 1, aQ[:, h - 1, :])
                o_split("a", 3, aQ[:, 3, :])
                gate_sigmoid("a")
                act.wait_ge(sem("a_olo"), 4)
                for i in range(4):
                    ps = big_wait(act, ("cq", i))
                    big_free(A(cQ[:, i, :], ps[:, :], ACT.Copy, scale=DH ** -0.5), ("cq", i))
                for i in range(4):
                    ps = big_wait(act, ("ck", i))
                    big_free(A(cK[:, i, :], ps[:, :], ACT.Copy), ("ck", i))
                for i in range(4):
                    ps = big_wait(act, ("cv", i))
                    big_free(A(cV[:, i, :], ps[:, :], ACT.Copy), ("cv", i))

                def stick_A(h):
                    for j in range(NT):
                        n = S - j * P
                        ps = mix_wait(act, ("cs", h, j))
                        if h >= 2 and j == 0:
                            mix_wait(act, ("cpv", h // 2 - 1))
                        mix_free(A(c_A[h % 2][:, OFF[j]:OFF[j] + n], ps[:, 0:n], ACT.Exp), ("cs", h, j))

                for h in range(SBH + 1):
                    if h < SBH:
                        for j in reversed(range(NT)):
                            n = S - j * P
                            sl = c_sp[h % 2][:, OFF[j]:OFF[j] + n]
                            ps = mix_wait(act, ("z", h, j))
                            if h >= 2 and j == NT - 1:
                                mix_wait(act, ("cs", h - 2, NT - 1))
                            c = 3 * (NT * h + NT - 1 - j)
                            A(sl, ps[:, 0:n], ACT.Abs).then_inc(sem("c_act"), 1)
                            act.wait_ge(sem("c_act"), c + 1)
                            A(sl, sl, ACT.Exp, scale=-1.0).then_inc(sem("c_act"), 1)
                            act.wait_ge(sem("c_act"), c + 2)
                            A(sl, sl, ACT.Ln, bias=1.0).then_inc(sem("c_act"), 1)
                    if h >= 1:
                        stick_A(h - 1)
                    if h % 2 == 0 and h:
                        i = h // 2 - 1
                        ps = mix_wait(act, ("cpv", i))
                        if i == 0:
                            big_freed(act, ("ya1", 3))
                        A(oH[:, i, :], ps[:, :], ACT.Copy).then_inc(sem("c_ohi"), 1)
                    if h == 2:
                        gate_copy("c", 0)
                    if h == 5:
                        gate_copy("c", 1)
                gate_sigmoid("c")
                mix_freed(act, ("cpv", 3))
                act.dma_start(dTab, ins["tables"][:, TD:TD + 3072]).then_inc(sem("tab"), 16)
                for i in range(4):
                    ps = big_wait(act, ("dqk", i))
                    if i >= 2:
                        act.wait_ge(sem("d_rope"), i - 1)
                    big_free(A(dX[:, i % 2, :], ps[:, :], ACT.Copy), ("dqk", i))
                for i in range(4):
                    ps = big_wait(act, ("dv", i))
                    big_free(A(dV[:, i, :], ps[:, :], ACT.Copy), ("dv", i))
                for i in range(4):
                    ps = big_wait(act, ("dg", i))
                    big_free(A(dG[:, i, :], ps[:, :], ACT.Silu), ("dg", i))
                for h in range(4):
                    ps = mix_wait(act, ("dpv", h))
                    if h:
                        act.wait_ge(sem("d_out"), h)
                        o_split("d", h - 1, dG[:, h - 1, :])
                    else:
                        act.wait_ge(sem("d_rope"), 4)
                    mix_free(A(dO, ps[:, :], ACT.Copy), ("dpv", h))
                    head_norm(h, ("dn", h), dO, dSq, dSq, "dn", lambda: mix_freed(act, ("dpv", h)))
                    if h == 1:
                        gate_copy("d", 0)
                    if h == 3:
                        gate_copy("d", 1)
                o_split("d", 3, dG[:, 3, :])
                gate_sigmoid("d")
                act.wait_ge(sem("d_olo"), 4)
                act.dma_start(bTab, ins["tables"][:, TWC:TWC + 1024]).then_inc(sem("tab"), 16)
                for i in range(10):
                    key = (("bq0", i), ("bq1", 0), ("bk0", i - 5), ("bk1", 0))[(i >= 4) + (i >= 5) + (i >= 9)]
                    ps = big_wait(act, key)
                    if i >= 2:
                        act.wait_ge(sem("b_rope"), i - 1)
                    big_free(A(bX[:, i % 2, :], ps[:, :], ACT.Copy), key)
                for g in range(3):
                    for i in range(4):
                        ps = big_wait(act, (f"bv{g}", i))
                        big_free(A(bV[:, g, i, :], ps[:, 0:192], ACT.Copy), (f"bv{g}", i))
                nexp = 0
                for i in range(len(WU) + 2):
                    if i < len(WU):
                        g, h, b0, nb, w = WU[i]
                        act.wait_ge(sem("b_nm"), i + 1)
                        pv = bP[:, i % 2, :].rearrange("p (b w) -> p b w", w=w)
                        for b in range(nb):
                            A(pv[:, b, :], pv[:, b, :], ACT.Exp, bias=w_nm[:, g, b0 + b, h:h + 1],
                              accum_out=w_z[:, g, b0 + b, h:h + 1]).then_inc(sem("b_exp"), 1)
                            nexp += 1
                    if 1 <= i <= len(WU):
                        ps = mix_wait(act, ("pt", i - 1))
                        if i >= 3:
                            mix_wait(act, ("wpv", i - 3))
                        mix_free(A(bPT[:, (i - 1) % 2, :], ps[:, :], ACT.Copy), ("pt", i - 1))
                    if i >= 2:
                        g, h, b0, nb, w = WU[i - 2]
                        hh = 3 * g + h
                        p0, tl = hh % 2 * DH, hh // 2
                        ps = mix_wait(act, ("wpv", i - 2))
                        if g == 0:
                            o_, i_ = bQ[p0:p0 + DH, tl, b0 * P:(b0 + nb) * P], ps[p0:p0 + DH, 0:nb * P]
                        else:
                            o_ = bQ[p0:p0 + DH, tl, :].rearrange("p (l r) -> p r l", r=DIL[g])
                            i_ = ps[p0:p0 + DH, :].rearrange("p (r l) -> p r l", r=DIL[g])
                        mix_free(A(o_, i_, ACT.Copy), ("wpv", i - 2))
                    if i == 4:
                        gate_copy("b", 0)
                    if i == 9:
                        gate_copy("b", 1)
                for n in range(2):
                    for g in range(3):
                        ps = mix_wait(act, ("st", n, g))
                        o_ = (bFM, bFZ)[n][:, g, :]
                        i_ = ps[0:3, :]
                        if g:
                            o_ = o_.rearrange("p (l r) -> p r l", r=DIL[g])
                            i_ = i_.rearrange("p (r l) -> p r l", r=DIL[g])
                        mix_free(A(o_, i_, ACT.Copy), ("st", n, g))
                act.wait_ge(sem("b_fac"), 3)
                A(bFM, bFM, ACT.Exp).then_inc(sem("b_fexp"), 1)
                for i in range(5):
                    r = P if i < 4 else DH
                    o_split("b", i, bQ[0:r, i, :], r)
                gate_sigmoid("b")
                for k in range(KT):
                    act.wait_ge(sem("mixed"), k + 1)
                    A(hH[:, k, :], mixed[:, k, :], ACT.Copy).then_inc(sem("m_hi"), 1)

                def y_copy(jobs, hf):
                    for t in range(NT):
                        ps = big_wait(act, (f"{jobs}{hf}", t))
                        big_free(A(yhalf[hf][:, t, :], ps[:, :], ACT.Copy), (f"{jobs}{hf}", t))

                def post(jobs, tag, norm):
                    act.dma_start(postw, ins[norm][bass.ds(l, 1), :].to_broadcast((P, DM))).then_inc(sem("postw"), 16)
                    y_copy(jobs, 1)
                    norm_stats(yhalf, lambda q, t: big_freed(act, (f"{jobs}{q}", t)), tag)

                act.wait_ge(sem("b_olo"), 5)
                y_copy("o", 0)
                post("o", "n2", "norm_post_mix")
                norm_stats([xv], lambda q, t: act.wait_ge(sem("n2_x"), 2 * t + 2), "n3")
                split_hi("pre2", LN2)
                for g in range(8):
                    for i in range(4):
                        ps = big_wait(act, (f"up{g}", i))
                        if g == 0 and i == 0:
                            mix_freed(act, ("pre2", KT - 1))
                        A(fT[:, 4 * g + i, :], ps[:, :], ACT.Relu).then_inc(sem("f_relu"), 1)
                for hf in range(2):
                    for u in range(16):
                        n = 16 * hf + u
                        if n == 0:
                            for i in range(4):
                                big_freed(act, ("up7", i))
                        if n == 19:
                            y_copy("dn", 0)
                        if n >= 4:
                            act.wait_ge(sem("w_used"), DN0 + n - 3)
                        q = n % 4 * 2
                        A(hH[:, q:q + 2, :], fT[:, 2 * u:2 * u + 2, :], ACT.Copy).then_inc(sem("f_hi"), 1)
                act.wait_ge(sem("f_lo"), 32)
                post("dn", "n4", "norm_post_mlp")

            @block.vector
            def _(dve):
                V = nc.vector
                TT, TS, STT = V.tensor_tensor, V.tensor_scalar, V.scalar_tensor_tensor

                def rstd(tag):
                    c = sem(f"{tag}_nw")
                    if tag in ("n2", "n4"):
                        dve.wait_ge(sem(f"{tag}_ss"), 2 * NT)
                        STT(n_v, n_ss[:, 0:NT], EPS, n_ss[:, NT:2 * NT], ALU.add, ALU.add).then_inc(sem(f"{tag}_v"), 1)
                    else:
                        dve.wait_ge(sem(f"{tag}_ss"), NT)
                        V.tensor_scalar_add(n_v, n_ss[:, 0:NT], EPS).then_inc(sem(f"{tag}_v"), 1)
                    dve.wait_ge(sem(f"{tag}_y"), 1)
                    TT(n_t, n_y, n_y, ALU.mult).then_inc(c, 1)
                    dve.wait_ge(c, 1)
                    TT(n_t, n_t, n_v, ALU.mult).then_inc(c, 1)
                    dve.wait_ge(c, 2)
                    TS(n_t, n_t, -0.5, 1.5, ALU.mult, ALU.add).then_inc(c, 1)
                    dve.wait_ge(c, 3)
                    TT(n_y, n_y, n_t, ALU.mult).then_inc(c, 1)
                    dve.wait_ge(c, 4)

                def pre(tag, ntag, nw):
                    rstd(ntag)
                    for t in range(NT):
                        TS(hn[:, t, :], xv[:, t, :], n_y[:, t:t + 1], None, ALU.mult).then_inc(sem(f"{tag}_h"), 1)
                    for k in range(KT):
                        ps = mix_wait(dve, (tag, k))
                        dve.wait_ge(sem(f"{tag}_hi"), k + 1)
                        mix_free(STT(hL[:, k, :], ps[:, :], lw[:, nw + k:nw + k + 1], f32(hH[:, k, :]), ALU.mult, ALU.subtract), (tag, k))

                def o_lo_split(tag, i, src, rows=P):
                    dve.wait_ge(sem(f"{tag}_ohi"), i + 1)
                    TT(oL[0:rows, i, :], src, f32(oH[0:rows, i, :]), ALU.subtract).then_inc(sem(f"{tag}_olo"), 1)

                def gated(b):
                    for hf in range(2):
                        for i in range(4):
                            k = 4 * hf + i
                            ps = big_wait(dve, (f"y{b}{hf}", i))
                            dve.wait_ge(sem(f"sig{b}"), hf + 1)
                            if b == "a":
                                big_free(TT(mixed[:, k, :], ps[:, :], sg[:, k, :], ALU.mult), (f"y{b}{hf}", i))
                            else:
                                big_free(TT(sg[:, k, :], ps[:, :], sg[:, k, :], ALU.mult), (f"y{b}{hf}", i))
                                big_freed(dve, (f"y{b}{hf}", i))
                                TT(mixed[:, k, :], mixed[:, k, :], sg[:, k, :], ALU.add).then_inc(sem(f"mixed_{b}") if b != "b" else sem("mixed"), 1)

                def per_head(ap4):
                    return ap4.unsqueeze(2).to_broadcast((P, GH, P))

                def per_mask(ap):
                    return ap.unsqueeze(1).to_broadcast((P, GH, P))

                pre("pre1", "n1", LN1)
                V.memset(g_S, 0.0).then_inc(sem("a_S0"), 1)
                dve.wait_ge(sem("small_loaded"), 16)
                mix_wait(dve, ("pre1", KT - 1))
                n = 0
                for i in range(12):
                    key = (("aq", "ak", "av")[i // 4], i % 4)
                    ps = big_wait(dve, key)
                    if i >= 2:
                        dve.wait_ge(sem("a_silu"), i - 1)
                    cv = g_cv[:, i % 2, :]
                    tap = lambda q: lw[:, LCW + 12 * q + i:LCW + 12 * q + i + 1]
                    TS(cv, ps[:, :], tap(3), None, ALU.mult).then_inc(sem("a_tap"), 1)
                    for q in (1, 2):
                        dve.wait_ge(sem("a_tap"), 3 * i + q)
                        STT(cv[:, q:], ps[:, 0:S - q], tap(3 - q), cv[:, q:], ALU.mult, ALU.add).then_inc(sem("a_tap"), 1)
                    dve.wait_ge(sem("a_tap"), 3 * i + 3)
                    big_free(STT(cv[:, 3:], ps[:, 0:S - 3], tap(0), cv[:, 3:], ALU.mult, ALU.add), key)
                for i in range(8):
                    dve.wait_ge(sem("a_rs"), i + 1)
                    t = (aQ, aK)[i // 4][:, i % 4, :]
                    STT(t, t, DK ** -0.5 if i < 4 else 1.0, g_rs[:, i % 2, :], ALU.mult, ALU.mult).then_inc(sem("a_l2"), 1)
                ps = mix_wait(dve, "ab")
                abv = ps[:, 0:32].rearrange("p (b c) -> p b c", b=4)
                c = sem("a_sc")
                TT(s_a, abv[:, :, 0:4], lw[:, LDT:LDT + GH].unsqueeze(1).to_broadcast((P, 4, GH)), ALU.add).then_inc(c, 1)
                mix_free(V.tensor_scalar_max(s_be, abv[:, :, 4:8], -80.0), "ab")
                dve.wait_ge(c, 1)
                mix_freed(dve, "ab")
                STT(s_e, s_a, -1.0, s_a, ALU.mult, ALU.max).then_inc(sem("a_small"), 1)
                TS(s_a, s_a, 0.0, None, ALU.max).then_inc(sem("a_small"), 1)
                dve.wait_ge(sem("a_smallact"), 4)
                TT(s_g, s_a, s_l, ALU.add).then_inc(c, 1)
                V.tensor_scalar_add(s_be, s_be, 1.0).then_inc(c, 1)
                dve.wait_ge(c, 2)
                STT(s_g, s_g, -1.0, s_ea[:, 0, :].unsqueeze(1).to_broadcast((P, 4, GH)), ALU.mult, ALU.mult).then_inc(sem("a_g"), 1)
                dve.wait_ge(c, 3)
                V.reciprocal(s_be, s_be).then_inc(sem("a_g"), 1)
                ps = mix_wait(dve, "gc")
                mix_free(V.tensor_copy(s_gc, ps[:, 0:16].rearrange("p (b h) -> p b h", b=4)), "gc")
                mix_freed(dve, "gc")
                for b in range(NT):
                    bs = slice(b * P, (b + 1) * P)
                    ps = mix_wait(dve, ("R", b))
                    R = heads(ps)
                    dve.wait_ge(sem("a_eR"), b + 1)
                    TT(s_ed[:, b, :], R[:, :, P - 1], s_gc[:, b, :], ALU.subtract).then_inc(sem("a_edarg"), 1)
                    mix_free(TT(g_dec, R, per_head(s_gc[:, b, :]), ALU.subtract), ("R", b))
                    mix_freed(dve, ("R", b))
                    V.tensor_scalar_min(g_dec, g_dec, 0.0).then_inc(sem("a_min"), 1)
                    ps = mix_wait(dve, ("B", b))
                    mix_free(TT(g_kb, aK[:, :, bs], heads(ps), ALU.mult), ("B", b))
                    dve.wait_ge(sem("a_dec"), b + 1)
                    TT(g_dec, g_dec, per_mask(triu), ALU.mult).then_inc(sem("a_decm"), 1)
                    dve.wait_ge(sem("a_decm"), b + 1)
                    ps = mix_wait(dve, ("LT", b))
                    mix_free(TT(g_LT, heads(ps), g_dec, ALU.mult), ("LT", b))
                    ps = mix_wait(dve, ("att", b))
                    mix_free(TT(g_att, heads(ps), g_dec, ALU.mult), ("att", b))
                    mix_freed(dve, ("LT", b))
                    TT(g_LTm, g_LT, per_mask(consts[:, CLV:CLV + P]), ALU.mult).then_inc(sem("a_LTm"), 1)
                    dve.wait_ge(sem("a_LTm"), 1 + LEVELS * b)
                    TT(g_U, per_mask(ident), g_LTm, ALU.subtract).then_inc(sem("a_U"), 1)
                    TT(aQ[:, :, bs], aQ[:, :, bs], g_eR, ALU.mult).then_inc(sem("a_qd"), 1)
                    TT(g_kb, g_kb, g_eR, ALU.mult).then_inc(sem("a_kbe"), 1)
                    ps = mix_wait(dve, ("kn", b))
                    dve.wait_ge(sem("a_ed"), b + 1)
                    mix_free(TT(g_kd, heads(ps), per_head(s_ed[:, b, :]), ALU.mult), ("kn", b))
                    ps = mix_wait(dve, ("vn", b))
                    mix_free(TT(g_vb, heads(ps), per_head(s_be[:, b, :]), ALU.mult), ("vn", b))
                    for n in range(1, LEVELS):
                        if n > 1:
                            mix_wait(dve, ("Y", b, n - 1))
                        TT(g_LTm, g_LT, per_mask(consts[:, CLV + n * P:CLV + (n + 1) * P]), ALU.mult).then_inc(sem("a_LTm"), 1)
                        if n < LEVELS - 1:
                            ps = mix_wait(dve, ("X", b, n))
                            mix_wait(dve, ("XT", b, n))
                            mix_free(TT(g_T, g_T, heads(ps), ALU.subtract), ("X", b, n))
                        ps = mix_wait(dve, ("XT", b, n))
                        mix_free(TT(g_U, g_U, heads(ps), ALU.subtract), ("XT", b, n))
                        if n < LEVELS - 1:
                            mix_freed(dve, ("XT", b, n))
                    ps = mix_wait(dve, ("ks", b))
                    mix_free(TT(g_vb, g_vb, heads(ps), ALU.subtract), ("ks", b))
                    ps = mix_wait(dve, ("dS", b))
                    for h in range(GH):
                        i = STT(g_S[:, h, :], g_S[:, h, :], g_eR[:, h, P - 1:P], ps[:, h * P:(h + 1) * P], ALU.mult, ALU.add)
                    mix_free(i, ("dS", b))

                def head_out(h, o, rs, w, gate, dst, tag):
                    dve.wait_ge(sem(f"{tag}n_rs"), h + 1)
                    TT(o, o, rs, ALU.mult).then_inc(sem(f"{tag}_nrm"), 1)
                    dve.wait_ge(sem(f"{tag}_nrm"), h + 1)
                    STT(dst, o, lw[:, w:w + 1], gate, ALU.mult, ALU.mult).then_inc(sem(f"{tag}_out"), 1)

                big_freed(dve, ("az", 3))
                big_freed(dve, ("az", 2))
                big_freed(dve, ("az", 1))
                big_freed(dve, ("az", 0))
                for h in range(4):
                    head_out(h, aQ[:, h, :], g_rs[:, h % 2, :], LGN, aK[:, h, :], aQ[:, h, :], "a")
                    if h:
                        o_lo_split("a", h - 1, aQ[:, h - 1, :])
                o_lo_split("a", 3, aQ[:, 3, :])
                gated("a")
                for h in range(SBH + 1):
                    if h < SBH:
                        for j in reversed(range(NT)):
                            n = S - j * P
                            c = NT * h + NT - 1 - j
                            ps = mix_wait(dve, ("z", h, j))
                            sl = c_sp[h % 2][:, OFF[j]:OFF[j] + n]
                            dve.wait_ge(sem("c_act"), 3 * c + 3)
                            mix_free(STT(sl, ps[:, 0:n], 0.0, sl, ALU.max, ALU.add), ("z", h, j))
                            mix_freed(dve, ("z", h, j))
                            TT(sl[:, 0:P], sl[:, 0:P], strict, ALU.mult).then_inc(sem("c_sp"), 1)
                    if h % 2 == 0 and h:
                        i = h // 2 - 1
                        ps = mix_wait(dve, ("cpv", i))
                        dve.wait_ge(sem("c_ohi"), i + 1)
                        mix_free(TT(oL[:, i, :], ps[:, :], f32(oH[:, i, :]), ALU.subtract), ("cpv", i))
                gated("c")

                def rope(i, key, x, cos, sin, t1, t2, dsts, tag):
                    ps = mix_wait(dve, key)
                    n = sem(f"{tag}_rp")
                    if i:
                        dve.wait_ge(sem(f"{tag}_rope"), i)
                    TT(t1, x, cos, ALU.mult).then_inc(n, 1)
                    mix_free(TT(t2, ps[:, :], sin, ALU.mult), key)
                    dve.wait_ge(n, i + 1)
                    mix_freed(dve, key)
                    for q, (r0, r1, dst, dil) in enumerate(dsts):
                        a, b_ = t1[r0:r1, :], t2[r0:r1, :]
                        if dil > 1:
                            dst = dst.rearrange("p (r l) -> p r l", r=dil)
                            a = a.rearrange("p (l r) -> p r l", r=dil)
                            b_ = b_.rearrange("p (l r) -> p r l", r=dil)
                        ins_ = TT(dst, a, b_, ALU.add)
                        if q == len(dsts) - 1:
                            ins_.then_inc(sem(f"{tag}_rope"), 1)

                dve.wait_ge(sem("tab"), 16)
                mix_freed(dve, ("cpv", 3))
                for i in range(4):
                    rope(i, ("drot", i), dX[:, i % 2, :], dTab[:, TRC:TRC + S], dTab[:, TRS:TRS + S],
                         dY[:, 0, :], dY[:, 1, :], [(0, P, dQK[:, i, :], 1)], "d")
                for h in range(4):
                    for j in range(NT):
                        n = S - j * P
                        ps = mix_wait(dve, ("dz", h, j))
                        if h:
                            mix_wait(dve, ("dpv", h - 1))
                        else:
                            dve.wait_ge(sem("d_rope"), 4)
                        mix_free(TT(dP[:, j, 0:n], ps[:, 0:n], dTab[:, TD + S * h:TD + S * h + n], ALU.mult), ("dz", h, j))
                    if h == 0:
                        for i in range(4):
                            big_freed(dve, ("dg", i))
                    if h:
                        o_lo_split("d", h - 1, dG[:, h - 1, :])
                    head_out(h, dO, dSq, LRN, dG[:, h, :], dG[:, h, :], "d")
                o_lo_split("d", 3, dG[:, 3, :])
                gated("d")
                dve.wait_ge(sem("tab"), 32)
                for i in range(10):
                    dst, tl = (bQ, bK)[i // 5], i % 5
                    half = [(0, DH, dst[0:DH, tl, :], DIL[2 * tl // 3]), (DH, P, dst[DH:P, tl, :], DIL[min((2 * tl + 1) // 3, 2)])]
                    rope(i, ("brot", i), bX[:, i % 2, :], bTab[:, 0:S], bTab[:, S:2 * S],
                         bP[:, 0, :], bP[:, 1, :], half if tl < 4 else half[:1], "b")
                for i, (g, h, b0, nb, w) in enumerate(WU):
                    ps = mix_wait(dve, ("sc", i))
                    if i == 0:
                        dve.wait_ge(sem("b_rope"), 10)
                    if i >= 2:
                        mix_wait(dve, ("pt", i - 2))
                    if g == 0:
                        mask = consts[:, CMG0 + b0 * 128:CMG0 + b0 * 128 + 512].rearrange("p (b w) -> p b w", w=w)
                    else:
                        m0 = (CMG1, CMG2)[g - 1]
                        mask = consts[:, m0:m0 + P].unsqueeze(1).to_broadcast((P, 4, P))
                    pv = bP[:, i % 2, :].rearrange("p (b w) -> p b w", w=w)
                    mix_free(STT(pv, ps[:, :].rearrange("p (b w) -> p b w", w=w), DH ** -0.5, mask, ALU.mult, ALU.add), ("sc", i))
                    mix_freed(dve, ("sc", i))
                    V.reduce_max(w_m[:, g, b0:b0 + nb, h], pv, AX_X).then_inc(sem("b_max"), 1)
                    dve.wait_ge(sem("b_max"), i + 1)
                    TS(w_nm[:, g, b0:b0 + nb, h], w_m[:, g, b0:b0 + nb, h], -1.0, None, ALU.mult).then_inc(sem("b_nm"), 1)
                for n in range(2):
                    for g in range(3):
                        mix_freed(dve, ("st", n, g))
                fc = sem("b_fc")
                TT(bFS, bFM[:, 0, :], bFM[:, 1, :], ALU.max).then_inc(fc, 1)
                dve.wait_ge(fc, 1)
                TT(bFS, bFS, bFM[:, 2, :], ALU.max).then_inc(fc, 1)
                dve.wait_ge(fc, 2)
                for g in range(3):
                    TT(bFM[:, g, :], bFM[:, g, :], bFS, ALU.subtract).then_inc(sem("b_fac"), 1)
                dve.wait_ge(sem("b_fexp"), 1)
                TT(bFZ, bFZ, bFM, ALU.mult).then_inc(fc, 1)
                dve.wait_ge(fc, 3)
                TT(bFS, bFZ[:, 0, :], bFZ[:, 1, :], ALU.add).then_inc(fc, 1)
                dve.wait_ge(fc, 4)
                TT(bFS, bFS, bFZ[:, 2, :], ALU.add).then_inc(fc, 1)
                dve.wait_ge(fc, 5)
                V.reciprocal(bFS, bFS).then_inc(fc, 1)
                dve.wait_ge(fc, 6)
                for g in range(3):
                    TT(bFM[:, g, :], bFM[:, g, :], bFS, ALU.mult).then_inc(sem("b_share"), 1)
                for i in range(5):
                    r = P if i < 4 else DH
                    ps = mix_wait(dve, ("bf", i))
                    mix_free(TT(bQ[0:r, i, :], bQ[0:r, i, :], ps[0:r, :], ALU.mult), ("bf", i))
                for i in range(5):
                    r = P if i < 4 else DH
                    o_lo_split("b", i, bQ[0:r, i, :], r)
                gated("b")
                for k in range(KT):
                    dve.wait_ge(sem("m_hi"), k + 1)
                    TT(hL[:, k, :], mixed[:, k, :], f32(hH[:, k, :]), ALU.subtract).then_inc(sem("m_lo"), 1)

                def residual(tag):
                    rstd(tag)
                    dve.wait_ge(sem("postw"), 16 if tag == "n2" else 32)
                    for t in range(NT):
                        for hf in range(2):
                            n = 2 * t + hf
                            cs = slice(hf * 512, hf * 512 + 512)
                            STT(ytmp[:, hf, :], yhalf[hf][:, t, :], n_y[:, t:t + 1], postw[:, cs], ALU.mult, ALU.mult).then_inc(sem(f"{tag}_t"), 1)
                            dve.wait_ge(sem(f"{tag}_t"), n + 1)
                            TT(xv[:, t, cs], xv[:, t, cs], ytmp[:, hf, :], ALU.add).then_inc(sem(f"{tag}_x"), 1)

                residual("n2")
                pre("pre2", "n3", LN2)
                for g in range(8):
                    for i in range(4):
                        k = 4 * g + i
                        ps = big_wait(dve, (f"up{g}", i))
                        dve.wait_ge(sem("f_relu"), k + 1)
                        big_free(STT(fT[:, k, :], ps[:, :], 0.0, fT[:, k, :], ALU.max, ALU.mult), (f"up{g}", i))
                for hf in range(2):
                    for u in range(16):
                        n = 16 * hf + u
                        dve.wait_ge(sem("f_hi"), n + 1)
                        q = n % 4 * 2
                        TT(hL[:, q:q + 2, :], fT[:, 2 * u:2 * u + 2, :], f32(hH[:, q:q + 2, :]), ALU.subtract).then_inc(sem("f_lo"), 1)
                residual("n4")
                dve.wait_ge(sem("n4_x"), 2 * NT)

            @block.tensor
            def _(pe):
                MM, TR = nc.tensor.matmul, nc.tensor.transpose
                state = {"u": 0}

                def unit(job, i):
                    u = state["u"]
                    assert UNITS[u][0] is job and UNITS[u][1] == i
                    slot = u % RING
                    r0, rows = job.units[i]
                    kts = [(r0 // P + k, min(P, rows - k * P)) for k in range(max(1, -(-rows // P)))]
                    pe.wait_ge(sem("w_ready"), u + 1)
                    sH, sL = (oH, oL) if job.src == "o" else (hH, hL)
                    last_unit = i == len(job.units) - 1
                    first = True
                    for t in range(job.tiles):
                        b, use = BIG[(job.name, t)]
                        if i == 0 and use > 1:
                            pe.wait_ge(sem(f"big_free{b}"), use - 1)
                        for k, (kt, rr) in enumerate(kts):
                            ks = (2 * (i % 4) + k) if job.src == "f" else kt
                            for m, (wt, xt) in enumerate(((rH, sH), (rL, sH), (rH, sL))):
                                if job.kind == "T":
                                    o_ = big[b][:, 0:S]
                                    a_, r_ = wt[0:rr, slot, k, t * P:(t + 1) * P], xt[0:rr, ks, :]
                                else:
                                    o_ = big[b][:, 0:job.n]
                                    d = DIL[job.perm]
                                    if job.perm == 0:
                                        a_ = xt[0:rr, ks, t * P:(t + 1) * P]
                                    else:
                                        a_ = xt[0:rr, ks, :].rearrange("p (l r) -> p r l", r=d)
                                        a_ = a_[:, t, :]
                                    r_ = wt[0:rr, slot, k, 0:job.n]
                                s0 = i == 0 and k == 0 and m == 0
                                s1 = last_unit and k == len(kts) - 1 and m == 2
                                ins_ = MM(o_, a_, r_, start=s0, stop=s1)
                                if s1:
                                    ins_.then_inc(sem(f"big_done{b}"), 1)
                                elif first and u > 0:
                                    ins_.then_inc(sem("w_used"), 1)
                                first = False
                    state["u"] += 1

                def do(name):
                    job = JOB[name]
                    for i in range(len(job.units)):
                        unit(job, i)

                fills = []

                def fill(n=1):
                    for _ in range(n):
                        if fills:
                            unit(*fills.pop(0))

                def set_fill(b):
                    fills.extend((JOB[f"gate{b}{hf}"], i) for hf in range(2) for i in range(4))

                order = iter(MIX)

                def tile_of(key):
                    assert next(order) == key, key
                    b, k = MIX[key]
                    if k > 1:
                        pe.wait_ge(sem(f"mix_free{b}"), k - 1)
                    return mxb[b]

                def done(ins_, key):
                    ins_.then_inc(sem(f"mix_done{MIX[key][0]}"), 1)

                def pre(tag):
                    for k in range(KT):
                        ps = tile_of((tag, k))
                        pe.wait_ge(sem(f"{tag}_h"), NT)
                        for t in range(NT):
                            i = TR(ps[:, t * P:(t + 1) * P], hn[:, t, k * P:(k + 1) * P], ident)
                        done(i, (tag, k))
                    for k in range(KT - 4, KT):
                        mix_freed(pe, (tag, k))

                pre("pre1")
                for n in ("aq", "ak", "av", "aab"):
                    do(n)
                set_fill("a")
                for i in range(8):
                    ps = tile_of(("l2", i))
                    pe.wait_ge(sem("a_sq"), i + 1)
                    done(MM(ps[:, :], ones[:, :], g_sq[:, i % 2, :], start=True, stop=True), ("l2", i))
                ps = tile_of("ab")
                big_freed(pe, ("aab", 0))
                for t in range(NT):
                    i = TR(ps[:, 8 * t:8 * t + 8], g_ab[:, t * P:(t + 1) * P], ident[0:8, 0:8])
                done(i, "ab")
                fill(1)
                pe.wait_ge(sem("a_g"), 2)
                ps = tile_of("gc")
                done(MM(ps[:, 0:16], triu, st[:, 64:80], start=True, stop=True), "gc")
                pe.wait_ge(sem("a_l2"), 8)
                for b in range(NT):
                    bs = slice(b * P, (b + 1) * P)
                    ps = tile_of(("R", b))
                    for h in range(GH):
                        i = MM(ps[:, h * P:(h + 1) * P], s_g[:, b, h:h + 1].to_broadcast((P, P)), triu, start=True, stop=True)
                    done(i, ("R", b))
                    ps = tile_of(("B", b))
                    for h in range(GH):
                        i = MM(ps[:, h * P:(h + 1) * P], s_be[:, b, h:h + 1].to_broadcast((P, P)), ident, start=True, stop=True)
                    done(i, ("B", b))
                    ps = tile_of(("LT", b))
                    mix_freed(pe, ("B", b))
                    for h in range(GH):
                        i = MM(ps[:, h * P:(h + 1) * P], aK[:, h, bs], g_kb[:, h, :], start=True, stop=True)
                    done(i, ("LT", b))
                    ps = tile_of(("att", b))
                    for h in range(GH):
                        i = MM(ps[:, h * P:(h + 1) * P], aK[:, h, bs], aQ[:, h, bs], start=True, stop=True)
                    done(i, ("att", b))
                    if b % 2 == 0:
                        fill(1)
                    ps = tile_of(("T0", b))
                    pe.wait_ge(sem("a_U"), b + 1)
                    for h in range(GH):
                        i = TR(ps[:, h * P:(h + 1) * P], g_U[:, h, :], ident)
                    done(i, ("T0", b))
                    ps = tile_of(("kn", b))
                    for h in range(GH):
                        i = TR(ps[:, h * P:(h + 1) * P], aK[:, h, bs], ident)
                    done(i, ("kn", b))
                    ps = tile_of(("vn", b))
                    for h in range(GH):
                        i = TR(ps[:, h * P:(h + 1) * P], aV[:, h, bs], ident)
                    done(i, ("vn", b))
                    for n in range(1, LEVELS):
                        ps = tile_of(("Y", b, n))
                        pe.wait_ge(sem("a_LTm"), LEVELS * b + n + 1)
                        mix_freed(pe, ("T0", b) if n == 1 else ("X", b, n - 1))
                        for h in range(GH):
                            i = MM(ps[:, h * P:(h + 1) * P], g_LTm[:, h, :], g_T[:, h, :], start=True, stop=True)
                        done(i, ("Y", b, n))
                        if n > 1:
                            mix_freed(pe, ("XT", b, n - 1))
                        if n < LEVELS - 1:
                            ps = tile_of(("X", b, n))
                            mix_freed(pe, ("Y", b, n))
                            for h in range(GH):
                                i = MM(ps[:, h * P:(h + 1) * P], g_U[:, h, :], g_Y[:, h, :], start=True, stop=True)
                            done(i, ("X", b, n))
                        ps = tile_of(("XT", b, n))
                        mix_freed(pe, ("Y", b, n))
                        for h in range(GH):
                            i = MM(ps[:, h * P:(h + 1) * P], g_Y[:, h, :], g_U[:, h, :], start=True, stop=True)
                        done(i, ("XT", b, n))
                        if b % 2 == 0 and n in (2, 4):
                            fill(1)
                    if b % 2 == 0 and b:
                        fill(1)
                    ps = tile_of(("ks", b))
                    pe.wait_ge(sem("a_kbe"), b + 1)
                    pe.wait_ge(sem("a_S0"), 1)
                    if b:
                        mix_freed(pe, ("dS", b - 1))
                    for h in range(GH):
                        i = MM(ps[:, h * P:(h + 1) * P], g_kb[:, h, :], g_S[:, h, :], start=True, stop=True)
                    done(i, ("ks", b))
                    ps = tile_of(("new", b))
                    mix_freed(pe, ("XT", b, LEVELS - 1))
                    mix_freed(pe, ("ks", b))
                    for h in range(GH):
                        i = MM(ps[:, h * P:(h + 1) * P], g_U[:, h, :], g_vb[:, h, :], start=True, stop=True)
                    done(i, ("new", b))
                    ps = tile_of(("o", b))
                    pe.wait_ge(sem("a_qd"), b + 1)
                    mix_freed(pe, ("new", b))
                    mix_freed(pe, ("att", b))
                    for h in range(GH):
                        MM(ps[:, h * P:(h + 1) * P], g_S[:, h, :], aQ[:, h, bs], start=True, stop=False)
                        i = MM(ps[:, h * P:(h + 1) * P], g_Y[:, h, :], g_att[:, h, :], start=False, stop=True)
                    done(i, ("o", b))
                    ps = tile_of(("dS", b))
                    for h in range(GH):
                        i = MM(ps[:, h * P:(h + 1) * P], g_kd[:, h, :], g_Y[:, h, :], start=True, stop=True)
                    done(i, ("dS", b))
                fill(8)
                do("az")
                for h in range(4):
                    ps = tile_of(("an", h))
                    pe.wait_ge(sem("an_sq"), h + 1)
                    done(MM(ps[:, :], ones[:, :], g_sq[:, h % 2, :], start=True, stop=True), ("an", h))
                pe.wait_ge(sem("a_olo"), 4)
                do("ya0")
                do("ya1")
                for n in ("cq", "ck", "cv"):
                    do(n)
                set_fill("c")
                for n in ("cq", "ck", "cv"):
                    for i in range(4):
                        big_freed(pe, (n, i))

                def hv(t, h):
                    return t[h % 2 * DH:h % 2 * DH + DH, h // 2, :]

                for h in range(SBH + 1):
                    if h < SBH:
                        for j in reversed(range(NT)):
                            n = S - j * P
                            ps = tile_of(("z", h, j))
                            done(MM(ps[:, 0:n], hv(cK, h)[:, j * P:(j + 1) * P], hv(cQ, h)[:, j * P:], start=True, stop=True), ("z", h, j))
                    if h in (0, 1, 2, 3, 4, 5):
                        fill(2 if h in (1, 4) else 1)
                    if h >= 1:
                        g = h - 1
                        pe.wait_ge(sem("c_sp"), NT * h)
                        for j in range(NT):
                            n = S - j * P
                            ps = tile_of(("cs", g, j))
                            MM(ps[:, 0:n], hv(cK, g)[:, j * P:(j + 1) * P], hv(cQ, g)[:, j * P:], start=True, stop=False)
                            MM(ps[:, 0:P], idb[:, :], strictb[:, :], start=False, stop=False)
                            i = MM(ps[:, 0:n], consts[:, CNTL:CNTL + P], c_sp[g % 2][:, OFF[j]:OFF[j] + n], start=False, stop=j == NT - 1)
                            for q in range(j + 1, NT):
                                i = MM(ps[:, (q - j) * P:n], consts[:, CNON:CNON + P], c_sp[g % 2][:, OFF[q]:OFF[q] + S - q * P],
                                       start=False, stop=q == NT - 1)
                            done(i, ("cs", g, j))
                    if h % 2 == 0 and h:
                        i = h // 2 - 1
                        ps = tile_of(("cpv", i))
                        for g in (h - 2, h - 1):
                            for j in range(NT):
                                mix_freed(pe, ("cs", g, j))
                                r = MM(ps[g % 2 * DH:g % 2 * DH + DH, j * P:], cV[:, j, g * DH:(g + 1) * DH],
                                       c_A[g % 2][:, OFF[j]:OFF[j] + S - j * P], start=j == 0, stop=j == NT - 1)
                        done(r, ("cpv", i))
                fill(8)
                for i in range(4):
                    mix_freed(pe, ("cpv", i))
                do("yc0")
                do("yc1")
                do("dqk")
                for i in range(4):
                    ps = tile_of(("drot", i))
                    big_freed(pe, ("dqk", i))
                    done(MM(ps[:, :], consts[:, CRR:CRR + P], dX[:, i % 2, :], start=True, stop=True), ("drot", i))
                do("dv")
                do("dg")
                for i in range(4):
                    big_freed(pe, ("dv", i))
                set_fill("d")
                pe.wait_ge(sem("d_rope"), 4)
                for h in range(4):
                    for j in range(NT):
                        n = S - j * P
                        ps = tile_of(("dz", h, j))
                        q, k = dQK[:, h // 2, :], dQK[:, 2 + h // 2, :]
                        r0 = h % 2 * DH
                        done(MM(ps[:, 0:n], k[r0:r0 + DH, j * P:(j + 1) * P], q[r0:r0 + DH, j * P:], start=True, stop=True), ("dz", h, j))
                    fill(1)
                    ps = tile_of(("dpv", h))
                    for j in range(NT):
                        mix_freed(pe, ("dz", h, j))
                        r = MM(ps[:, j * P:], dV[:, j, h * P:(h + 1) * P], dP[:, j, 0:S - j * P], start=j == 0, stop=j == NT - 1)
                    done(r, ("dpv", h))
                    fill(1)
                    ps = tile_of(("dn", h))
                    pe.wait_ge(sem("dn_sq"), h + 1)
                    done(MM(ps[:, :], ones[:, :], dSq, start=True, stop=True), ("dn", h))
                pe.wait_ge(sem("d_olo"), 4)
                do("yd0")
                do("yd1")
                i = 0
                for n in ("bq0", "bq1", "bk0", "bk1"):
                    do(n)
                    for t in range(JOB[n].tiles):
                        ps = tile_of(("brot", i))
                        big_freed(pe, (n, t))
                        done(MM(ps[:, :], consts[:, CRD:CRD + P], bX[:, i % 2, :], start=True, stop=True), ("brot", i))
                        i += 1
                for g in range(3):
                    do(f"bv{g}")
                for g in range(3):
                    for i in range(4):
                        big_freed(pe, (f"bv{g}", i))
                set_fill("b")
                pe.wait_ge(sem("b_rope"), 10)
                nexp = 0
                for i in range(len(WU) + 2):
                    if i < len(WU):
                        g, h, b0, nb, w = WU[i]
                        ps = tile_of(("sc", i))
                        hh = 3 * g + h
                        q, k = hv(bQ, hh), hv(bK, hh)
                        for b in range(nb):
                            bb = b0 + b
                            keys = slice(bb * P, (bb + 1) * P) if g else slice(max(bb - 1, 0) * P, max(bb - 1, 0) * P + 2 * P)
                            if g == 0 and bb == 0:
                                MM(ps[:, 0:P], q[:, 0:P], k[:, 0:P], start=True, stop=True)
                                r = MM(ps[:, P:2 * P], q[:, 0:P], k[:, 0:P], start=True, stop=True)
                            else:
                                r = MM(ps[:, b * w:(b + 1) * w], q[:, bb * P:(bb + 1) * P], k[:, keys], start=True, stop=True)
                        done(r, ("sc", i))
                    if 1 <= i <= len(WU):
                        nexp += WU[i - 1][3]
                        ps = tile_of(("pt", i - 1))
                        pe.wait_ge(sem("b_exp"), nexp)
                        for b in range(4):
                            r = TR(ps[:, b * P:(b + 1) * P], bP[:, (i - 1) % 2, b * P:(b + 1) * P], ident)
                        done(r, ("pt", i - 1))
                    if i in (0, 1, 2, 3, 5, 6, 7, 8):
                        fill(1)
                    if i >= 2:
                        g, h, b0, nb, w = WU[i - 2]
                        hh = 3 * g + h
                        p0 = hh % 2 * DH
                        ps = tile_of(("wpv", i - 2))
                        mix_freed(pe, ("pt", i - 2))
                        pt = bPT[:, (i - 2) % 2, :]
                        vs = lambda b: bV[:, g, b, h * DH:(h + 1) * DH]
                        for b in range(nb):
                            o_ = ps[p0:p0 + DH, b * P:(b + 1) * P]
                            if g == 0:
                                MM(o_, vs(max(b0 + b - 1, 0)), pt[:, 2 * b * P:2 * b * P + P], start=True, stop=False)
                                r = MM(o_, vs(b0 + b), pt[:, 2 * b * P + P:2 * b * P + 2 * P], start=False, stop=True)
                            else:
                                r = MM(o_, vs(b), pt[:, b * P:(b + 1) * P], start=True, stop=True)
                        done(r, ("wpv", i - 2))
                for n in range(2):
                    for g in range(3):
                        ps = tile_of(("st", n, g))
                        for b in range(NT):
                            r = TR(ps[0:3, b * P:(b + 1) * P], (w_m, w_z)[n][:, g, b, :], ident)
                        done(r, ("st", n, g))
                pe.wait_ge(sem("b_share"), 3)
                for t in range(5):
                    ps = tile_of(("bf", t))
                    for hh in (2 * t, 2 * t + 1):
                        if hh < 9:
                            g, h = hh // 3, hh % 3
                            r = MM(ps[hh % 2 * DH:hh % 2 * DH + DH, :], consts[0:3, CSEL + h * DH:CSEL + (h + 1) * DH], bFM[:, g, :], start=True, stop=True)
                    done(r, ("bf", t))
                pe.wait_ge(sem("b_olo"), 5)
                do("yb0")
                do("yb1")
                pe.wait_ge(sem("m_lo"), KT)
                do("o0")
                do("o1")
                pre("pre2")
                for g in range(8):
                    do(f"up{g}")
                for hf in range(2):
                    job = JOB[f"dn{hf}"]
                    for i in range(16):
                        pe.wait_ge(sem("f_lo"), 16 * hf + i + 1)
                        unit(job, i)

        with nc.Fori(0, DEPTH) as l:
            with nc.Block() as block:
                build_layer(l, block)
            with nc.Block() as block:
                @block.sync
                def _(sp):
                    for s in sems.values():
                        sp.sem_clear(s)

        with nc.Block() as block:
            @block.sync
            def _(sp):
                stored = once
                sp.dma_start(out.rearrange("a (t p) d -> p (a t) d", p=P), xv).then_inc(stored, 16)
                sp.wait_ge(stored, 48)


_NAMES = ["x", "norm_pre_mix", "norm_post_mix", "norm_pre_mlp", "norm_post_mlp", "w_in", "conv_w", "a_log",
          "dt_bias", "gdn_norm", "ret_norm", "w_br_a", "w_br_b", "w_br_c", "w_br_d", "w_o", "w_mlp_in", "w_mlp_out"]


def small_weights(a):
    out = []
    for l in range(DEPTH):
        cols = lambda v: v.reshape(-1, P).T
        rows = lambda v: np.broadcast_to(v[None, :], (P, v.shape[0]))
        out.append(np.concatenate(
            [cols(a["norm_pre_mix"][l]), cols(a["norm_pre_mlp"][l]), cols(a["gdn_norm"][l]), cols(a["ret_norm"][l]),
             *[cols(a["conv_w"][l, tap]) for tap in range(4)], rows(a["a_log"][l]), rows(a["dt_bias"][l])], 1))
    return np.ascontiguousarray(np.stack(out))


def kernel(**inputs):
    import concourse.bacc as bacc
    from concourse.bass_utils import run_bass_kernel_spmd

    nc = bacc.Bacc("TRN2", target_bir_lowering=False, num_devices=1)
    arrays = {n: np.ascontiguousarray(inputs[n]) for n in _NAMES}
    arrays["small"] = small_weights(arrays)
    arrays["consts"] = shape_constants()
    arrays["tables"] = shape_tables()
    aps = {n: nc.dram_tensor(f"in_{n}", a.shape, mybir.dt.from_np(a.dtype), kind="ExternalInput").ap()
           for n, a in arrays.items()}
    out = nc.dram_tensor("out_0", (1, S, DM), F32, kind="ExternalOutput").ap()
    hybrid_kernel(nc, aps, out)
    r = run_bass_kernel_spmd(nc, [{f"in_{n}": a for n, a in arrays.items()}], core_ids=[0])
    return r.results[0]["out_0"]
```

```python
import math
from contextlib import ExitStack

import numpy as np
import concourse.bass as bass
from concourse import mybir

F32 = mybir.dt.float32
F32R = mybir.dt.float32r
BF16 = mybir.dt.bfloat16
ALU = mybir.AluOpType
ACT = mybir.ActivationFunctionType
AX_X = mybir.AxisListType.X

P = 128
S = 512
NT = S // P
DM = 1024
KT = DM // P
DEPTH = 2
FF = 4 * DM
EPS = 1e-6
NEG = -1e30

C_GDN, C_Z, C_AB, C_DSWA, C_SB, C_RET, C_RV, C_RG, C_GATE = np.cumsum(
    [0, 1536, 512, 8, 1728, 1536, 512, 512, 512]).tolist()
GH, DK = 4, 128
DH = 64
SBH = 8
DIL = (1, 4, 4)
UK = 2
STAGES = 4
RING = 4

CI, CTU, CST, CLV, CNTL, CNON, CMG0, CMG1, CMG2, CSEL, CRD, CRR, CEND = np.cumsum(
    [0, P, P, P, 7 * P, P, P, 768, P, P, 3 * DH, P, P]).tolist()
TD, TRC, TRS, TWC, TWS, TEND = np.cumsum([0, 4 * S, S, S, S, S]).tolist()
LN1, LN2, LGN, LRN, LCW, LAL, LDT, LEND = np.cumsum([0, KT, KT, 1, 1, 48, GH, GH]).tolist()


def shape_constants():
    p = np.arange(P)[:, None]
    c = np.arange(P)[None, :]
    one = lambda m: m.astype(np.float32)
    neg = lambda m: np.where(m, 0.0, NEG).astype(np.float32)
    levels = []
    for n in range(7):
        z = 1 << n
        levels.append(one((c // (2 * z) == p // (2 * z)) & (c % (2 * z) >= z) & (p % (2 * z) < z)))
    k = np.arange(2 * P)[None, :]
    near = (k <= p + P) & (k >= p)
    first = (k <= p + P) & (k >= P)
    sel = np.zeros((P, 3 * DH), np.float32)
    for h in range(3):
        sel[h, h * DH:(h + 1) * DH] = 1.0

    def rotation(half):
        r = np.zeros((P, P), np.float32)
        for b in range(0, P, DH):
            for i in range(half):
                r[b + i + half, b + i] = -1.0
                r[b + i, b + i + half] = 1.0
        return r

    consts = np.concatenate(
        [one(p == c), one(c >= p), one(c > p), *levels, -one(c <= p), -np.ones((P, P), np.float32),
         neg(np.concatenate([first, near, near], 1)), neg(c <= p),
         neg((c <= p) & ((p - c) % 4 == 0)), sel, rotation(8), rotation(32)], 1)
    return np.ascontiguousarray(consts.astype(np.float32))


def shape_tables():
    p = np.arange(P)[:, None].astype(np.float64)
    c = np.arange(S)[None, :].astype(np.float64)
    out = []
    for h in range(4):
        lg = math.log1p(-2.0 ** (-5.0 - h))
        out.append(np.where(c >= p, np.exp((c - p) * lg), 0.0) * DH ** -0.5)
    pos = np.arange(S, dtype=np.float32)[None, :]
    lin = np.linspace(0.0, 1.0, 32, dtype=np.float32)
    fr = (np.float64(10000.0) ** -lin.astype(np.float64)).astype(np.float32)
    fw = (np.float64(500000.0) ** (-np.arange(0, 16, 2, dtype=np.float32).astype(np.float64) / 16)).astype(np.float32)
    for f, half in ((fr, 32), (fw, 8)):
        ang = (pos * f[:, None]).astype(np.float32)
        cos, sin = np.ones((DH, S)), np.zeros((DH, S))
        for b in (0, half):
            cos[b:b + half] = np.cos(ang.astype(np.float64))
            sin[b:b + half] = np.sin(ang.astype(np.float64))
        out += [np.tile(cos, (2, 1)), np.tile(sin, (2, 1))]
    return np.ascontiguousarray(np.concatenate(out, 1).astype(np.float32))


class Job:

    def __init__(self, name, w, c0, n, rows, kind, src, tiles=None, perm=0):
        self.name, self.w, self.c0, self.n, self.kind, self.src, self.perm = name, w, c0, n, kind, src, perm
        self.tiles = tiles or (n // P if kind == "T" else NT)
        self.units = []
        r = 0
        while r < rows:
            k = min(UK * P, rows - r)
            self.units.append((r, k))
            r += k


def make_jobs():
    jobs = []

    def add(*a, **k):
        jobs.append(Job(*a, **k))

    def gates(b):
        for hf in range(2):
            add(f"gate{b}{hf}", "w_in", C_GATE + "abcd".index(b) * DM + hf * 512, 512, DM, "T", "h")

    def branch(b, rows):
        for hf in range(2):
            add(f"y{b}{hf}", f"w_br_{b}", hf * 512, 512, rows, "T", "o")

    for n, c in (("aq", 0), ("ak", 512), ("av", 1024)):
        add(n, "w_in", C_GDN + c, 512, DM, "T", "h")
    add("aab", "w_in", C_AB, P, DM, "T", "h")
    gates("a")
    add("az", "w_in", C_Z, 512, DM, "T", "h")
    branch("a", 512)
    add("cq", "w_in", C_SB, 512, DM, "T", "h")
    add("ck", "w_in", C_SB + 512, 512, DM, "T", "h")
    add("cv", "w_in", C_SB + 1024, 512, DM, "N", "h")
    gates("c")
    branch("c", 512)
    add("dqk", "w_in", C_RET, 512, DM, "T", "h")
    add("dv", "w_in", C_RV, 512, DM, "N", "h")
    add("dg", "w_in", C_RG, 512, DM, "T", "h")
    gates("d")
    branch("d", 512)
    for i, n in enumerate("qk"):
        add(f"b{n}0", "w_in", C_DSWA + 576 * i, 512, DM, "T", "h")
    for i, n in enumerate("qk"):
        add(f"b{n}1", "w_in", C_DSWA + 576 * i + 512, P, DM, "T", "h")
    for g in range(3):
        add(f"bv{g}", "w_in", C_DSWA + 1152 + 192 * g, 192, DM, "N", "h", perm=g)
    gates("b")
    branch("b", 576)
    for hf in range(2):
        add(f"o{hf}", "w_o", hf * 512, 512, DM, "N", "h")
    for g in range(FF // 512):
        add(f"up{g}", "w_mlp_in", g * 512, 512, DM, "T", "h")
    for hf in range(2):
        add(f"dn{hf}", "w_mlp_out", hf * 512, 512, FF, "N", "f")
    return jobs


JOBS = make_jobs()
JOB = {j.name: j for j in JOBS}
UNITS = [(j, i) for j in JOBS for i in range(len(j.units))]


def number(keys, banks):
    return {k: (i % banks, i // banks + 1) for i, k in enumerate(keys)}


DN0 = next(i for i, (j, _) in enumerate(UNITS) if j.name == "dn0")
BIG = number([(j.name, t) for j in JOBS for t in range(j.tiles)], 4)


def window_units():
    out = []
    for g in range(3):
        for h in range(3):
            if g == 0:
                out += [(g, h, 0, 2, 2 * P), (g, h, 2, 2, 2 * P)]
            else:
                out.append((g, h, 0, 4, P))
    return out


WU = window_units()
WROPE = ([(("bq0", t), 0, t) for t in range(4)] + [(("bk0", t), 1, t) for t in range(4)]
         + [(("bq1", 0), 0, 4), (("bk1", 0), 1, 4)])
LEVELS = 7


def mixer_keys():
    k = [("pre1", i) for i in range(KT)]
    k += [("l2", i) for i in range(8)]
    k += ["ab", "gc"]
    for b in range(NT):
        k += [("R", b), ("B", b), ("LT", b), ("att", b), ("T0", b), ("kn", b), ("vn", b)]
        for n in range(1, LEVELS):
            k += [("Y", b, n, 0), ("Y", b, n, 1), ("X", b, n, 0), ("X", b, n, 1)]
        k += [("ks", b), ("new", b), ("o", b), ("dS", b)]
    k += [("an", h) for h in range(4)]
    for h in range(SBH + 1):
        for j in reversed(range(NT)):
            if h < SBH:
                k.append(("z", h, j))
        if h >= 1:
            k += [("cs", h - 1, j) for j in range(NT)]
            if h % 2 == 0:
                k.append(("cpv", h // 2 - 1))
    k += [("drot", i) for i in range(4)]
    for h in range(4):
        k += [("dz", h, j) for j in range(NT)] + [("dpv", h), ("dn", h)]
    k += [("brot", i) for i in range(10)]
    for i in range(len(WU) + 2):
        if i < len(WU):
            k.append(("sc", i))
        if 1 <= i <= len(WU):
            k.append(("pt", i - 1))
        if i >= 2:
            k.append(("wpv", i - 2))
    k += [("st", n, g) for n in range(2) for g in range(3)]
    k += [("bf", t) for t in range(5)]
    k += [("pre2", i) for i in range(KT)]
    return k


MIX = number(mixer_keys(), 4)


def hybrid_kernel(nc, ins, out):
    ctx = ExitStack()
    with ctx:
        def sb(name, n, dt=F32):
            return ctx.enter_context(nc.sbuf_tensor(name, [P, n], dt))

        x_sb = sb("x_sb", NT * DM)
        h_hi, h_lo = sb("h_hi", KT * S, F32R), sb("h_lo", KT * S, F32R)
        o_hi, o_lo = sb("o_hi", 5 * S, F32R), sb("o_lo", 5 * S, F32R)
        stage = sb("stage", STAGES * UK * S)
        ring_hi, ring_lo = sb("ring_hi", RING * UK * S, F32R), sb("ring_lo", RING * UK * S, F32R)
        consts = sb("consts", CEND)
        ones = sb("ones", P)
        idb, strictb = sb("idb", P, BF16), sb("strictb", P, BF16)
        lw = sb("lw", LEND)
        st = sb("st", 320)
        scr = sb("scr", 19712)
        big = [ctx.enter_context(nc.psum_tensor(f"big{i}", [P, S], F32)) for i in range(4)]
        mxb = [ctx.enter_context(nc.psum_tensor(f"mix{i}", [P, S], F32)) for i in range(4)]

        def at(t, base, k, n, w=S):
            return t[:, base + k * w:base + k * w + n]

        xv = x_sb[:, :].rearrange("p (t d) -> p t d", t=NT)
        hH, hL = (t[:, :].rearrange("p (k s) -> p k s", s=S) for t in (h_hi, h_lo))
        oH, oL = (t[:, :].rearrange("p (k s) -> p k s", s=S) for t in (o_hi, o_lo))
        rH, rL = (t[:, :].rearrange("p (r k s) -> p r k s", r=RING, s=S) for t in (ring_hi, ring_lo))
        stg = stage[:, :].rearrange("p (r k s) -> p r k s", r=STAGES, s=S)
        ident = consts[:, CI:CI + P]
        triu = consts[:, CTU:CTU + P]
        strict = consts[:, CST:CST + P]

        def sview(base, k, w=S):
            return scr[:, base:base + k * w].rearrange("p (k w) -> p k w", w=w)

        mixed, sg = sview(0, KT), sview(4096, KT)
        MB = 8192
        fT = sview(0, FF // P)
        hn = scr[:, MB:MB + 4096].rearrange("p (t d) -> p t d", t=NT)
        yhalf = (sview(FF // P * S, NT), sview(0, NT))
        postw = scr[:, FF // P * S + 2048:FF // P * S + 2048 + DM]
        aQ, aK, aV = sview(MB, 4), sview(MB + 2048, 4), sview(MB + 4096, 4)
        (g_eR, g_dec, g_kb, g_LT, g_att, g_LTm, _, _, g_Y, g_kd) = (
            scr[:, MB + 6144 + i * S:MB + 6144 + (i + 1) * S].rearrange("p (h c) -> p h c", h=GH) for i in range(10))
        g_TU = scr[:, MB + 6144 + 6 * S:MB + 6144 + 8 * S].rearrange("p (c t w) -> p c t w", c=2, t=2)
        g_T = lambda h: g_TU[:, h // 2, 0, h % 2 * P:h % 2 * P + P]
        g_U = lambda h: g_TU[:, h // 2, 1, h % 2 * P:h % 2 * P + P]
        g_Uh = lambda c: g_TU[:, c, 1, :].rearrange("p (h w) -> p h w", h=2)
        g_S = scr[:, 0:S].rearrange("p (h c) -> p h c", h=GH)
        g_sq, g_rs = sview(S, 2), sview(3 * S, 2)
        g_ab = scr[0:8, 5 * S:6 * S]
        g_cv = sview(6 * S, 2)
        g_vb = scr[:, 6 * S:7 * S].rearrange("p (h c) -> p h c", h=GH)
        cQ, cK = sview(MB, 4), sview(MB + 2048, 4)
        cV = sview(MB + 4096, 4)
        OFF = [0, 512, 896, 1152]
        c_sp = [scr[:, MB + 6144 + i * 1280:MB + 6144 + (i + 1) * 1280] for i in range(2)]
        c_A = [scr[:, MB + 8704 + i * 1280:MB + 8704 + (i + 1) * 1280] for i in range(2)]
        dQK, dV, dG = sview(MB, 4), sview(MB + 2048, 4), sview(MB + 4096, 4)
        dTab = scr[:, MB + 6144:MB + 6144 + 3072]
        dX, dY = sview(MB + 4096, 4), sview(MB + 10240, 2)
        dP = sview(MB + 9216, 4)
        dO, dSq = scr[:, MB + 8192:MB + 8704], scr[:, MB + 8704:MB + 9216]
        bQ, bK = sview(MB, 5), sview(MB + 2560, 5)
        bV = scr[:, MB + 5120:MB + 5120 + 2304].rearrange("p (g b c) -> p g b c", g=3, b=4)
        bP, bPT = sview(MB + 7424, 2), sview(MB + 8448, 2)
        bX = sview(MB + 8448, 4)
        bTab = scr[:, MB + 10496:MB + 11520]
        bFM = scr[0:3, MB + 2560:MB + 2560 + 1536].rearrange("p (g s) -> p g s", g=3)
        bFZ = scr[0:3, MB + 5120:MB + 5120 + 1536].rearrange("p (g s) -> p g s", g=3)
        bFS = scr[0:3, MB + 7424:MB + 7424 + 512]
        n_v, n_y, n_t = (st[:, 4 * i:4 * i + 4] for i in range(3))
        n_ss = st[:, 296:304]
        s16 = [st[:, 16 + 16 * i:32 + 16 * i].rearrange("p (b h) -> p b h", b=4) for i in range(10)]
        s_a, s_e, s_l, s_g, s_be, s_gc, s_ed, s_b1, s_gl, s_ea = s16
        w_m, w_nm, w_z = (st[:, 176 + 36 * i:212 + 36 * i].rearrange("p (g b h) -> p g b h", g=3, b=4) for i in range(3))

        sems = {}

        def sem(name):
            if name not in sems:
                sems[name] = ctx.enter_context(nc.semaphore(name))
            return sems[name]

        once = ctx.enter_context(nc.semaphore("once"))
        idready = ctx.enter_context(nc.semaphore("idready"))

        def big_wait(eng, key):
            b, k = BIG[key]
            eng.wait_ge(sem(f"big_done{b}"), k)
            return big[b]

        def mix_wait(eng, key):
            b, k = MIX[key]
            eng.wait_ge(sem(f"mix_done{b}"), k)
            return mxb[b]

        def big_free(ins_, key):
            return ins_.then_inc(sem(f"big_free{BIG[key][0]}"), 1)

        def mix_free(ins_, key):
            return ins_.then_inc(sem(f"mix_free{MIX[key][0]}"), 1)

        def mix_freed(eng, key):
            b, k = MIX[key]
            eng.wait_ge(sem(f"mix_free{b}"), k)

        def big_freed(eng, key):
            b, k = BIG[key]
            eng.wait_ge(sem(f"big_free{b}"), k)

        def heads(t):
            return t[:, 0:S].rearrange("p (h c) -> p h c", h=GH)

        def f32(ap):
            return ap.bitcast(F32)

        with nc.Block() as block:
            @block.sync
            def _(sp):
                sp.dma_start(xv, ins["x"].rearrange("a (t p) d -> p (a t) d", p=P)).then_inc(once, 16)
                sp.dma_start(consts[:, :], ins["consts"]).then_inc(once, 16)

            @block.vector
            def _(dve):
                nc.vector.memset(ones[:, :], 1.0).then_inc(idready, 1)
                dve.wait_ge(once, 32)
                nc.vector.tensor_copy(idb[:, :], ident).then_inc(idready, 1)
                nc.vector.tensor_scalar(strictb[:, :], strict, -NEG, NEG, ALU.mult, ALU.add).then_inc(idready, 1)

        def build_layer(l, block):
            @block.sync
            def _(sp):
                sp.dma_start(lw[:, :], ins["small"][bass.ds(l, 1), :, :].rearrange("a p n -> p (a n)")).then_inc(sem("small_loaded"), 16)
                for u, (job, i) in enumerate(UNITS):
                    if u >= STAGES:
                        sp.wait_ge(sem("w_ready"), u - STAGES + 1)
                    r0, rows = job.units[i]
                    w = ins[job.w]
                    src = w[bass.ds(l, 1), r0:r0 + rows, job.c0:job.c0 + job.n]
                    s = u % STAGES
                    if rows >= P:
                        sp.dma_start(stg[:, s, 0:rows // P, 0:job.n],
                                     src.rearrange("a (t p) n -> p (a t) n", p=P)).then_inc(sem(f"w_loaded{s}"), 16)
                    else:
                        sp.dma_start(stg[0:rows, s, 0, 0:job.n],
                                     src.rearrange("a p n -> p (a n)")).then_inc(sem(f"w_loaded{s}"), 16)

            @block.gpsimd
            def _(pool):
                for u, (job, i) in enumerate(UNITS):
                    r0, rows = job.units[i]
                    s, r = u % STAGES, u % RING
                    pp, kk = min(rows, P), max(rows // P, 1)
                    pool.wait_ge(sem(f"w_loaded{s}"), 16 * (u // STAGES + 1))
                    if u >= RING:
                        pool.wait_ge(sem("w_used"), u - RING + 1)
                    w = stg[0:pp, s, 0:kk, 0:job.n]
                    nc.gpsimd.tensor_scalar(rH[0:pp, r, 0:kk, 0:job.n], w, 1.0, 0.0, ALU.mult, ALU.add).then_inc(sem("w_hi"), 1)
                    pool.wait_ge(sem("w_hi"), u + 1)
                    nc.gpsimd.tensor_tensor(rL[0:pp, r, 0:kk, 0:job.n], w, f32(rH[0:pp, r, 0:kk, 0:job.n]),
                                            ALU.subtract).then_inc(sem("w_ready"), 1)

            @block.scalar
            def _(act):
                A = nc.scalar.activation

                def exp_ln_tables():
                    nc.scalar.preload_act_table_set("natural_log_exp_and_others")

                exp_ln_tables()

                def norm_stats(src, ready, tag):
                    for t in range(NT):
                        ready(t)
                        A(hn[:, t, :], src[:, t, :], ACT.Square, scale=DM ** -0.5,
                          accum_out=n_ss[:, t:t + 1]).then_inc(sem(f"{tag}_ss"), 1)
                    act.wait_ge(sem(f"{tag}_v"), 1)
                    A(n_t, n_v, ACT.Ln).then_inc(sem(f"{tag}_ln"), 1)
                    act.wait_ge(sem(f"{tag}_ln"), 1)
                    A(n_y, n_t, ACT.Exp, scale=-0.5).then_inc(sem(f"{tag}_y"), 1)

                def split_hi(tag, nw, kk=KT):
                    for k in range(kk):
                        ps = mix_wait(act, (tag, k))
                        A(hH[:, k, :], ps[:, :], ACT.Copy, scale=lw[:, nw + k:nw + k + 1]).then_inc(sem(f"{tag}_hi"), 1)

                def gate_copy(b, hf):
                    if hf == 0 and b != "a":
                        prev = {"c": "a", "d": "c", "b": "d"}[b]
                        big_freed(act, (f"y{prev}1", 3))
                    for i in range(4):
                        ps = big_wait(act, (f"gate{b}{hf}", i))
                        big_free(A(sg[:, 4 * hf + i, :], ps[:, :], ACT.Copy), (f"gate{b}{hf}", i))

                def gate_sigmoid(b):
                    for hf in range(2):
                        big_freed(act, (f"gate{b}{hf}", 3))
                        A(sg[:, 4 * hf:4 * hf + 4, :], sg[:, 4 * hf:4 * hf + 4, :], ACT.Sigmoid).then_inc(sem(f"sig{b}"), 1)

                act.wait_ge(sem("small_loaded"), 16)
                norm_stats(xv, lambda t: None, "n1")
                split_hi("pre1", LN1)
                for i in range(12):
                    big_freed(act, (("aq", "ak", "av")[i // 4], i % 4))
                    dst = (aQ, aK, aV)[i // 4][:, i % 4, :]
                    A(dst, g_cv[:, i % 2, :], ACT.Silu).then_inc(sem("a_silu"), 1)
                exp_ln_tables()
                big_freed(act, ("av", 3))
                ps = big_wait(act, ("aab", 0))
                big_free(A(g_ab, ps[0:8, :], ACT.Copy), ("aab", 0))
                for i in range(-1, 8):
                    if i < 7:
                        if i >= 1:
                            mix_wait(act, ("l2", i - 1))
                        else:
                            act.wait_ge(sem("a_silu"), i + 2)
                        A(g_sq[:, (i + 1) % 2, :], (aQ, aK)[(i + 1) // 4][:, (i + 1) % 4, :], ACT.Square).then_inc(sem("a_sq"), 1)
                    if i < 0:
                        continue
                    if i >= 2:
                        act.wait_ge(sem("a_l2"), i - 1)
                    ps = mix_wait(act, ("l2", i))
                    mix_free(A(g_rs[:, i % 2, :], ps[:, :], ACT.Ln, bias=EPS), ("l2", i))
                    mix_freed(act, ("l2", i))
                    A(g_rs[:, i % 2, :], g_rs[:, i % 2, :], ACT.Exp, scale=-0.5).then_inc(sem("a_rs"), 1)
                act.wait_ge(sem("a_small"), 2)
                A(s_e, s_e, ACT.Exp, scale=-1.0).then_inc(sem("a_smallact"), 1)
                A(s_be, s_be, ACT.Exp, scale=-1.0).then_inc(sem("a_smallact"), 1)
                A(s_ea[:, 0, :], lw[:, LAL:LAL + GH], ACT.Exp).then_inc(sem("a_smallact"), 1)
                act.wait_ge(sem("a_smallact"), 1)
                A(s_l, s_e, ACT.Ln, bias=1.0).then_inc(sem("a_smallact"), 1)
                gate_copy("a", 0)
                for b in range(NT):
                    ps = mix_wait(act, ("R", b))
                    if b:
                        mix_freed(act, ("dS", b - 1))
                    A(g_eR, heads(ps), ACT.Exp).then_inc(sem("a_eR"), 1)
                    act.wait_ge(sem("a_min"), b + 1)
                    A(g_dec, g_dec, ACT.Exp).then_inc(sem("a_dec"), 1)
                    act.wait_ge(sem("a_edarg"), b + 1)
                    A(s_ed[:, b, :], s_ed[:, b, :], ACT.Exp).then_inc(sem("a_ed"), 1)
                    ps = mix_wait(act, ("T0", b))
                    mix_free(A(g_TU[:, :, 0, :], ps[:, :].rearrange("p (c w) -> p c w", c=2), ACT.Copy), ("T0", b))
                    for n in range(1, LEVELS):
                        for c in range(2):
                            ps = mix_wait(act, ("Y", b, n, c))
                            mix_free(A(g_Y[:, 2 * c:2 * c + 2, :], ps[:, 0:2 * P].rearrange("p (h w) -> p h w", h=2), ACT.Copy), ("Y", b, n, c))
                    if b == 3:
                        gate_copy("a", 1)
                    ps = mix_wait(act, ("new", b))
                    mix_free(A(g_Y, heads(ps), ACT.Copy), ("new", b))
                    ps = mix_wait(act, ("o", b))
                    mix_free(A(aQ[:, :, b * P:(b + 1) * P], heads(ps), ACT.Copy), ("o", b))

                def head_squares(o, sq, tag):
                    A(sq, o, ACT.Square, scale=P ** -0.5).then_inc(sem(f"{tag}_sq"), 1)

                def head_root(h, key, rs, tag):
                    ps = mix_wait(act, key)
                    mix_free(A(rs, ps[:, :], ACT.Ln, bias=EPS), key)
                    mix_freed(act, key)
                    A(rs, rs, ACT.Exp, scale=-0.5).then_inc(sem(f"{tag}_rs"), 1)

                def o_split(tag, i, src, rows=P):
                    if tag == "b":
                        mix_freed(act, ("bf", i))
                    else:
                        act.wait_ge(sem(f"{tag}_out"), i + 1)
                    if i == 0 and tag != "a":
                        big_freed(act, ({"d": "yc1", "b": "yd1"}[tag], 3))
                    A(oH[0:rows, i, :], src, ACT.Copy).then_inc(sem(f"{tag}_ohi"), 1)

                mix_freed(act, ("o", NT - 1))
                for h in range(-1, 4):
                    if h < 3:
                        if h >= 1:
                            mix_wait(act, ("an", h - 1))
                        head_squares(aQ[:, h + 1, :], g_sq[:, (h + 1) % 2, :], "an")
                    if h >= 0:
                        if h >= 2:
                            act.wait_ge(sem("a_nrm"), h - 1)
                        head_root(h, ("an", h), g_rs[:, h % 2, :], "an")
                for i in range(4):
                    ps = big_wait(act, ("az", i))
                    big_free(A(aK[:, i, :], ps[:, :], ACT.Silu), ("az", i))
                for h in range(4):
                    o_split("a", h, aQ[:, h, :])
                gate_sigmoid("a")
                exp_ln_tables()
                act.wait_ge(sem("a_olo"), 4)
                for i in range(4):
                    ps = big_wait(act, ("cq", i))
                    big_free(A(cQ[:, i, :], ps[:, :], ACT.Copy, scale=DH ** -0.5), ("cq", i))
                for i in range(4):
                    ps = big_wait(act, ("ck", i))
                    big_free(A(cK[:, i, :], ps[:, :], ACT.Copy), ("ck", i))
                for i in range(4):
                    ps = big_wait(act, ("cv", i))
                    big_free(A(cV[:, i, :], ps[:, :], ACT.Copy), ("cv", i))

                def stick_A(h):
                    for j in range(NT):
                        n = S - j * P
                        ps = mix_wait(act, ("cs", h, j))
                        if h >= 2 and j == 0:
                            mix_wait(act, ("cpv", h // 2 - 1))
                        mix_free(A(c_A[h % 2][:, OFF[j]:OFF[j] + n], ps[:, 0:n], ACT.Exp), ("cs", h, j))

                for h in range(SBH + 1):
                    if h < SBH:
                        for j in reversed(range(NT)):
                            n = S - j * P
                            sl = c_sp[h % 2][:, OFF[j]:OFF[j] + n]
                            ps = mix_wait(act, ("z", h, j))
                            if h >= 2 and j == NT - 1:
                                mix_wait(act, ("cs", h - 2, NT - 1))
                            c = 3 * (NT * h + NT - 1 - j)
                            A(sl, ps[:, 0:n], ACT.Abs).then_inc(sem("c_act"), 1)
                            act.wait_ge(sem("c_act"), c + 1)
                            A(sl, sl, ACT.Exp, scale=-1.0).then_inc(sem("c_act"), 1)
                            act.wait_ge(sem("c_act"), c + 2)
                            A(sl, sl, ACT.Ln, bias=1.0).then_inc(sem("c_act"), 1)
                    if h >= 1:
                        stick_A(h - 1)
                    if h % 2 == 0 and h:
                        i = h // 2 - 1
                        ps = mix_wait(act, ("cpv", i))
                        if i == 0:
                            big_freed(act, ("ya1", 3))
                        A(oH[:, i, :], ps[:, :], ACT.Copy).then_inc(sem("c_ohi"), 1)
                    if h == 2:
                        gate_copy("c", 0)
                    if h == 5:
                        gate_copy("c", 1)
                gate_sigmoid("c")
                exp_ln_tables()
                mix_freed(act, ("cpv", 3))
                act.dma_start(dTab, ins["tables"][:, TD:TD + 3072]).then_inc(sem("tab"), 16)
                for i in range(4):
                    ps = big_wait(act, ("dqk", i))
                    big_free(A(dX[:, i, :], ps[:, :], ACT.Copy), ("dqk", i))
                for i in range(4):
                    ps = big_wait(act, ("dv", i))
                    big_free(A(dV[:, i, :], ps[:, :], ACT.Copy), ("dv", i))
                act.wait_ge(sem("d_rope"), 4)
                for i in range(4):
                    ps = big_wait(act, ("dg", i))
                    big_free(A(dG[:, i, :], ps[:, :], ACT.Silu), ("dg", i))
                exp_ln_tables()
                for h in range(4):
                    ps = mix_wait(act, ("dpv", h))
                    if h:
                        act.wait_ge(sem("d_out"), h)
                        o_split("d", h - 1, dG[:, h - 1, :])
                    else:
                        act.wait_ge(sem("d_rope"), 4)
                    mix_free(A(dO, ps[:, :], ACT.Copy), ("dpv", h))
                    mix_freed(act, ("dpv", h))
                    head_squares(dO, dSq, "dn")
                    head_root(h, ("dn", h), dSq, "dn")
                    if h == 1:
                        gate_copy("d", 0)
                    if h == 3:
                        gate_copy("d", 1)
                o_split("d", 3, dG[:, 3, :])
                gate_sigmoid("d")
                exp_ln_tables()
                act.wait_ge(sem("d_olo"), 4)
                act.dma_start(bTab, ins["tables"][:, TWC:TWC + 1024]).then_inc(sem("tab"), 16)
                def window_v(g):
                    for t in range(4):
                        ps = big_wait(act, (f"bv{g}", t))
                        big_free(A(bV[:, g, t, :], ps[:, 0:192], ACT.Copy), (f"bv{g}", t))

                for i, (key, _, _) in enumerate(WROPE):
                    ps = big_wait(act, key)
                    if i >= 4:
                        act.wait_ge(sem("b_rope"), i - 3)
                    big_free(A(bX[:, i % 4, :], ps[:, :], ACT.Copy), key)
                for g in range(3):
                    window_v(g)
                nexp = 0
                for i in range(len(WU) + 2):
                    if i < len(WU):
                        g, h, b0, nb, w = WU[i]
                        act.wait_ge(sem("b_nm"), i + 1)
                        pv = bP[:, i % 2, :].rearrange("p (b w) -> p b w", w=w)
                        for b in range(nb):
                            A(pv[:, b, :], pv[:, b, :], ACT.Exp, bias=w_nm[:, g, b0 + b, h:h + 1],
                              accum_out=w_z[:, g, b0 + b, h:h + 1]).then_inc(sem("b_exp"), 1)
                            nexp += 1
                    if 1 <= i <= len(WU):
                        ps = mix_wait(act, ("pt", i - 1))
                        if i >= 3:
                            mix_wait(act, ("wpv", i - 3))
                        mix_free(A(bPT[:, (i - 1) % 2, :], ps[:, :], ACT.Copy), ("pt", i - 1))
                    if i >= 2:
                        g, h, b0, nb, w = WU[i - 2]
                        hh = 3 * g + h
                        p0, tl = hh % 2 * DH, hh // 2
                        ps = mix_wait(act, ("wpv", i - 2))
                        if g == 0:
                            o_, i_ = bQ[p0:p0 + DH, tl, b0 * P:(b0 + nb) * P], ps[p0:p0 + DH, 0:nb * P]
                        else:
                            o_ = bQ[p0:p0 + DH, tl, :].rearrange("p (l r) -> p r l", r=DIL[g])
                            i_ = ps[p0:p0 + DH, :].rearrange("p (r l) -> p r l", r=DIL[g])
                        mix_free(A(o_, i_, ACT.Copy), ("wpv", i - 2))
                    if i == 4:
                        gate_copy("b", 0)
                for n in range(2):
                    for g in range(3):
                        ps = mix_wait(act, ("st", n, g))
                        o_ = (bFM, bFZ)[n][:, g, :]
                        i_ = ps[0:3, :]
                        if g:
                            o_ = o_.rearrange("p (l r) -> p r l", r=DIL[g])
                            i_ = i_.rearrange("p (r l) -> p r l", r=DIL[g])
                        mix_free(A(o_, i_, ACT.Copy), ("st", n, g))
                act.wait_ge(sem("b_fac"), 3)
                A(bFM, bFM, ACT.Exp).then_inc(sem("b_fexp"), 1)
                gate_copy("b", 1)
                for i in range(5):
                    r = P if i < 4 else DH
                    o_split("b", i, bQ[0:r, i, :], r)
                gate_sigmoid("b")
                exp_ln_tables()
                for k in range(KT):
                    act.wait_ge(sem("mixed"), k + 1)
                    A(hH[:, k, :], mixed[:, k, :], ACT.Copy).then_inc(sem("m_hi"), 1)

                def y_squares(jobs, hf, tag):
                    for t in range(NT):
                        ps = big_wait(act, (f"{jobs}{hf}", t))
                        n = NT * hf + t
                        if n:
                            act.wait_ge(sem(f"{tag}_ss"), n)
                        A(oH[:, 0, :], ps[:, :], ACT.Square, scale=DM ** -0.5, accum_out=n_ss[:, n:n + 1]).then_inc(sem(f"{tag}_ss"), 1)

                def post_weights(norm):
                    act.dma_start(postw, ins[norm][bass.ds(l, 1), :].to_broadcast((P, DM))).then_inc(sem("postw"), 16)

                def root(tag):
                    act.wait_ge(sem(f"{tag}_v"), 1)
                    A(n_t, n_v, ACT.Ln).then_inc(sem(f"{tag}_ln"), 1)
                    act.wait_ge(sem(f"{tag}_ln"), 1)
                    A(n_y, n_t, ACT.Exp, scale=-0.5).then_inc(sem(f"{tag}_y"), 1)


                act.wait_ge(sem("b_olo"), 5)
                post_weights("norm_post_mix")
                for hf in range(2):
                    y_squares("o", hf, "n2")
                root("n2")
                norm_stats(xv, lambda t: act.wait_ge(sem("n2_x"), 2 * t + 2), "n3")
                post_weights("norm_post_mlp")
                split_hi("pre2", LN2)
                for g in range(8):
                    for i in range(4):
                        ps = big_wait(act, (f"up{g}", i))
                        if g == 0 and i == 0:
                            mix_freed(act, ("pre2", KT - 1))
                        A(fT[:, 4 * g + i, :], ps[:, :], ACT.Relu).then_inc(sem("f_relu"), 1)
                for hf in range(2):
                    for u in range(16):
                        n = 16 * hf + u
                        if n == 0:
                            for i in range(4):
                                big_freed(act, ("up7", i))
                        if n == 19:
                            y_squares("dn", 0, "n4")
                        if n >= 4:
                            act.wait_ge(sem("w_used"), DN0 + n - 3)
                        q = n % 4 * 2
                        A(hH[:, q:q + 2, :], fT[:, 2 * u:2 * u + 2, :], ACT.Copy).then_inc(sem("f_hi"), 1)
                y_squares("dn", 1, "n4")
                root("n4")

            @block.vector
            def _(dve):
                V = nc.vector
                TT, TS, STT = V.tensor_tensor, V.tensor_scalar, V.scalar_tensor_tensor

                def rstd(tag):
                    c = sem(f"{tag}_nw")
                    if tag in ("n2", "n4"):
                        dve.wait_ge(sem(f"{tag}_ss"), 2 * NT)
                        STT(n_v, n_ss[:, 0:NT], EPS, n_ss[:, NT:2 * NT], ALU.add, ALU.add).then_inc(sem(f"{tag}_v"), 1)
                    else:
                        dve.wait_ge(sem(f"{tag}_ss"), NT)
                        V.tensor_scalar_add(n_v, n_ss[:, 0:NT], EPS).then_inc(sem(f"{tag}_v"), 1)
                    dve.wait_ge(sem(f"{tag}_y"), 1)
                    TT(n_t, n_y, n_y, ALU.mult).then_inc(c, 1)
                    dve.wait_ge(c, 1)
                    TT(n_t, n_t, n_v, ALU.mult).then_inc(c, 1)
                    dve.wait_ge(c, 2)
                    TS(n_t, n_t, -0.5, 1.5, ALU.mult, ALU.add).then_inc(c, 1)
                    dve.wait_ge(c, 3)
                    TT(n_y, n_y, n_t, ALU.mult).then_inc(c, 1)
                    dve.wait_ge(c, 4)

                def pre(tag, ntag, nw):
                    rstd(ntag)
                    for t in range(NT):
                        TS(hn[:, t, :], xv[:, t, :], n_y[:, t:t + 1], None, ALU.mult).then_inc(sem(f"{tag}_h"), 1)
                    for k in range(KT):
                        ps = mix_wait(dve, (tag, k))
                        dve.wait_ge(sem(f"{tag}_hi"), k + 1)
                        mix_free(STT(hL[:, k, :], ps[:, :], lw[:, nw + k:nw + k + 1], f32(hH[:, k, :]), ALU.mult, ALU.subtract), (tag, k))

                def o_lo_split(tag, i, src, rows=P):
                    dve.wait_ge(sem(f"{tag}_ohi"), i + 1)
                    TT(oL[0:rows, i, :], src, f32(oH[0:rows, i, :]), ALU.subtract).then_inc(sem(f"{tag}_olo"), 1)

                def gated(b):
                    for hf in range(2):
                        for i in range(4):
                            k = 4 * hf + i
                            ps = big_wait(dve, (f"y{b}{hf}", i))
                            dve.wait_ge(sem(f"sig{b}"), hf + 1)
                            if b == "a":
                                big_free(TT(mixed[:, k, :], ps[:, :], sg[:, k, :], ALU.mult), (f"y{b}{hf}", i))
                            else:
                                big_free(TT(sg[:, k, :], ps[:, :], sg[:, k, :], ALU.mult), (f"y{b}{hf}", i))
                                big_freed(dve, (f"y{b}{hf}", i))
                                TT(mixed[:, k, :], mixed[:, k, :], sg[:, k, :], ALU.add).then_inc(sem(f"mixed_{b}") if b != "b" else sem("mixed"), 1)

                def per_head(ap4):
                    return ap4.unsqueeze(2).to_broadcast((P, GH, P))

                def two(ap):
                    return ap.unsqueeze(1).to_broadcast((P, 2, P))

                def level_mask(b, n, c):
                    if n == 1:
                        dve.wait_ge(sem("a_U"), 2 * b + 2)
                    else:
                        mix_wait(dve, ("Y", b, n - 1, c))
                    hs = slice(2 * c, 2 * c + 2)
                    TT(g_LTm[:, hs, :], g_LT[:, hs, :], two(consts[:, CLV + n * P:CLV + (n + 1) * P]), ALU.mult).then_inc(sem("a_LTm"), 1)

                def per_mask(ap):
                    return ap.unsqueeze(1).to_broadcast((P, GH, P))

                pre("pre1", "n1", LN1)
                V.memset(g_S, 0.0).then_inc(sem("a_S0"), 1)
                dve.wait_ge(sem("small_loaded"), 16)
                mix_wait(dve, ("pre1", KT - 1))
                n = 0
                for i in range(12):
                    key = (("aq", "ak", "av")[i // 4], i % 4)
                    ps = big_wait(dve, key)
                    if i >= 2:
                        dve.wait_ge(sem("a_silu"), i - 1)
                    cv = g_cv[:, i % 2, :]
                    tap = lambda q: lw[:, LCW + 12 * q + i:LCW + 12 * q + i + 1]
                    TS(cv, ps[:, :], tap(3), None, ALU.mult).then_inc(sem("a_tap"), 1)
                    for q in (1, 2):
                        dve.wait_ge(sem("a_tap"), 3 * i + q)
                        STT(cv[:, q:], ps[:, 0:S - q], tap(3 - q), cv[:, q:], ALU.mult, ALU.add).then_inc(sem("a_tap"), 1)
                    dve.wait_ge(sem("a_tap"), 3 * i + 3)
                    big_free(STT(cv[:, 3:], ps[:, 0:S - 3], tap(0), cv[:, 3:], ALU.mult, ALU.add), key)
                for i in range(8):
                    dve.wait_ge(sem("a_rs"), i + 1)
                    t = (aQ, aK)[i // 4][:, i % 4, :]
                    STT(t, t, DK ** -0.5 if i < 4 else 1.0, g_rs[:, i % 2, :], ALU.mult, ALU.mult).then_inc(sem("a_l2"), 1)
                ps = mix_wait(dve, "ab")
                abv = ps[:, 0:32].rearrange("p (b c) -> p b c", b=4)
                c = sem("a_sc")
                TT(s_a, abv[:, :, 0:4], lw[:, LDT:LDT + GH].unsqueeze(1).to_broadcast((P, 4, GH)), ALU.add).then_inc(c, 1)
                mix_free(V.tensor_scalar_max(s_be, abv[:, :, 4:8], -80.0), "ab")
                dve.wait_ge(c, 1)
                mix_freed(dve, "ab")
                STT(s_e, s_a, -1.0, s_a, ALU.mult, ALU.max).then_inc(sem("a_small"), 1)
                TS(s_a, s_a, 0.0, None, ALU.max).then_inc(sem("a_small"), 1)
                dve.wait_ge(sem("a_smallact"), 4)
                TT(s_g, s_a, s_l, ALU.add).then_inc(c, 1)
                V.tensor_scalar_add(s_be, s_be, 1.0).then_inc(c, 1)
                dve.wait_ge(c, 2)
                STT(s_g, s_g, -1.0, s_ea[:, 0, :].unsqueeze(1).to_broadcast((P, 4, GH)), ALU.mult, ALU.mult).then_inc(sem("a_g"), 1)
                dve.wait_ge(c, 3)
                V.reciprocal(s_be, s_be).then_inc(sem("a_g"), 1)
                ps = mix_wait(dve, "gc")
                mix_free(V.tensor_copy(s_gc, ps[:, 0:16].rearrange("p (b h) -> p b h", b=4)), "gc")
                mix_freed(dve, "gc")
                for b in range(NT):
                    bs = slice(b * P, (b + 1) * P)
                    ps = mix_wait(dve, ("R", b))
                    R = heads(ps)
                    dve.wait_ge(sem("a_eR"), b + 1)
                    TT(s_ed[:, b, :], R[:, :, P - 1], s_gc[:, b, :], ALU.subtract).then_inc(sem("a_edarg"), 1)
                    mix_free(TT(g_dec, R, per_head(s_gc[:, b, :]), ALU.subtract), ("R", b))
                    mix_freed(dve, ("R", b))
                    V.tensor_scalar_min(g_dec, g_dec, 0.0).then_inc(sem("a_min"), 1)
                    ps = mix_wait(dve, ("B", b))
                    mix_free(TT(g_kb, aK[:, :, bs], heads(ps), ALU.mult), ("B", b))
                    dve.wait_ge(sem("a_dec"), b + 1)
                    TT(g_dec, g_dec, per_mask(triu), ALU.mult).then_inc(sem("a_decm"), 1)
                    dve.wait_ge(sem("a_decm"), b + 1)
                    ps = mix_wait(dve, ("LT", b))
                    mix_free(TT(g_LT, heads(ps), g_dec, ALU.mult), ("LT", b))
                    ps = mix_wait(dve, ("att", b))
                    mix_free(TT(g_att, heads(ps), g_dec, ALU.mult), ("att", b))
                    mix_freed(dve, ("LT", b))
                    TT(g_LTm, g_LT, per_mask(consts[:, CLV:CLV + P]), ALU.mult).then_inc(sem("a_LTm"), 1)
                    dve.wait_ge(sem("a_LTm"), 1 + (2 * LEVELS - 1) * b)
                    for c in range(2):
                        TT(g_Uh(c), two(ident), g_LTm[:, 2 * c:2 * c + 2, :], ALU.subtract).then_inc(sem("a_U"), 1)
                    for c in range(2):
                        level_mask(b, 1, c)
                    TT(aQ[:, :, bs], aQ[:, :, bs], g_eR, ALU.mult).then_inc(sem("a_qd"), 1)
                    TT(g_kb, g_kb, g_eR, ALU.mult).then_inc(sem("a_kbe"), 1)
                    ps = mix_wait(dve, ("kn", b))
                    dve.wait_ge(sem("a_ed"), b + 1)
                    mix_free(TT(g_kd, heads(ps), per_head(s_ed[:, b, :]), ALU.mult), ("kn", b))
                    ps = mix_wait(dve, ("vn", b))
                    mix_free(TT(g_vb, heads(ps), per_head(s_be[:, b, :]), ALU.mult), ("vn", b))
                    for n in range(1, LEVELS):
                        if n < LEVELS - 1:
                            for c in range(2):
                                level_mask(b, n + 1, c)
                        for c in range(2):
                            ps = mix_wait(dve, ("X", b, n, c))
                            if n < LEVELS - 1:
                                mix_free(TT(g_TU[:, c, :, :], g_TU[:, c, :, :], ps[:, :].rearrange("p (t w) -> p t w", t=2), ALU.subtract), ("X", b, n, c))
                            else:
                                mix_free(TT(g_TU[:, c, 1, :], g_TU[:, c, 1, :], ps[:, 2 * P:4 * P], ALU.subtract), ("X", b, n, c))
                            if n < LEVELS - 1:
                                mix_freed(dve, ("X", b, n, c))
                    ps = mix_wait(dve, ("ks", b))
                    mix_free(TT(g_vb, g_vb, heads(ps), ALU.subtract), ("ks", b))
                    ps = mix_wait(dve, ("dS", b))
                    for h in range(GH):
                        i = STT(g_S[:, h, :], g_S[:, h, :], g_eR[:, h, P - 1:P], ps[:, h * P:(h + 1) * P], ALU.mult, ALU.add)
                    mix_free(i, ("dS", b))

                def head_normed(h, o, rs, tag):
                    dve.wait_ge(sem(f"{tag}n_rs"), h + 1)
                    TT(o, o, rs, ALU.mult).then_inc(sem(f"{tag}_nrm"), 1)

                def head_out(h, o, w, gate, dst, tag):
                    dve.wait_ge(sem(f"{tag}_nrm"), h + 1)
                    STT(dst, o, lw[:, w:w + 1], gate, ALU.mult, ALU.mult).then_inc(sem(f"{tag}_out"), 1)

                for h in range(4):
                    head_normed(h, aQ[:, h, :], g_rs[:, h % 2, :], "a")
                for h in range(4):
                    big_freed(dve, ("az", h))
                    head_out(h, aQ[:, h, :], LGN, aK[:, h, :], aQ[:, h, :], "a")
                    if h:
                        o_lo_split("a", h - 1, aQ[:, h - 1, :])
                o_lo_split("a", 3, aQ[:, 3, :])
                gated("a")
                for h in range(SBH + 1):
                    if h < SBH:
                        for j in reversed(range(NT)):
                            n = S - j * P
                            c = NT * h + NT - 1 - j
                            ps = mix_wait(dve, ("z", h, j))
                            sl = c_sp[h % 2][:, OFF[j]:OFF[j] + n]
                            dve.wait_ge(sem("c_act"), 3 * c + 3)
                            mix_free(STT(sl, ps[:, 0:n], 0.0, sl, ALU.max, ALU.add), ("z", h, j))
                            mix_freed(dve, ("z", h, j))
                            TT(sl[:, 0:P], sl[:, 0:P], strict, ALU.mult).then_inc(sem("c_sp"), 1)
                    if h % 2 == 0 and h:
                        i = h // 2 - 1
                        ps = mix_wait(dve, ("cpv", i))
                        dve.wait_ge(sem("c_ohi"), i + 1)
                        mix_free(TT(oL[:, i, :], ps[:, :], f32(oH[:, i, :]), ALU.subtract), ("cpv", i))
                gated("c")

                def rope(i, key, x, cos, sin, t1, t2, dsts, tag):
                    ps = mix_wait(dve, key)
                    n = sem(f"{tag}_rp")
                    if i:
                        dve.wait_ge(sem(f"{tag}_rope"), i)
                    TT(t1, x, cos, ALU.mult).then_inc(n, 1)
                    mix_free(TT(t2, ps[:, :], sin, ALU.mult), key)
                    dve.wait_ge(n, i + 1)
                    mix_freed(dve, key)
                    for q, (r0, r1, dst, dil) in enumerate(dsts):
                        a, b_ = t1[r0:r1, :], t2[r0:r1, :]
                        if dil > 1:
                            dst = dst.rearrange("p (r l) -> p r l", r=dil)
                            a = a.rearrange("p (l r) -> p r l", r=dil)
                            b_ = b_.rearrange("p (l r) -> p r l", r=dil)
                        ins_ = TT(dst, a, b_, ALU.add)
                        if q == len(dsts) - 1:
                            ins_.then_inc(sem(f"{tag}_rope"), 1)

                dve.wait_ge(sem("tab"), 16)
                mix_freed(dve, ("cpv", 3))
                for i in range(4):
                    rope(i, ("drot", i), dX[:, i, :], dTab[:, TRC:TRC + S], dTab[:, TRS:TRS + S],
                         dY[:, 0, :], dY[:, 1, :], [(0, P, dQK[:, i, :], 1)], "d")
                for h in range(4):
                    for j in range(NT):
                        n = S - j * P
                        ps = mix_wait(dve, ("dz", h, j))
                        if h:
                            mix_wait(dve, ("dpv", h - 1))
                        else:
                            dve.wait_ge(sem("d_rope"), 4)
                        mix_free(TT(dP[:, j, 0:n], ps[:, 0:n], dTab[:, TD + S * h:TD + S * h + n], ALU.mult), ("dz", h, j))
                    if h == 0:
                        for i in range(4):
                            big_freed(dve, ("dg", i))
                    if h:
                        o_lo_split("d", h - 1, dG[:, h - 1, :])
                    head_normed(h, dO, dSq, "d")
                    head_out(h, dO, LRN, dG[:, h, :], dG[:, h, :], "d")
                o_lo_split("d", 3, dG[:, 3, :])
                gated("d")
                dve.wait_ge(sem("tab"), 32)
                for i, (_, q, tl) in enumerate(WROPE):
                    dst = (bQ, bK)[q]
                    half = [(0, DH, dst[0:DH, tl, :], DIL[2 * tl // 3]), (DH, P, dst[DH:P, tl, :], DIL[min((2 * tl + 1) // 3, 2)])]
                    rope(i, ("brot", i), bX[:, i % 4, :], bTab[:, 0:S], bTab[:, S:2 * S],
                         bP[:, 0, :], bP[:, 1, :], half if tl < 4 else half[:1], "b")
                for i, (g, h, b0, nb, w) in enumerate(WU):
                    ps = mix_wait(dve, ("sc", i))
                    if i == 0:
                        dve.wait_ge(sem("b_rope"), 10)
                    if i >= 2:
                        mix_wait(dve, ("pt", i - 2))
                    if g == 0:
                        mask = consts[:, CMG0 + b0 * 128:CMG0 + b0 * 128 + 512].rearrange("p (b w) -> p b w", w=w)
                    else:
                        m0 = (CMG1, CMG2)[g - 1]
                        mask = consts[:, m0:m0 + P].unsqueeze(1).to_broadcast((P, 4, P))
                    pv = bP[:, i % 2, :].rearrange("p (b w) -> p b w", w=w)
                    mix_free(STT(pv, ps[:, :].rearrange("p (b w) -> p b w", w=w), DH ** -0.5, mask, ALU.mult, ALU.add), ("sc", i))
                    mix_freed(dve, ("sc", i))
                    V.reduce_max(w_m[:, g, b0:b0 + nb, h], pv, AX_X).then_inc(sem("b_max"), 1)
                    dve.wait_ge(sem("b_max"), i + 1)
                    TS(w_nm[:, g, b0:b0 + nb, h], w_m[:, g, b0:b0 + nb, h], -1.0, None, ALU.mult).then_inc(sem("b_nm"), 1)
                for n in range(2):
                    for g in range(3):
                        mix_freed(dve, ("st", n, g))
                fc = sem("b_fc")
                TT(bFS, bFM[:, 0, :], bFM[:, 1, :], ALU.max).then_inc(fc, 1)
                dve.wait_ge(fc, 1)
                TT(bFS, bFS, bFM[:, 2, :], ALU.max).then_inc(fc, 1)
                dve.wait_ge(fc, 2)
                for g in range(3):
                    TT(bFM[:, g, :], bFM[:, g, :], bFS, ALU.subtract).then_inc(sem("b_fac"), 1)
                dve.wait_ge(sem("b_fexp"), 1)
                TT(bFZ, bFZ, bFM, ALU.mult).then_inc(fc, 1)
                dve.wait_ge(fc, 3)
                TT(bFS, bFZ[:, 0, :], bFZ[:, 1, :], ALU.add).then_inc(fc, 1)
                dve.wait_ge(fc, 4)
                TT(bFS, bFS, bFZ[:, 2, :], ALU.add).then_inc(fc, 1)
                dve.wait_ge(fc, 5)
                V.reciprocal(bFS, bFS).then_inc(fc, 1)
                dve.wait_ge(fc, 6)
                for g in range(3):
                    TT(bFM[:, g, :], bFM[:, g, :], bFS, ALU.mult).then_inc(sem("b_share"), 1)
                for i in range(5):
                    r = P if i < 4 else DH
                    ps = mix_wait(dve, ("bf", i))
                    mix_free(TT(bQ[0:r, i, :], bQ[0:r, i, :], ps[0:r, :], ALU.mult), ("bf", i))
                for i in range(5):
                    r = P if i < 4 else DH
                    o_lo_split("b", i, bQ[0:r, i, :], r)
                gated("b")
                for k in range(KT):
                    dve.wait_ge(sem("m_hi"), k + 1)
                    TT(hL[:, k, :], mixed[:, k, :], f32(hH[:, k, :]), ALU.subtract).then_inc(sem("m_lo"), 1)

                def y_weighted(jobs, hf, tag):
                    for t in range(NT):
                        ps = big_wait(dve, (f"{jobs}{hf}", t))
                        dve.wait_ge(sem(f"{tag}_ss"), NT * hf + t + 1)
                        big_free(TT(yhalf[hf][:, t, :], ps[:, :], postw[:, hf * 512:hf * 512 + 512], ALU.mult), (f"{jobs}{hf}", t))

                def residual(jobs, tag):
                    rstd(tag)
                    for t in range(NT):
                        for hf in range(2):
                            cs = slice(hf * 512, hf * 512 + 512)
                            big_freed(dve, (f"{jobs}{hf}", t))
                            STT(xv[:, t, cs], yhalf[hf][:, t, :], n_y[:, t:t + 1], xv[:, t, cs], ALU.mult, ALU.add).then_inc(sem(f"{tag}_x"), 1)

                dve.wait_ge(sem("postw"), 16)
                for hf in range(2):
                    y_weighted("o", hf, "n2")
                residual("o", "n2")
                pre("pre2", "n3", LN2)
                for g in range(8):
                    for i in range(4):
                        k = 4 * g + i
                        ps = big_wait(dve, (f"up{g}", i))
                        dve.wait_ge(sem("f_relu"), k + 1)
                        big_free(STT(fT[:, k, :], ps[:, :], 0.0, fT[:, k, :], ALU.max, ALU.mult), (f"up{g}", i))
                for hf in range(2):
                    for u in range(16):
                        n = 16 * hf + u
                        if n == 19:
                            dve.wait_ge(sem("postw"), 32)
                            y_weighted("dn", 0, "n4")
                        dve.wait_ge(sem("f_hi"), n + 1)
                        q = n % 4 * 2
                        TT(hL[:, q:q + 2, :], fT[:, 2 * u:2 * u + 2, :], f32(hH[:, q:q + 2, :]), ALU.subtract).then_inc(sem("f_lo"), 1)
                y_weighted("dn", 1, "n4")
                residual("dn", "n4")
                dve.wait_ge(sem("n4_x"), 2 * NT)

            @block.tensor
            def _(pe):
                MM, TR = nc.tensor.matmul, nc.tensor.transpose
                state = {"u": 0}

                def unit(job, i):
                    u = state["u"]
                    assert UNITS[u][0] is job and UNITS[u][1] == i
                    slot = u % RING
                    r0, rows = job.units[i]
                    kts = [(r0 // P + k, min(P, rows - k * P)) for k in range(max(1, -(-rows // P)))]
                    pe.wait_ge(sem("w_ready"), u + 1)
                    sH, sL = (oH, oL) if job.src == "o" else (hH, hL)
                    last_unit = i == len(job.units) - 1
                    first = True
                    for t in range(job.tiles):
                        b, use = BIG[(job.name, t)]
                        if i == 0 and use > 1:
                            pe.wait_ge(sem(f"big_free{b}"), use - 1)
                        for k, (kt, rr) in enumerate(kts):
                            ks = (2 * (i % 4) + k) if job.src == "f" else kt
                            for m, (wt, xt) in enumerate(((rH, sH), (rL, sH), (rH, sL))):
                                if job.kind == "T":
                                    o_ = big[b][:, 0:S]
                                    a_, r_ = wt[0:rr, slot, k, t * P:(t + 1) * P], xt[0:rr, ks, :]
                                else:
                                    o_ = big[b][:, 0:job.n]
                                    d = DIL[job.perm]
                                    if job.perm == 0:
                                        a_ = xt[0:rr, ks, t * P:(t + 1) * P]
                                    else:
                                        a_ = xt[0:rr, ks, :].rearrange("p (l r) -> p r l", r=d)
                                        a_ = a_[:, t, :]
                                    r_ = wt[0:rr, slot, k, 0:job.n]
                                s0 = i == 0 and k == 0 and m == 0
                                s1 = last_unit and k == len(kts) - 1 and m == 2
                                ins_ = MM(o_, a_, r_, start=s0, stop=s1)
                                if s1:
                                    ins_.then_inc(sem(f"big_done{b}"), 1)
                                elif first and u > 0:
                                    ins_.then_inc(sem("w_used"), 1)
                                first = False
                    state["u"] += 1

                def do(name, need=None, between=None):
                    job = JOB[name]
                    for i in range(len(job.units)):
                        if need:
                            need(i)
                        unit(job, i)
                        if between:
                            between(i)

                fills = []

                def fill(n=1):
                    for _ in range(n):
                        if fills:
                            unit(*fills.pop(0))

                def set_fill(b):
                    fills.extend((JOB[f"gate{b}{hf}"], i) for hf in range(2) for i in range(4))

                order = iter(MIX)

                def tile_of(key):
                    assert next(order) == key, key
                    b, k = MIX[key]
                    if k > 1:
                        pe.wait_ge(sem(f"mix_free{b}"), k - 1)
                    return mxb[b]

                def done(ins_, key):
                    ins_.then_inc(sem(f"mix_done{MIX[key][0]}"), 1)

                def pre(tag):
                    for k in range(KT):
                        ps = tile_of((tag, k))
                        pe.wait_ge(sem(f"{tag}_h"), NT)
                        for t in range(NT):
                            i = TR(ps[:, t * P:(t + 1) * P], hn[:, t, k * P:(k + 1) * P], ident)
                        done(i, (tag, k))

                def pre_split(tag):
                    return lambda i: [mix_freed(pe, (tag, k)) for k in (2 * i, 2 * i + 1)]

                pre("pre1")
                do("aq", pre_split("pre1"))
                for n in ("ak", "av", "aab"):
                    do(n)
                set_fill("a")
                for i in range(8):
                    ps = tile_of(("l2", i))
                    pe.wait_ge(sem("a_sq"), i + 1)
                    done(MM(ps[:, :], ones[:, :], g_sq[:, i % 2, :], start=True, stop=True), ("l2", i))
                    if i in (0, 3, 5):
                        fill(1)
                ps = tile_of("ab")
                big_freed(pe, ("aab", 0))
                for t in range(NT):
                    i = TR(ps[:, 8 * t:8 * t + 8], g_ab[:, t * P:(t + 1) * P], ident[0:8, 0:8])
                done(i, "ab")
                fill(1)
                pe.wait_ge(sem("a_g"), 2)
                ps = tile_of("gc")
                done(MM(ps[:, 0:16], triu, st[:, 64:80], start=True, stop=True), "gc")
                pe.wait_ge(sem("a_l2"), 8)
                for b in range(NT):
                    bs = slice(b * P, (b + 1) * P)
                    ps = tile_of(("R", b))
                    for h in range(GH):
                        i = MM(ps[:, h * P:(h + 1) * P], s_g[:, b, h:h + 1].to_broadcast((P, P)), triu, start=True, stop=True)
                    done(i, ("R", b))
                    ps = tile_of(("B", b))
                    for h in range(GH):
                        i = MM(ps[:, h * P:(h + 1) * P], s_be[:, b, h:h + 1].to_broadcast((P, P)), ident, start=True, stop=True)
                    done(i, ("B", b))
                    ps = tile_of(("LT", b))
                    mix_freed(pe, ("B", b))
                    for h in range(GH):
                        i = MM(ps[:, h * P:(h + 1) * P], aK[:, h, bs], g_kb[:, h, :], start=True, stop=True)
                    done(i, ("LT", b))
                    ps = tile_of(("att", b))
                    for h in range(GH):
                        i = MM(ps[:, h * P:(h + 1) * P], aK[:, h, bs], aQ[:, h, bs], start=True, stop=True)
                    done(i, ("att", b))
                    fill(1)
                    ps = tile_of(("T0", b))
                    pe.wait_ge(sem("a_U"), 2 * b + 2)
                    for h in range(GH):
                        i = TR(ps[:, h * P:(h + 1) * P], g_U(h), ident)
                    done(i, ("T0", b))
                    ps = tile_of(("kn", b))
                    for h in range(GH):
                        i = TR(ps[:, h * P:(h + 1) * P], aK[:, h, bs], ident)
                    done(i, ("kn", b))
                    ps = tile_of(("vn", b))
                    for h in range(GH):
                        i = TR(ps[:, h * P:(h + 1) * P], aV[:, h, bs], ident)
                    done(i, ("vn", b))
                    for n in range(1, LEVELS):
                        for c in range(2):
                            ps = tile_of(("Y", b, n, c))
                            pe.wait_ge(sem("a_LTm"), (2 * LEVELS - 1) * b + 2 * n + c)
                            mix_freed(pe, ("T0", b) if n == 1 else ("X", b, n - 1, c))
                            for q in range(2):
                                i = MM(ps[:, q * P:(q + 1) * P], g_LTm[:, 2 * c + q, :], g_T(2 * c + q), start=True, stop=True)
                            done(i, ("Y", b, n, c))
                        for c in range(2):
                            ps = tile_of(("X", b, n, c))
                            mix_freed(pe, ("Y", b, n, c))
                            if n < LEVELS - 1:
                                for q in range(2):
                                    MM(ps[:, q * P:(q + 1) * P], g_U(2 * c + q), g_Y[:, 2 * c + q, :], start=True, stop=True)
                            for q in range(2):
                                i = MM(ps[:, (2 + q) * P:(3 + q) * P], g_Y[:, 2 * c + q, :], g_U(2 * c + q), start=True, stop=True)
                            done(i, ("X", b, n, c))
                    ps = tile_of(("ks", b))
                    pe.wait_ge(sem("a_kbe"), b + 1)
                    pe.wait_ge(sem("a_S0"), 1)
                    if b:
                        mix_freed(pe, ("dS", b - 1))
                    for h in range(GH):
                        i = MM(ps[:, h * P:(h + 1) * P], g_kb[:, h, :], g_S[:, h, :], start=True, stop=True)
                    done(i, ("ks", b))
                    ps = tile_of(("new", b))
                    for c in range(2):
                        mix_freed(pe, ("X", b, LEVELS - 1, c))
                    mix_freed(pe, ("ks", b))
                    for h in range(GH):
                        i = MM(ps[:, h * P:(h + 1) * P], g_U(h), g_vb[:, h, :], start=True, stop=True)
                    done(i, ("new", b))
                    ps = tile_of(("o", b))
                    pe.wait_ge(sem("a_qd"), b + 1)
                    mix_freed(pe, ("new", b))
                    mix_freed(pe, ("att", b))
                    for h in range(GH):
                        MM(ps[:, h * P:(h + 1) * P], g_S[:, h, :], aQ[:, h, bs], start=True, stop=False)
                        i = MM(ps[:, h * P:(h + 1) * P], g_Y[:, h, :], g_att[:, h, :], start=False, stop=True)
                    done(i, ("o", b))
                    ps = tile_of(("dS", b))
                    for h in range(GH):
                        i = MM(ps[:, h * P:(h + 1) * P], g_kd[:, h, :], g_Y[:, h, :], start=True, stop=True)
                    done(i, ("dS", b))
                fill(8)

                def head_mean(h):
                    ps = tile_of(("an", h))
                    pe.wait_ge(sem("an_sq"), h + 1)
                    done(MM(ps[:, :], ones[:, :], g_sq[:, h % 2, :], start=True, stop=True), ("an", h))

                do("az", between=head_mean)
                do("ya0", lambda i: pe.wait_ge(sem("a_olo"), 2 * i + 2))
                do("ya1")
                for n in ("cq", "ck", "cv"):
                    do(n)
                set_fill("c")
                for n in ("cq", "ck", "cv"):
                    for i in range(4):
                        big_freed(pe, (n, i))

                def hv(t, h):
                    return t[h % 2 * DH:h % 2 * DH + DH, h // 2, :]

                for h in range(SBH + 1):
                    if h < SBH:
                        for j in reversed(range(NT)):
                            n = S - j * P
                            ps = tile_of(("z", h, j))
                            done(MM(ps[:, 0:n], hv(cK, h)[:, j * P:(j + 1) * P], hv(cQ, h)[:, j * P:], start=True, stop=True), ("z", h, j))
                    if h in (0, 1, 2, 3, 4, 5):
                        fill(2 if h in (1, 4) else 1)
                    if h >= 1:
                        g = h - 1
                        pe.wait_ge(sem("c_sp"), NT * h)
                        for j in range(NT):
                            n = S - j * P
                            ps = tile_of(("cs", g, j))
                            MM(ps[:, 0:n], hv(cK, g)[:, j * P:(j + 1) * P], hv(cQ, g)[:, j * P:], start=True, stop=False)
                            MM(ps[:, 0:P], idb[:, :], strictb[:, :], start=False, stop=False)
                            i = MM(ps[:, 0:n], consts[:, CNTL:CNTL + P], c_sp[g % 2][:, OFF[j]:OFF[j] + n], start=False, stop=j == NT - 1)
                            for q in range(j + 1, NT):
                                i = MM(ps[:, (q - j) * P:n], consts[:, CNON:CNON + P], c_sp[g % 2][:, OFF[q]:OFF[q] + S - q * P],
                                       start=False, stop=q == NT - 1)
                            done(i, ("cs", g, j))
                    if h % 2 == 0 and h:
                        i = h // 2 - 1
                        ps = tile_of(("cpv", i))
                        for j in range(NT):
                            for g in (h - 2, h - 1):
                                mix_freed(pe, ("cs", g, j))
                                r = MM(ps[g % 2 * DH:g % 2 * DH + DH, j * P:], cV[:, j, g * DH:(g + 1) * DH],
                                       c_A[g % 2][:, OFF[j]:OFF[j] + S - j * P], start=j == 0, stop=j == NT - 1)
                        done(r, ("cpv", i))
                fill(8)
                do("yc0", lambda i: [mix_freed(pe, ("cpv", q)) for q in (2 * i, 2 * i + 1)])
                do("yc1")
                do("dqk")

                def d_rotate(i):
                    ps = tile_of(("drot", i))
                    big_freed(pe, ("dqk", i))
                    done(MM(ps[:, :], consts[:, CRR:CRR + P], dX[:, i, :], start=True, stop=True), ("drot", i))

                do("dv", between=d_rotate)
                do("dg")
                for i in range(4):
                    big_freed(pe, ("dv", i))
                set_fill("d")
                pe.wait_ge(sem("d_rope"), 4)
                for h in range(4):
                    for j in range(NT):
                        n = S - j * P
                        ps = tile_of(("dz", h, j))
                        q, k = dQK[:, h // 2, :], dQK[:, 2 + h // 2, :]
                        r0 = h % 2 * DH
                        done(MM(ps[:, 0:n], k[r0:r0 + DH, j * P:(j + 1) * P], q[r0:r0 + DH, j * P:], start=True, stop=True), ("dz", h, j))
                    fill(1)
                    ps = tile_of(("dpv", h))
                    for j in range(NT):
                        mix_freed(pe, ("dz", h, j))
                        r = MM(ps[:, j * P:], dV[:, j, h * P:(h + 1) * P], dP[:, j, 0:S - j * P], start=j == 0, stop=j == NT - 1)
                    done(r, ("dpv", h))
                    fill(1)
                    ps = tile_of(("dn", h))
                    pe.wait_ge(sem("dn_sq"), h + 1)
                    done(MM(ps[:, :], ones[:, :], dSq, start=True, stop=True), ("dn", h))
                do("yd0", lambda i: pe.wait_ge(sem("d_olo"), 2 * i + 2))
                do("yd1")
                def b_rotate(i):
                    ps = tile_of(("brot", i))
                    big_freed(pe, WROPE[i][0])
                    done(MM(ps[:, :], consts[:, CRD:CRD + P], bX[:, i % 4, :], start=True, stop=True), ("brot", i))

                do("bq0")
                do("bk0", between=b_rotate)
                do("bq1")
                b_rotate(4)
                do("bk1")
                b_rotate(5)
                do("bv0", between=lambda i: b_rotate(6 + i))
                do("bv1")
                do("bv2")
                for g in range(3):
                    for i in range(4):
                        big_freed(pe, (f"bv{g}", i))
                set_fill("b")
                pe.wait_ge(sem("b_rope"), 10)
                nexp = 0
                for i in range(len(WU) + 2):
                    if i < len(WU):
                        g, h, b0, nb, w = WU[i]
                        ps = tile_of(("sc", i))
                        hh = 3 * g + h
                        q, k = hv(bQ, hh), hv(bK, hh)
                        for b in range(nb):
                            bb = b0 + b
                            keys = slice(bb * P, (bb + 1) * P) if g else slice(max(bb - 1, 0) * P, max(bb - 1, 0) * P + 2 * P)
                            if g == 0 and bb == 0:
                                MM(ps[:, 0:P], q[:, 0:P], k[:, 0:P], start=True, stop=True)
                                r = MM(ps[:, P:2 * P], q[:, 0:P], k[:, 0:P], start=True, stop=True)
                            else:
                                r = MM(ps[:, b * w:(b + 1) * w], q[:, bb * P:(bb + 1) * P], k[:, keys], start=True, stop=True)
                        done(r, ("sc", i))
                    if 1 <= i <= len(WU):
                        nexp += WU[i - 1][3]
                        ps = tile_of(("pt", i - 1))
                        pe.wait_ge(sem("b_exp"), nexp)
                        for b in range(4):
                            r = TR(ps[:, b * P:(b + 1) * P], bP[:, (i - 1) % 2, b * P:(b + 1) * P], ident)
                        done(r, ("pt", i - 1))
                    if i in (0, 1, 2, 3, 6, 9):
                        fill(1)
                    if i >= 2:
                        g, h, b0, nb, w = WU[i - 2]
                        hh = 3 * g + h
                        p0 = hh % 2 * DH
                        ps = tile_of(("wpv", i - 2))
                        mix_freed(pe, ("pt", i - 2))
                        pt = bPT[:, (i - 2) % 2, :]
                        vs = lambda b: bV[:, g, b, h * DH:(h + 1) * DH]
                        for b in range(nb):
                            o_ = ps[p0:p0 + DH, b * P:(b + 1) * P]
                            if g == 0:
                                MM(o_, vs(max(b0 + b - 1, 0)), pt[:, 2 * b * P:2 * b * P + P], start=True, stop=False)
                                r = MM(o_, vs(b0 + b), pt[:, 2 * b * P + P:2 * b * P + 2 * P], start=False, stop=True)
                            else:
                                r = MM(o_, vs(b), pt[:, b * P:(b + 1) * P], start=True, stop=True)
                        done(r, ("wpv", i - 2))
                for n in range(2):
                    for g in range(3):
                        ps = tile_of(("st", n, g))
                        for b in range(NT):
                            r = TR(ps[0:3, b * P:(b + 1) * P], (w_m, w_z)[n][:, g, b, :], ident)
                        done(r, ("st", n, g))
                fill(8)
                pe.wait_ge(sem("b_share"), 3)
                for t in range(5):
                    ps = tile_of(("bf", t))
                    for hh in (2 * t, 2 * t + 1):
                        if hh < 9:
                            g, h = hh // 3, hh % 3
                            r = MM(ps[hh % 2 * DH:hh % 2 * DH + DH, :], consts[0:3, CSEL + h * DH:CSEL + (h + 1) * DH], bFM[:, g, :], start=True, stop=True)
                    done(r, ("bf", t))
                do("yb0", lambda i: pe.wait_ge(sem("b_olo"), min(2 * i + 2, 5)))
                do("yb1")
                do("o0", lambda i: pe.wait_ge(sem("m_lo"), 2 * i + 2))
                do("o1")
                pre("pre2")
                for g in range(8):
                    do(f"up{g}", None if g else pre_split("pre2"))
                for hf in range(2):
                    job = JOB[f"dn{hf}"]
                    for i in range(16):
                        pe.wait_ge(sem("f_lo"), 16 * hf + i + 1)
                        unit(job, i)

        with nc.Fori(0, DEPTH) as l:
            with nc.Block() as block:
                build_layer(l, block)
            with nc.Block() as block:
                @block.sync
                def _(sp):
                    for s in sems.values():
                        sp.sem_clear(s)

        with nc.Block() as block:
            @block.sync
            def _(sp):
                stored = once
                sp.dma_start(out.rearrange("a (t p) d -> p (a t) d", p=P), xv).then_inc(stored, 16)
                sp.wait_ge(stored, 48)


_NAMES = ["x", "norm_pre_mix", "norm_post_mix", "norm_pre_mlp", "norm_post_mlp", "w_in", "conv_w", "a_log",
          "dt_bias", "gdn_norm", "ret_norm", "w_br_a", "w_br_b", "w_br_c", "w_br_d", "w_o", "w_mlp_in", "w_mlp_out"]


def small_weights(a):
    out = []
    for l in range(DEPTH):
        cols = lambda v: v.reshape(-1, P).T
        rows = lambda v: np.broadcast_to(v[None, :], (P, v.shape[0]))
        out.append(np.concatenate(
            [cols(a["norm_pre_mix"][l]), cols(a["norm_pre_mlp"][l]), cols(a["gdn_norm"][l]), cols(a["ret_norm"][l]),
             *[cols(a["conv_w"][l, tap]) for tap in range(4)], rows(a["a_log"][l]), rows(a["dt_bias"][l])], 1))
    return np.ascontiguousarray(np.stack(out))


def kernel(**inputs):
    import concourse.bacc as bacc
    from concourse.bass_utils import run_bass_kernel_spmd

    nc = bacc.Bacc("TRN2", target_bir_lowering=False, num_devices=1)
    arrays = {n: np.ascontiguousarray(inputs[n]) for n in _NAMES}
    arrays["small"] = small_weights(arrays)
    arrays["consts"] = shape_constants()
    arrays["tables"] = shape_tables()
    aps = {n: nc.dram_tensor(f"in_{n}", a.shape, mybir.dt.from_np(a.dtype), kind="ExternalInput").ap()
           for n, a in arrays.items()}
    out = nc.dram_tensor("out_0", (1, S, DM), F32, kind="ExternalOutput").ap()
    hybrid_kernel(nc, aps, out)
    r = run_bass_kernel_spmd(nc, [{f"in_{n}": a for n, a in arrays.items()}], core_ids=[0])
    return r.results[0]["out_0"]
```

```python
import math
from contextlib import ExitStack

import numpy as np
import concourse.bass as bass
from concourse import mybir

F32 = mybir.dt.float32
F32R = mybir.dt.float32r
BF16 = mybir.dt.bfloat16
ALU = mybir.AluOpType
ACT = mybir.ActivationFunctionType
AX_X = mybir.AxisListType.X

P = 128
S = 512
NT = S // P
DM = 1024
KT = DM // P
DEPTH = 2
FF = 4 * DM
EPS = 1e-6
NEG = -1e30

C_GDN, C_Z, C_AB, C_DSWA, C_SB, C_RET, C_RV, C_RG, C_GATE = np.cumsum(
    [0, 1536, 512, 8, 1728, 1536, 512, 512, 512]).tolist()
GH, DK = 4, 128
DH = 64
SBH = 8
DIL = (1, 4, 4)
UK = 2
STAGES = 4
RING = 4

CI, CTU, CST, CLV, CNTL, CNTU, CMG0, CMG1, CMG2, CSEL, CRD, CRR, CEND = np.cumsum(
    [0, P, P, P, 7 * P, P, P, 768, P, P, 3 * DH, P, P]).tolist()
TD, TRC, TRS, TWC, TWS, TEND = np.cumsum([0, 4 * S, S, S, S, S]).tolist()
LN1, LN2, LGN, LRN, LCW, LAL, LDT, LEND = np.cumsum([0, KT, KT, 1, 1, 48, GH, GH]).tolist()


def shape_constants():
    p = np.arange(P)[:, None]
    c = np.arange(P)[None, :]
    one = lambda m: m.astype(np.float32)
    neg = lambda m: np.where(m, 0.0, NEG).astype(np.float32)
    levels = []
    for n in range(7):
        z = 1 << n
        levels.append(one((c // (2 * z) == p // (2 * z)) & (c % (2 * z) >= z) & (p % (2 * z) < z)))
    k = np.arange(2 * P)[None, :]
    near = (k <= p + P) & (k >= p)
    first = (k <= p + P) & (k >= P)
    sel = np.zeros((P, 3 * DH), np.float32)
    for h in range(3):
        sel[h, h * DH:(h + 1) * DH] = 1.0

    def rotation(half):
        r = np.zeros((P, P), np.float32)
        for b in range(0, P, DH):
            for i in range(half):
                r[b + i + half, b + i] = -1.0
                r[b + i, b + i + half] = 1.0
        return r

    consts = np.concatenate(
        [one(p == c), one(c >= p), one(c > p), *levels, -one(c <= p), -one(c > p),
         neg(np.concatenate([first, near, near], 1)), neg(c <= p),
         neg((c <= p) & ((p - c) % 4 == 0)), sel, rotation(8), rotation(32)], 1)
    return np.ascontiguousarray(consts.astype(np.float32))


def shape_tables():
    p = np.arange(P)[:, None].astype(np.float64)
    c = np.arange(S)[None, :].astype(np.float64)
    out = []
    for h in range(4):
        lg = math.log1p(-2.0 ** (-5.0 - h))
        out.append(np.where(c >= p, np.exp((c - p) * lg), 0.0) * DH ** -0.5)
    pos = np.arange(S, dtype=np.float32)[None, :]
    lin = np.linspace(0.0, 1.0, 32, dtype=np.float32)
    fr = (np.float64(10000.0) ** -lin.astype(np.float64)).astype(np.float32)
    fw = (np.float64(500000.0) ** (-np.arange(0, 16, 2, dtype=np.float32).astype(np.float64) / 16)).astype(np.float32)
    for f, half in ((fr, 32), (fw, 8)):
        ang = (pos * f[:, None]).astype(np.float32)
        cos, sin = np.ones((DH, S)), np.zeros((DH, S))
        for b in (0, half):
            cos[b:b + half] = np.cos(ang.astype(np.float64))
            sin[b:b + half] = np.sin(ang.astype(np.float64))
        out += [np.tile(cos, (2, 1)), np.tile(sin, (2, 1))]
    return np.ascontiguousarray(np.concatenate(out, 1).astype(np.float32))


class Job:

    def __init__(self, name, w, c0, n, rows, kind, src, tiles=None, perm=0):
        self.name, self.w, self.c0, self.n, self.kind, self.src, self.perm = name, w, c0, n, kind, src, perm
        self.tiles = tiles or (n // P if kind == "T" else NT)
        self.units = []
        r = 0
        while r < rows:
            k = min(UK * P, rows - r)
            self.units.append((r, k))
            r += k


def make_jobs():
    jobs = []

    def add(*a, **k):
        jobs.append(Job(*a, **k))

    def gate(b, hf):
        add(f"gate{b}{hf}", "w_in", C_GATE + "abcd".index(b) * DM + hf * 512, 512, DM, "T", "h")

    def gates(b):
        gate(b, 0)
        gate(b, 1)

    def branch(b, rows):
        for hf in range(2):
            add(f"y{b}{hf}", f"w_br_{b}", hf * 512, 512, rows, "T", "o")

    add("aq", "w_in", C_GDN, 512, DM, "T", "h")
    add("ak", "w_in", C_GDN + 512, 512, DM, "T", "h")
    add("aab", "w_in", C_AB, P, DM, "T", "h")
    add("av", "w_in", C_GDN + 1024, 512, DM, "T", "h")
    gate("a", 0)
    add("az", "w_in", C_Z, 512, DM, "T", "h")
    gate("a", 1)
    branch("a", 512)
    add("cq", "w_in", C_SB, 512, DM, "T", "h")
    add("ck", "w_in", C_SB + 512, 512, DM, "T", "h")
    add("cv", "w_in", C_SB + 1024, 512, DM, "N", "h")
    gates("c")
    branch("c", 512)
    add("dqk", "w_in", C_RET, 512, DM, "T", "h")
    add("dv", "w_in", C_RV, 512, DM, "N", "h")
    add("dg", "w_in", C_RG, 512, DM, "T", "h")
    gates("d")
    branch("d", 512)
    for i, n in enumerate("qk"):
        add(f"b{n}0", "w_in", C_DSWA + 576 * i, 512, DM, "T", "h")
    for i, n in enumerate("qk"):
        add(f"b{n}1", "w_in", C_DSWA + 576 * i + 512, P, DM, "T", "h")
    add("bv1", "w_in", C_DSWA + 1152 + 192, 384, DM, "N", "h", perm=1)
    add("bv0", "w_in", C_DSWA + 1152, 192, DM, "N", "h")
    gates("b")
    branch("b", 576)
    for hf in range(2):
        add(f"o{hf}", "w_o", hf * 512, 512, DM, "N", "h")
    for g in range(FF // 512):
        add(f"up{g}", "w_mlp_in", g * 512, 512, DM, "T", "h")
    for hf in range(2):
        add(f"dn{hf}", "w_mlp_out", hf * 512, 512, FF, "N", "f")
    return jobs


JOBS = make_jobs()
JOB = {j.name: j for j in JOBS}
UNITS = [(j, i) for j in JOBS for i in range(len(j.units))]


def number(keys, banks):
    return {k: (i % banks, i // banks + 1) for i, k in enumerate(keys)}


DN0 = next(i for i, (j, _) in enumerate(UNITS) if j.name == "dn0")
BIG = number([(j.name, t) for j in JOBS for t in range(j.tiles)], 4)


def window_units():
    out = []
    for g in range(3):
        for h in range(3):
            if g == 0:
                out += [(g, h, 0, 2, 2 * P), (g, h, 2, 2, 2 * P)]
            else:
                out.append((g, h, 0, 4, P))
    return out


WU = window_units()
WROPE = ([(("bq0", t), 0, t) for t in range(4)] + [(("bk0", t), 1, t) for t in range(4)]
         + [(("bq1", 0), 0, 4), (("bk1", 0), 1, 4)])
LEVELS = 7


def mixer_keys():
    k = [("pre1", i) for i in range(KT)]
    k += [("l2", i) for i in range(8)]
    k += ["ab", "gc"]
    for b in range(2):
        k += [("R", b), ("B", b), ("LT", b), ("att", b)]
    for b0 in (0, 2):
        k += [("T0", b0), ("T0", b0 + 1), ("kn", b0), ("vn", b0)]
        for n in range(1, LEVELS):
            k += [(t, b0 + e, n, c) for t in "YX" for e in range(2) for c in range(2)]
        for b in (b0, b0 + 1):
            ahead = b + 2 < NT
            if b > b0:
                k += [("kn", b), ("vn", b)] + ([("att", b + 1)] if ahead else [])
            k.append(("ks", b))
            k += [("R", b + 2), ("B", b + 2)] if ahead else []
            k.append(("new", b))
            k += [("LT", b + 2)] if ahead else []
            k += [("o", b), ("dS", b)]
        if b0 == 0:
            k.append(("att", 3))
    k += [("an", h) for h in range(4)]
    for h in range(SBH + 1):
        for j in reversed(range(NT)):
            if h < SBH:
                k.append(("z", h, j))
        if h >= 1:
            k += [("cs", h - 1, j) for j in range(NT)]
            if h % 2 == 0:
                k.append(("cpv", h // 2 - 1))
    k += [("drot", i) for i in range(4)]
    for h in range(4):
        k += [("dz", h, j) for j in range(NT)] + [("dpv", h), ("dn", h)]
    k += [("brot", i) for i in range(10)]
    for i in range(len(WU) + 2):
        if i < len(WU):
            k.append(("sc", i))
        if 1 <= i <= len(WU):
            k.append(("pt", i - 1))
        if i >= 2:
            k.append(("wpv", i - 2))
    k += [("st", n, g) for n in range(2) for g in range(3)]
    k += [("bf", t) for t in range(5)]
    k += [("pre2", i) for i in range(KT)]
    return k


MIX = number(mixer_keys(), 4)
EXACT = [k for k in MIX if k[0] in ("drot", "dn", "brot")]


def hybrid_kernel(nc, ins, out):
    ctx = ExitStack()
    with ctx:
        def sb(name, n, dt=F32):
            return ctx.enter_context(nc.sbuf_tensor(name, [P, n], dt))

        x_sb = sb("x_sb", NT * DM)
        h_hi, h_lo = sb("h_hi", KT * S, F32R), sb("h_lo", KT * S, F32R)
        o_hi, o_lo = sb("o_hi", 5 * S, F32R), sb("o_lo", 5 * S, F32R)
        stage = sb("stage", STAGES * UK * S)
        ring_hi, ring_lo = sb("ring_hi", RING * UK * S, F32R), sb("ring_lo", RING * UK * S, F32R)
        consts = sb("consts", CRD)
        ones_r, rot_r = sb("ones_r", P, F32R), sb("rot_r", 2 * P, F32R)
        ones = sb("ones", P)
        idb, strictb = sb("idb", P, BF16), sb("strictb", P, BF16)
        lw = sb("lw", LEND)
        st = sb("st", 320)
        scr = sb("scr", 19712)
        big = [ctx.enter_context(nc.psum_tensor(f"big{i}", [P, S], F32)) for i in range(4)]
        mxb = [ctx.enter_context(nc.psum_tensor(f"mix{i}", [P, S], F32)) for i in range(4)]

        xv = x_sb[:, :].rearrange("p (t d) -> p t d", t=NT)
        hH, hL = (t[:, :].rearrange("p (k s) -> p k s", s=S) for t in (h_hi, h_lo))
        oH, oL = (t[:, :].rearrange("p (k s) -> p k s", s=S) for t in (o_hi, o_lo))
        rH, rL = (t[:, :].rearrange("p (r k s) -> p r k s", r=RING, s=S) for t in (ring_hi, ring_lo))
        stg = stage[:, :].rearrange("p (r k s) -> p r k s", r=STAGES, s=S)
        ident = consts[:, CI:CI + P]
        triu = consts[:, CTU:CTU + P]
        strict = consts[:, CST:CST + P]

        def sview(base, k, w=S):
            return scr[:, base:base + k * w].rearrange("p (k w) -> p k w", w=w)

        mixed, sg = sview(0, KT), sview(4096, KT)
        MB = 8192
        fT = sview(0, FF // P)
        hn = scr[:, MB:MB + 4096].rearrange("p (t d) -> p t d", t=NT)
        yhalf = (sview(FF // P * S, NT), sview(0, NT))
        postw = scr[:, FF // P * S + 2048:FF // P * S + 2048 + DM]
        aQ, aK, aV = sview(MB, 4), sview(MB + 2048, 4), sview(MB + 4096, 4)
        gslot = lambda i: i * S if i < 8 else MB + 6144 + (i - 8) * S
        by_head = lambda i: scr[:, gslot(i):gslot(i) + S].rearrange("p (h c) -> p h c", h=GH)
        g_S, g_vb, g_kd, g_eR = (by_head(i) for i in (0, 6, 7, 8))
        g_kb, g_LT, g_att, g_LTm, g_Y = ([by_head(i) for i in two_] for two_ in ((5, 9), (10, 11), (12, 13), (14, 15), (16, 17)))
        g_TU = [scr[:, gslot(i):gslot(i + 2)].rearrange("p (c t w) -> p c t w", c=2, t=2) for i in (1, 3)]
        g_T = lambda e, h: g_TU[e][:, h // 2, 0, h % 2 * P:h % 2 * P + P]
        g_U = lambda e, h: g_TU[e][:, h // 2, 1, h % 2 * P:h % 2 * P + P]
        four = lambda ap: ap.rearrange("p c (q w) -> p c q w", q=2)
        g_dec, g_Uall = ([four(g_TU[e][:, :, t, :]) for e in range(2)] for t in range(2))
        level_half = lambda ap, n, odd: ap.rearrange("p (m t z) -> p m t z", t=2, z=1 << n)[:, :, odd, :]
        gate_at = lambda b, hf: aK if (b, hf) == ("a", 1) else sg[:, 4 * hf:4 * hf + 4, :]
        g_sq, g_rs = sview(S, 2), sview(3 * S, 2)
        g_ab = scr[0:8, 5 * S:6 * S]
        g_cv = sview(6 * S, 2)
        cQ, cK = sview(MB, 4), sview(MB + 2048, 4)
        cV = sview(MB + 4096, 4)
        OFF = [0, 512, 896, 1152]
        c_sp = [scr[:, MB + 6144 + i * 1280:MB + 6144 + (i + 1) * 1280] for i in range(2)]
        c_A = [scr[:, MB + 8704 + i * 1280:MB + 8704 + (i + 1) * 1280] for i in range(2)]
        dQK, dV, dG = sview(MB, 4), sview(MB + 2048, 4), sview(MB + 4096, 4)
        dTab = scr[:, MB + 6144:MB + 6144 + 3072]
        dX, dY = sview(MB + 4096, 4), sview(MB + 10240, 2)
        dP = sview(MB + 9216, 4)
        dO, dSq = scr[:, MB + 8192:MB + 8704], scr[:, MB + 8704:MB + 9216]
        bQ, bK = sview(MB, 5), sview(MB + 2560, 5)
        bV = scr[:, MB + 5120:MB + 5120 + 2304].rearrange("p (g b c) -> p g b c", g=3, b=4)
        bP, bPT = sview(MB + 7424, 2), sview(MB + 8448, 2)
        bX = sview(MB + 8448, 4)
        bTab = scr[:, MB + 10496:MB + 11520]
        bFM = scr[0:3, MB + 2560:MB + 2560 + 1536].rearrange("p (g s) -> p g s", g=3)
        bFZ = scr[0:3, MB + 5120:MB + 5120 + 1536].rearrange("p (g s) -> p g s", g=3)
        bFS = scr[0:3, MB + 7424:MB + 7424 + 512]
        n_v, n_y, n_t, n_h = (st[:, 4 * i:4 * i + 4] for i in range(4))
        n_ss = st[:, 296:304]
        s16 = [st[:, 16 + 16 * i:32 + 16 * i].rearrange("p (b h) -> p b h", b=4) for i in range(10)]
        s_a, s_e, s_l, s_g, s_be, s_gc, s_ed, _, s_gl, s_ea = s16
        w_m, w_nm, w_z = (st[:, 176 + 36 * i:212 + 36 * i].rearrange("p (g b h) -> p g b h", g=3, b=4) for i in range(3))

        sems = {}

        def sem(name):
            if name not in sems:
                sems[name] = ctx.enter_context(nc.semaphore(name))
            return sems[name]

        x_loaded = [ctx.enter_context(nc.semaphore(f"x_loaded{t}")) for t in range(NT)]
        consts_loaded = ctx.enter_context(nc.semaphore("consts_loaded"))
        rots_loaded = ctx.enter_context(nc.semaphore("rots_loaded"))
        exact_ready = ctx.enter_context(nc.semaphore("exact_ready"))
        ones_ready = ctx.enter_context(nc.semaphore("ones_ready"))
        stored = ctx.enter_context(nc.semaphore("stored"))

        def big_wait(eng, key):
            b, k = BIG[key]
            eng.wait_ge(sem(f"big_done{b}"), k)
            return big[b]

        def mix_wait(eng, key):
            b, k = MIX[key]
            eng.wait_ge(sem(f"mix_done{b}"), k)
            return mxb[b]

        def big_free(ins_, key):
            return ins_.then_inc(sem(f"big_free{BIG[key][0]}"), 1)

        def mix_free(ins_, key):
            return ins_.then_inc(sem(f"mix_free{MIX[key][0]}"), 1)

        def mix_freed(eng, key):
            b, k = MIX[key]
            eng.wait_ge(sem(f"mix_free{b}"), k)

        def big_freed(eng, key):
            b, k = BIG[key]
            eng.wait_ge(sem(f"big_free{b}"), k)

        def exact_before(key):
            i = EXACT.index(key)
            return EXACT[i - 1] if i else None

        def heads(t):
            return t[:, 0:S].rearrange("p (h c) -> p h c", h=GH)

        def pairs(t):
            return t.rearrange("p (c q) w -> p c q w", c=2)

        def f32(ap):
            return ap.bitcast(F32)

        with nc.Block() as block:
            @block.sync
            def _(sp):
                sp.dma_start(scr[:, 0:2 * P], ins["consts"][:, CRD:CEND]).then_inc(rots_loaded, 16)
                x_in = ins["x"].rearrange("a (t p) d -> p (a t) d", p=P)
                for t in range(NT):
                    sp.dma_start(xv[:, t, :], x_in[:, t, :]).then_inc(x_loaded[t], 16)
                sp.dma_start(consts[:, :], ins["consts"][:, 0:CRD]).then_inc(consts_loaded, 16)

            @block.vector
            def _(dve):
                nc.vector.memset(ones[:, :], 1.0).then_inc(ones_ready, 1)
                dve.wait_ge(ones_ready, 1)
                nc.vector.tensor_copy(ones_r[:, :], ones[:, :]).then_inc(exact_ready, 1)
                dve.wait_ge(rots_loaded, 16)
                nc.vector.tensor_copy(rot_r[:, :], scr[:, 0:2 * P]).then_inc(exact_ready, 1)

        def build_layer(l, block):
            @block.sync
            def _(sp):
                sp.dma_start(lw[:, :], ins["small"][bass.ds(l, 1), :, :].rearrange("a p n -> p (a n)")).then_inc(sem("small_loaded"), 16)
                for u, (job, i) in enumerate(UNITS):
                    if u >= STAGES:
                        sp.wait_ge(sem("w_ready"), u - STAGES + 1)
                    r0, rows = job.units[i]
                    w = ins[job.w]
                    src = w[bass.ds(l, 1), r0:r0 + rows, job.c0:job.c0 + job.n]
                    s = u % STAGES
                    if rows >= P:
                        sp.dma_start(stg[:, s, 0:rows // P, 0:job.n],
                                     src.rearrange("a (t p) n -> p (a t) n", p=P)).then_inc(sem(f"w_loaded{s}"), 16)
                    else:
                        sp.dma_start(stg[0:rows, s, 0, 0:job.n],
                                     src.rearrange("a p n -> p (a n)")).then_inc(sem(f"w_loaded{s}"), 16)

            @block.gpsimd
            def _(pool):
                for u, (job, i) in enumerate(UNITS):
                    r0, rows = job.units[i]
                    s, r = u % STAGES, u % RING
                    pp, kk = min(rows, P), max(rows // P, 1)
                    pool.wait_ge(sem(f"w_loaded{s}"), 16 * (u // STAGES + 1))
                    if u >= RING:
                        pool.wait_ge(sem("w_used"), u - RING + 1)
                    w = stg[0:pp, s, 0:kk, 0:job.n]
                    nc.gpsimd.tensor_scalar(rH[0:pp, r, 0:kk, 0:job.n], w, 1.0, 0.0, ALU.mult, ALU.add).then_inc(sem("w_hi"), 1)
                    pool.wait_ge(sem("w_hi"), u + 1)
                    nc.gpsimd.tensor_tensor(rL[0:pp, r, 0:kk, 0:job.n], w, f32(rH[0:pp, r, 0:kk, 0:job.n]),
                                            ALU.subtract).then_inc(sem("w_ready"), 1)

            @block.scalar
            def _(act):
                A = nc.scalar.activation

                def exp_ln_tables():
                    nc.scalar.preload_act_table_set("natural_log_exp_and_others")

                exp_ln_tables()

                def norm_stats(src, ready, tag, tiles=range(NT)):
                    for t in tiles:
                        ready(t)
                        A(hn[:, t, :], src[:, t, :], ACT.Square, scale=DM ** -0.5,
                          accum_out=n_ss[:, t:t + 1]).then_inc(sem(f"{tag}_ss"), 1)
                    act.wait_ge(sem(f"{tag}_v"), 1)
                    A(n_t, n_v, ACT.Ln).then_inc(sem(f"{tag}_ln"), 1)
                    act.wait_ge(sem(f"{tag}_ln"), 1)
                    A(n_y, n_t, ACT.Exp, scale=-0.5).then_inc(sem(f"{tag}_y"), 1)

                def normed(tag, ntag):
                    act.wait_ge(sem(f"{ntag}_nw"), 4)
                    for hf in range(2):
                        cs = slice(hf * 512, hf * 512 + 512)
                        for t in range(2):
                            A(hn[:, t, cs], xv[:, t, cs], ACT.Copy, scale=n_y[:, t:t + 1]).then_inc(sem(f"{tag}_ha"), 1)

                def split_hi(tag, nw, kk=KT):
                    for k in range(kk):
                        ps = mix_wait(act, (tag, k))
                        A(hH[:, k, :], ps[:, :], ACT.Copy, scale=lw[:, nw + k:nw + k + 1]).then_inc(sem(f"{tag}_hi"), 1)

                def gate_copy(b, hf):
                    if hf == 0 and b != "a":
                        prev = {"c": "a", "d": "c", "b": "d"}[b]
                        big_freed(act, (f"y{prev}1", 3))
                    for i in range(4):
                        ps = big_wait(act, (f"gate{b}{hf}", i))
                        big_free(A(gate_at(b, hf)[:, i, :], ps[:, :], ACT.Copy), (f"gate{b}{hf}", i))

                def gate_sigmoid(b):
                    for hf in range(2):
                        big_freed(act, (f"gate{b}{hf}", 3))
                        A(gate_at(b, hf), gate_at(b, hf), ACT.Sigmoid).then_inc(sem(f"sig{b}"), 1)

                norm_stats(xv, lambda t: act.wait_ge(x_loaded[t], 16), "n1", range(2))
                normed("pre1", "n1")
                act.wait_ge(sem("small_loaded"), 16)
                split_hi("pre1", LN1)
                def qkv_raw(part):
                    for i in range(4):
                        key = (("aq", "ak", "av")[part], i)
                        ps = big_wait(act, key)
                        big_free(A((aQ, aK, aV)[part][:, i, :], ps[:, :], ACT.Copy), key)

                def conv_silu(i):
                    act.wait_ge(sem("a_conv"), i + 1)
                    A((aQ, aK, aV)[i // 4][:, i % 4, :], g_cv[:, i % 2, :], ACT.Silu).then_inc(sem("a_silu"), 1)

                def qk_squares(i):
                    if i >= 2:
                        mix_wait(act, ("l2", i - 2))
                    act.wait_ge(sem("a_silu"), i + 1)
                    A(g_sq[:, i % 2, :], (aQ, aK)[i // 4][:, i % 4, :], ACT.Square).then_inc(sem("a_sq"), 1)

                def qk_root(i):
                    if i >= 2:
                        act.wait_ge(sem("a_l2"), i - 1)
                    ps = mix_wait(act, ("l2", i))
                    mix_free(A(g_rs[:, i % 2, :], ps[:, :], ACT.Ln, bias=EPS), ("l2", i))
                    mix_freed(act, ("l2", i))
                    A(g_rs[:, i % 2, :], g_rs[:, i % 2, :], ACT.Exp, scale=-0.5).then_inc(sem("a_rs"), 1)

                qkv_raw(0)
                for i in range(4):
                    conv_silu(i)
                    if i < 2:
                        qk_squares(i)
                qk_squares(2)
                qk_squares(3)
                qkv_raw(1)
                for i in range(4, 8):
                    conv_silu(i)
                    if i < 6:
                        qk_squares(i)
                    if i == 5:
                        ps = big_wait(act, ("aab", 0))
                        big_free(A(g_ab, ps[0:8, :], ACT.Copy), ("aab", 0))
                exp_ln_tables()
                for i in range(8):
                    if i in (4, 5):
                        qk_squares(i + 2)
                    qk_root(i)
                qkv_raw(2)
                act.wait_ge(sem("a_small"), 2)
                A(s_e, s_e, ACT.Exp, scale=-1.0).then_inc(sem("a_smallact"), 1)
                A(s_be, s_be, ACT.Exp, scale=-1.0).then_inc(sem("a_smallact"), 1)
                A(s_ea[:, 0, :], lw[:, LAL:LAL + GH], ACT.Exp).then_inc(sem("a_smallact"), 1)
                act.wait_ge(sem("a_smallact"), 1)
                A(s_l, s_e, ACT.Ln, bias=1.0).then_inc(sem("a_smallact"), 1)
                for i in range(8, 12):
                    conv_silu(i)
                exp_ln_tables()

                def key_decays(b):
                    ps = mix_wait(act, ("R", b))
                    if b:
                        act.wait_ge(sem("a_kbe"), b)
                    A(g_eR, heads(ps), ACT.Exp).then_inc(sem("a_eR"), 1)

                def pair_decays(b):
                    act.wait_ge(sem("a_min"), b + 1)
                    A(g_dec[b % 2], g_dec[b % 2], ACT.Exp).then_inc(sem("a_dec"), 1)
                    act.wait_ge(sem("a_edarg"), b + 1)
                    A(s_ed[:, b, :], s_ed[:, b, :], ACT.Exp).then_inc(sem("a_ed"), 1)

                for b in range(2):
                    key_decays(b)
                    pair_decays(b)
                gate_copy("a", 0)
                for b0 in (0, 2):
                    for e in range(2):
                        ps = mix_wait(act, ("T0", b0 + e))
                        mix_free(A(g_TU[e][:, :, 0, :], ps[:, :].rearrange("p (c w) -> p c w", c=2), ACT.Copy), ("T0", b0 + e))
                    for n in range(1, LEVELS):
                        for e in range(2):
                            for c in range(2):
                                ps = mix_wait(act, ("Y", b0 + e, n, c))
                                mix_free(A(g_Y[e][:, 2 * c:2 * c + 2, :], ps[:, 0:2 * P].rearrange("p (h w) -> p h w", h=2), ACT.Copy), ("Y", b0 + e, n, c))
                    for b in (b0, b0 + 1):
                        if b + 2 < NT:
                            key_decays(b + 2)
                        ps = mix_wait(act, ("new", b))
                        mix_free(A(g_Y[b % 2], heads(ps), ACT.Copy), ("new", b))
                        if b + 2 < NT:
                            pair_decays(b + 2)
                        ps = mix_wait(act, ("o", b))
                        mix_free(A(aQ[:, :, b * P:(b + 1) * P], heads(ps), ACT.Copy), ("o", b))
                for i in range(4):
                    ps = big_wait(act, ("az", i))
                    big_free(A(sg[:, 4 + i, :], ps[:, :], ACT.Copy), ("az", i))

                def exact_hi(key, src):
                    if exact_before(key):
                        mix_wait(act, exact_before(key))
                    A(oH[:, 4, :], src, ACT.Copy).then_inc(sem("x_hi"), 1)

                def head_squares(o, sq, tag):
                    A(sq, o, ACT.Square, scale=P ** -0.5).then_inc(sem(f"{tag}_sq"), 1)

                def head_root(h, key, rs, tag):
                    ps = mix_wait(act, key)
                    mix_free(A(rs, ps[:, :], ACT.Ln, bias=EPS), key)
                    mix_freed(act, key)
                    A(rs, rs, ACT.Exp, scale=-0.5).then_inc(sem(f"{tag}_rs"), 1)

                def o_split(tag, i, src, rows=P):
                    if tag == "b":
                        mix_freed(act, ("bf", i))
                    else:
                        act.wait_ge(sem(f"{tag}_out"), i + 1)
                    if i == 0 and tag != "a":
                        big_freed(act, ({"d": "yc1", "b": "yd1"}[tag], 3))
                    A(oH[0:rows, i, :], src, ACT.Copy).then_inc(sem(f"{tag}_ohi"), 1)

                mix_freed(act, ("o", NT - 1))
                head_squares(aQ[:, 0, :], g_sq[:, 0, :], "an")
                head_squares(aQ[:, 1, :], g_sq[:, 1, :], "an")
                for i in range(4):
                    big_freed(act, ("az", i))
                    A(sg[:, 4 + i, :], sg[:, 4 + i, :], ACT.Silu).then_inc(sem("a_z"), 1)
                exp_ln_tables()
                for h in range(4):
                    if h < 2:
                        mix_wait(act, ("an", h))
                        head_squares(aQ[:, h + 2, :], g_sq[:, h, :], "an")
                    else:
                        act.wait_ge(sem("a_nrm"), h - 1)
                    head_root(h, ("an", h), g_rs[:, h % 2, :], "an")
                    if h == 1:
                        o_split("a", 0, aQ[:, 0, :])
                        o_split("a", 1, aQ[:, 1, :])
                o_split("a", 2, aQ[:, 2, :])
                o_split("a", 3, aQ[:, 3, :])
                gate_copy("a", 1)
                gate_sigmoid("a")
                exp_ln_tables()
                act.wait_ge(sem("a_olo"), 4)
                big_freed(act, ("ya1", 3))
                for i in range(4):
                    ps = big_wait(act, ("cq", i))
                    big_free(A(cQ[:, i, :], ps[:, :], ACT.Copy, scale=DH ** -0.5), ("cq", i))
                for i in range(4):
                    ps = big_wait(act, ("ck", i))
                    big_free(A(cK[:, i, :], ps[:, :], ACT.Copy), ("ck", i))
                for i in range(4):
                    ps = big_wait(act, ("cv", i))
                    big_free(A(cV[:, i, :], ps[:, :], ACT.Copy), ("cv", i))

                def stick_A(h):
                    for j in range(NT):
                        n = S - j * P
                        ps = mix_wait(act, ("cs", h, j))
                        if h >= 2 and j == 0:
                            mix_wait(act, ("cpv", h // 2 - 1))
                        mix_free(A(c_A[h % 2][:, OFF[j]:OFF[j] + n], ps[:, 0:n], ACT.Exp), ("cs", h, j))

                for h in range(SBH + 1):
                    if h < SBH:
                        for j in reversed(range(NT)):
                            n = S - j * P
                            sl = c_sp[h % 2][:, OFF[j]:OFF[j] + n]
                            ps = mix_wait(act, ("z", h, j))
                            if h >= 2 and j == NT - 1:
                                mix_wait(act, ("cs", h - 2, NT - 1))
                            c = 3 * (NT * h + NT - 1 - j)
                            A(sl, ps[:, 0:n], ACT.Abs).then_inc(sem("c_act"), 1)
                            act.wait_ge(sem("c_act"), c + 1)
                            A(sl, sl, ACT.Exp, scale=-1.0).then_inc(sem("c_act"), 1)
                            act.wait_ge(sem("c_act"), c + 2)
                            A(sl, sl, ACT.Ln, bias=1.0).then_inc(sem("c_act"), 1)
                    if h >= 1:
                        stick_A(h - 1)
                    if h % 2 == 0 and h:
                        i = h // 2 - 1
                        ps = mix_wait(act, ("cpv", i))
                        if i == 0:
                            big_freed(act, ("ya1", 3))
                        A(oH[:, i, :], ps[:, :], ACT.Copy).then_inc(sem("c_ohi"), 1)
                    if h == 3:
                        gate_copy("c", 0)
                    if h == 7:
                        gate_copy("c", 1)
                gate_sigmoid("c")
                exp_ln_tables()
                mix_freed(act, ("cpv", 3))
                act.dma_start(dTab, ins["tables"][:, TD:TD + 3072]).then_inc(sem("tab"), 16)
                for i in range(4):
                    ps = big_wait(act, ("dqk", i))
                    big_free(A(dX[:, i, :], ps[:, :], ACT.Copy), ("dqk", i))
                for i in range(4):
                    big_freed(act, ("dqk", i))
                    exact_hi(("drot", i), dX[:, i, :])
                for i in range(4):
                    ps = big_wait(act, ("dv", i))
                    big_free(A(dV[:, i, :], ps[:, :], ACT.Copy), ("dv", i))
                act.wait_ge(sem("d_rope"), 4)
                for i in range(4):
                    ps = big_wait(act, ("dg", i))
                    big_free(A(dG[:, i, :], ps[:, :], ACT.Silu), ("dg", i))
                exp_ln_tables()
                for h in range(4):
                    ps = mix_wait(act, ("dpv", h))
                    if h:
                        act.wait_ge(sem("d_out"), h)
                        o_split("d", h - 1, dG[:, h - 1, :])
                    else:
                        act.wait_ge(sem("d_rope"), 4)
                    mix_free(A(dO, ps[:, :], ACT.Copy), ("dpv", h))
                    mix_freed(act, ("dpv", h))
                    head_squares(dO, dSq, "dn")
                    act.wait_ge(sem("dn_sq"), h + 1)
                    exact_hi(("dn", h), dSq)
                    head_root(h, ("dn", h), dSq, "dn")
                    if h == 1:
                        gate_copy("d", 0)
                    if h == 3:
                        gate_copy("d", 1)
                o_split("d", 3, dG[:, 3, :])
                gate_sigmoid("d")
                exp_ln_tables()
                act.wait_ge(sem("d_olo"), 4)
                act.dma_start(bTab, ins["tables"][:, TWC:TWC + 1024]).then_inc(sem("tab"), 16)

                def rope_raw(i):
                    key = WROPE[i][0]
                    ps = big_wait(act, key)
                    if i >= 4:
                        act.wait_ge(sem("b_rope"), i - 3)
                    big_free(A(bX[:, i % 4, :], ps[:, :], ACT.Copy), key)

                def rope_hi(i):
                    big_freed(act, WROPE[i][0])
                    exact_hi(("brot", i), bX[:, i % 4, :])

                for i in range(4):
                    rope_raw(i)
                for i in range(4):
                    rope_hi(i)
                for i in range(4, 8):
                    rope_raw(i)
                rope_hi(4)
                rope_hi(5)
                rope_raw(8)
                rope_raw(9)
                for i in range(6, 10):
                    rope_hi(i)
                for g0, g1 in ((1, 3), (0, 1)):
                    for t in range(4):
                        key = (f"bv{g0}", t)
                        ps = big_wait(act, key)
                        v = ps[:, 0:192 * (g1 - g0)].rearrange("p (g c) -> p g c", c=192)
                        big_free(A(bV[:, g0:g1, t, :], v, ACT.Copy), key)
                nexp = 0
                for i in range(len(WU) + 2):
                    if i < len(WU):
                        g, h, b0, nb, w = WU[i]
                        act.wait_ge(sem("b_nm"), i + 1)
                        pv = bP[:, i % 2, :].rearrange("p (b w) -> p b w", w=w)
                        for b in range(nb):
                            A(pv[:, b, :], pv[:, b, :], ACT.Exp, bias=w_nm[:, g, b0 + b, h:h + 1],
                              accum_out=w_z[:, g, b0 + b, h:h + 1]).then_inc(sem("b_exp"), 1)
                            nexp += 1
                    if 1 <= i <= len(WU):
                        ps = mix_wait(act, ("pt", i - 1))
                        if i >= 3:
                            mix_wait(act, ("wpv", i - 3))
                        mix_free(A(bPT[:, (i - 1) % 2, :], ps[:, :], ACT.Copy), ("pt", i - 1))
                    if i >= 2:
                        g, h, b0, nb, w = WU[i - 2]
                        hh = 3 * g + h
                        p0, tl = hh % 2 * DH, hh // 2
                        ps = mix_wait(act, ("wpv", i - 2))
                        if g == 0:
                            o_, i_ = bQ[p0:p0 + DH, tl, b0 * P:(b0 + nb) * P], ps[p0:p0 + DH, 0:nb * P]
                        else:
                            o_ = bQ[p0:p0 + DH, tl, :].rearrange("p (l r) -> p r l", r=DIL[g])
                            i_ = ps[p0:p0 + DH, :].rearrange("p (r l) -> p r l", r=DIL[g])
                        mix_free(A(o_, i_, ACT.Copy), ("wpv", i - 2))
                    if i == 4:
                        gate_copy("b", 0)
                for n in range(2):
                    for g in range(3):
                        ps = mix_wait(act, ("st", n, g))
                        o_ = (bFM, bFZ)[n][:, g, :]
                        i_ = ps[0:3, :]
                        if g:
                            o_ = o_.rearrange("p (l r) -> p r l", r=DIL[g])
                            i_ = i_.rearrange("p (r l) -> p r l", r=DIL[g])
                        mix_free(A(o_, i_, ACT.Copy), ("st", n, g))
                act.wait_ge(sem("b_fac"), 3)
                A(bFM, bFM, ACT.Exp).then_inc(sem("b_fexp"), 1)
                gate_copy("b", 1)
                for i in range(5):
                    r = P if i < 4 else DH
                    o_split("b", i, bQ[0:r, i, :], r)
                gate_sigmoid("b")
                exp_ln_tables()
                for k in range(KT):
                    act.wait_ge(sem("mixed"), k + 1)
                    A(hH[:, k, :], mixed[:, k, :], ACT.Copy).then_inc(sem("m_hi"), 1)

                def y_squares(jobs, hf, tag):
                    for t in range(NT):
                        ps = big_wait(act, (f"{jobs}{hf}", t))
                        n = NT * hf + t
                        if n:
                            act.wait_ge(sem(f"{tag}_ss"), n)
                        A(oH[:, 0, :], ps[:, :], ACT.Square, scale=DM ** -0.5, accum_out=n_ss[:, n:n + 1]).then_inc(sem(f"{tag}_ss"), 1)

                def post_weights(norm):
                    act.dma_start(postw, ins[norm][bass.ds(l, 1), :].to_broadcast((P, DM))).then_inc(sem("postw"), 16)

                def root(tag):
                    act.wait_ge(sem(f"{tag}_v"), 1)
                    A(n_t, n_v, ACT.Ln).then_inc(sem(f"{tag}_ln"), 1)
                    act.wait_ge(sem(f"{tag}_ln"), 1)
                    A(n_y, n_t, ACT.Exp, scale=-0.5).then_inc(sem(f"{tag}_y"), 1)


                act.wait_ge(sem("b_olo"), 5)
                post_weights("norm_post_mix")
                for hf in range(2):
                    y_squares("o", hf, "n2")
                root("n2")
                norm_stats(xv, lambda t: act.wait_ge(sem("n2_x"), 2 * t + 2), "n3")
                normed("pre2", "n3")
                post_weights("norm_post_mlp")
                split_hi("pre2", LN2)
                def f_hi(n):
                    u = n % 16
                    act.wait_ge(sem("w_used"), DN0 + n - 3)
                    q = n % 4 * 2
                    A(hH[:, q:q + 2, :], fT[:, 2 * u:2 * u + 2, :], ACT.Copy).then_inc(sem("f_hi"), 1)

                for g in range(8):
                    if g == 7:
                        big_freed(act, ("up1", 1))
                        for n in range(3):
                            f_hi(n)
                    for i in range(4):
                        ps = big_wait(act, (f"up{g}", i))
                        if g == 0 and i == 0:
                            mix_freed(act, ("pre2", KT - 1))
                        A(fT[:, 4 * g + i, :], ps[:, :], ACT.Relu).then_inc(sem("f_relu"), 1)
                for i in range(4):
                    big_freed(act, ("up7", i))
                for n in range(3, 32):
                    if n == 19:
                        y_squares("dn", 0, "n4")
                    f_hi(n)
                y_squares("dn", 1, "n4")
                root("n4")

            @block.vector
            def _(dve):
                V = nc.vector
                TT, TS, STT = V.tensor_tensor, V.tensor_scalar, V.scalar_tensor_tensor

                def rstd(tag):
                    c = sem(f"{tag}_nw")
                    if tag in ("n2", "n4"):
                        dve.wait_ge(sem(f"{tag}_ss"), 2 * NT)
                        STT(n_v, n_ss[:, 0:NT], EPS, n_ss[:, NT:2 * NT], ALU.add, ALU.add).then_inc(sem(f"{tag}_v"), 1)
                    else:
                        dve.wait_ge(sem(f"{tag}_ss"), NT if tag == "n3" else 2)
                        if tag == "n1":
                            dve.wait_ge(sem("n1_ss2"), 2)
                        V.tensor_scalar_add(n_v, n_ss[:, 0:NT], EPS).then_inc(sem(f"{tag}_v"), 1)
                    dve.wait_ge(sem(f"{tag}_v"), 1)
                    TS(n_h, n_v, -0.5, None, ALU.mult).then_inc(c, 1)
                    dve.wait_ge(sem(f"{tag}_y"), 1)
                    TT(n_t, n_y, n_y, ALU.mult).then_inc(c, 1)
                    dve.wait_ge(c, 2)
                    TT(n_t, n_t, n_h, ALU.mult).then_inc(c, 1)
                    dve.wait_ge(c, 3)
                    STT(n_y, n_t, 1.5, n_y, ALU.add, ALU.mult).then_inc(c, 1)
                    dve.wait_ge(c, 4)

                def pre(tag, ntag, nw):
                    if ntag == "n1":
                        for t in range(2, NT):
                            dve.wait_ge(x_loaded[t], 16)
                            STT(hn[:, t, :], xv[:, t, :], 1.0 / DM, xv[:, t, :], ALU.mult, ALU.mult,
                                accum_out=n_ss[:, t:t + 1]).then_inc(sem("n1_ss2"), 1)
                    rstd(ntag)
                    for hf in range(2):
                        cs = slice(hf * 512, hf * 512 + 512)
                        for t in range(2, NT):
                            TS(hn[:, t, cs], xv[:, t, cs], n_y[:, t:t + 1], None, ALU.mult).then_inc(sem(f"{tag}_h"), 1)
                    for k in range(KT):
                        ps = mix_wait(dve, (tag, k))
                        dve.wait_ge(sem(f"{tag}_hi"), k + 1)
                        mix_free(STT(hL[:, k, :], ps[:, :], lw[:, nw + k:nw + k + 1], f32(hH[:, k, :]), ALU.mult, ALU.subtract), (tag, k))

                def o_lo_split(tag, i, src, rows=P):
                    dve.wait_ge(sem(f"{tag}_ohi"), i + 1)
                    TT(oL[0:rows, i, :], src, f32(oH[0:rows, i, :]), ALU.subtract).then_inc(sem(f"{tag}_olo"), 1)

                def mixed_lo(k):
                    dve.wait_ge(sem("m_hi"), k + 1)
                    TT(hL[:, k, :], mixed[:, k, :], f32(hH[:, k, :]), ALU.subtract).then_inc(sem("m_lo"), 1)

                def gated(b):
                    for hf in range(2):
                        for i in range(4):
                            k = 4 * hf + i
                            ps = big_wait(dve, (f"y{b}{hf}", i))
                            dve.wait_ge(sem(f"sig{b}"), hf + 1)
                            if b == "a":
                                big_free(TT(mixed[:, k, :], ps[:, :], gate_at(b, hf)[:, i, :], ALU.mult), (f"y{b}{hf}", i))
                            else:
                                big_free(TT(sg[:, k, :], ps[:, :], sg[:, k, :], ALU.mult), (f"y{b}{hf}", i))
                                big_freed(dve, (f"y{b}{hf}", i))
                                TT(mixed[:, k, :], mixed[:, k, :], sg[:, k, :], ALU.add).then_inc(sem(f"mixed_{b}") if b != "b" else sem("mixed"), 1)
                            if b == "b":
                                for q in {4: range(4), 5: (4,), 6: (5,), 7: (6,)}.get(k, ()):
                                    mixed_lo(q)

                def per_head(ap4):
                    return ap4.unsqueeze(2).to_broadcast((P, GH, P))

                def level_mask(b, n):
                    e = b % 2
                    if n > 1:
                        for c in range(2):
                            mix_wait(dve, ("Y", b, n - 1, c))
                    elif n == 1:
                        dve.wait_ge(sem(f"a_U{e}"), b // 2 + 1)
                    TT(g_LTm[e], g_LT[e], per_mask(consts[:, CLV + n * P:CLV + (n + 1) * P]), ALU.mult).then_inc(sem(f"a_LTm{e}"), 1)

                def per_mask(ap):
                    return ap.unsqueeze(1).to_broadcast((P, GH, P))

                pre("pre1", "n1", LN1)
                V.memset(g_S, 0.0).then_inc(sem("a_S0"), 1)
                dve.wait_ge(consts_loaded, 16)
                V.tensor_copy(idb[:, :], ident).then_inc(sem("c_bias"), 1)
                V.tensor_scalar(strictb[:, :], strict, -NEG, NEG, ALU.mult, ALU.add).then_inc(sem("c_bias"), 1)
                dve.wait_ge(sem("small_loaded"), 16)
                mix_wait(dve, ("pre1", KT - 1))

                def conv(i):
                    key = (("aq", "ak", "av")[i // 4], i % 4)
                    big_freed(dve, key)
                    if i >= 2:
                        dve.wait_ge(sem("a_silu"), i - 1)
                    cv, raw = g_cv[:, i % 2, :], (aQ, aK, aV)[i // 4][:, i % 4, :]
                    tap = lambda q: lw[:, LCW + 12 * q + i:LCW + 12 * q + i + 1]
                    TS(cv, raw, tap(3), None, ALU.mult).then_inc(sem("a_tap"), 1)
                    for q in (1, 2):
                        dve.wait_ge(sem("a_tap"), 3 * i + q)
                        STT(cv[:, q:], raw[:, 0:S - q], tap(3 - q), cv[:, q:], ALU.mult, ALU.add).then_inc(sem("a_tap"), 1)
                    dve.wait_ge(sem("a_tap"), 3 * i + 3)
                    STT(cv[:, 3:], raw[:, 0:S - 3], tap(0), cv[:, 3:], ALU.mult, ALU.add).then_inc(sem("a_conv"), 1)

                for i in range(8):
                    conv(i)
                for i in range(8):
                    dve.wait_ge(sem("a_rs"), i + 1)
                    t = (aQ, aK)[i // 4][:, i % 4, :]
                    STT(t, t, DK ** -0.5 if i < 4 else 1.0, g_rs[:, i % 2, :], ALU.mult, ALU.mult).then_inc(sem("a_l2"), 1)
                ps = mix_wait(dve, "ab")
                abv = ps[:, 0:32].rearrange("p (b c) -> p b c", b=4)
                c = sem("a_sc")
                TT(s_a, abv[:, :, 0:4], lw[:, LDT:LDT + GH].unsqueeze(1).to_broadcast((P, 4, GH)), ALU.add).then_inc(c, 1)
                mix_free(V.tensor_scalar_max(s_be, abv[:, :, 4:8], -80.0), "ab")
                dve.wait_ge(c, 1)
                mix_freed(dve, "ab")
                STT(s_e, s_a, -1.0, s_a, ALU.mult, ALU.max).then_inc(sem("a_small"), 1)
                TS(s_a, s_a, 0.0, None, ALU.max).then_inc(sem("a_small"), 1)
                dve.wait_ge(sem("a_smallact"), 4)
                TT(s_g, s_a, s_l, ALU.add).then_inc(c, 1)
                V.tensor_scalar_add(s_be, s_be, 1.0).then_inc(c, 1)
                dve.wait_ge(c, 2)
                STT(s_g, s_g, -1.0, s_ea[:, 0, :].unsqueeze(1).to_broadcast((P, 4, GH)), ALU.mult, ALU.mult).then_inc(sem("a_g"), 1)
                dve.wait_ge(c, 3)
                V.reciprocal(s_be, s_be).then_inc(sem("a_g"), 1)
                for i in range(8, 12):
                    conv(i)
                ps = mix_wait(dve, "gc")
                mix_free(V.tensor_copy(s_gc, ps[:, 0:16].rearrange("p (b h) -> p b h", b=4)), "gc")
                mix_freed(dve, "gc")

                def exponents(b):
                    ps = mix_wait(dve, ("R", b))
                    R = heads(ps)
                    dve.wait_ge(sem("a_eR"), b + 1)
                    TT(s_ed[:, b, :], R[:, :, P - 1], s_gc[:, b, :], ALU.subtract).then_inc(sem("a_edarg"), 1)
                    mix_free(TT(g_dec[b % 2], pairs(R), pairs(per_head(s_gc[:, b, :])), ALU.subtract), ("R", b))
                    mix_freed(dve, ("R", b))
                    V.tensor_scalar_min(g_dec[b % 2], g_dec[b % 2], 0.0).then_inc(sem("a_min"), 1)
                    ps = mix_wait(dve, ("B", b))
                    mix_free(TT(g_kb[b % 2], aK[:, :, b * P:(b + 1) * P], heads(ps), ALU.mult), ("B", b))

                def lower(b):
                    dve.wait_ge(sem("a_dec"), b + 1)
                    TT(g_dec[b % 2], g_dec[b % 2], pairs(per_mask(triu)), ALU.mult).then_inc(sem("a_decm"), 1)
                    dve.wait_ge(sem("a_decm"), b + 1)
                    ps = mix_wait(dve, ("LT", b))
                    mix_free(TT(pairs(g_LT[b % 2]), pairs(heads(ps)), g_dec[b % 2], ALU.mult), ("LT", b))

                def scores_and_first_level(b):
                    e = b % 2
                    ps = mix_wait(dve, ("att", b))
                    mix_free(TT(pairs(g_att[e]), pairs(heads(ps)), g_dec[e], ALU.mult), ("att", b))
                    mix_freed(dve, ("LT", b))
                    level_mask(b, 0)
                    dve.wait_ge(sem(f"a_LTm{e}"), 1 + LEVELS * (b // 2))
                    mix_freed(dve, ("att", b))
                    TT(g_Uall[e], pairs(per_mask(ident)), pairs(g_LTm[e]), ALU.subtract).then_inc(sem(f"a_U{e}"), 1)
                    level_mask(b, 1)
                    V.tensor_copy(s_gl[:, b, :], g_eR[:, :, P - 1])
                    bs = slice(b * P, (b + 1) * P)
                    TT(aQ[:, :, bs], aQ[:, :, bs], g_eR, ALU.mult).then_inc(sem("a_qd"), 1)
                    TT(g_kb[e], g_kb[e], g_eR, ALU.mult).then_inc(sem("a_kbe"), 1)

                def natural_k_v(b):
                    ps = mix_wait(dve, ("kn", b))
                    dve.wait_ge(sem("a_ed"), b + 1)
                    mix_free(TT(g_kd, heads(ps), per_head(s_ed[:, b, :]), ALU.mult), ("kn", b))
                    ps = mix_wait(dve, ("vn", b))
                    mix_free(TT(g_vb, heads(ps), per_head(s_be[:, b, :]), ALU.mult), ("vn", b))

                for b in range(2):
                    exponents(b)
                    lower(b)
                    scores_and_first_level(b)
                for b0 in (0, 2):
                    natural_k_v(b0)
                    for n in range(1, LEVELS):
                        if n < LEVELS - 1:
                            for e in range(2):
                                level_mask(b0 + e, n + 1)
                        for e in range(2):
                            for c in range(2):
                                key = ("X", b0 + e, n, c)
                                ps = mix_wait(dve, key)
                                if n < LEVELS - 1:
                                    t = level_half(g_TU[e][:, c, 0, :], n, 0)
                                    TT(t, t, ps[:, 0:P].rearrange("p (m z) -> p m z", z=1 << n), ALU.subtract)
                                t = level_half(g_TU[e][:, c, 1, :], n, 1)
                                mix_free(TT(t, t, ps[:, P:2 * P].rearrange("p (m z) -> p m z", z=1 << n), ALU.subtract), key)
                    for b in (b0, b0 + 1):
                        if b > b0:
                            natural_k_v(b)
                            if b0 == 0:
                                scores_and_first_level(2)
                        mix_freed(dve, ("vn", b))
                        ps = mix_wait(dve, ("ks", b))
                        mix_free(TT(g_vb, g_vb, heads(ps), ALU.subtract), ("ks", b))
                        if b + 2 < NT:
                            exponents(b + 2)
                            lower(b + 2)
                        ps = mix_wait(dve, ("dS", b))
                        dve.wait_ge(sem("a_kbe"), b + 1)
                        if b:
                            mix_freed(dve, ("dS", b - 1))
                        for h in range(GH):
                            i = STT(g_S[:, h, :], g_S[:, h, :], s_gl[:, b, h:h + 1], ps[:, h * P:(h + 1) * P], ALU.mult, ALU.add)
                        mix_free(i, ("dS", b))
                    if b0 == 0:
                        scores_and_first_level(3)

                def head_normed(h, o, rs, tag):
                    dve.wait_ge(sem(f"{tag}n_rs"), h + 1)
                    TT(o, o, rs, ALU.mult).then_inc(sem(f"{tag}_nrm"), 1)

                def head_out(h, o, w, gate, dst, tag):
                    dve.wait_ge(sem(f"{tag}_nrm"), h + 1)
                    STT(dst, o, lw[:, w:w + 1], gate, ALU.mult, ALU.mult).then_inc(sem(f"{tag}_out"), 1)

                for h0 in (0, 2):
                    for h in (h0, h0 + 1):
                        head_normed(h, aQ[:, h, :], g_rs[:, h % 2, :], "a")
                    for h in (h0, h0 + 1):
                        dve.wait_ge(sem("a_z"), h + 1)
                        head_out(h, aQ[:, h, :], LGN, sg[:, 4 + h, :], aQ[:, h, :], "a")
                    for h in (h0, h0 + 1):
                        o_lo_split("a", h, aQ[:, h, :])
                gated("a")
                for h in range(SBH + 1):
                    if h < SBH:
                        for j in reversed(range(NT)):
                            n = S - j * P
                            c = NT * h + NT - 1 - j
                            ps = mix_wait(dve, ("z", h, j))
                            sl = c_sp[h % 2][:, OFF[j]:OFF[j] + n]
                            dve.wait_ge(sem("c_act"), 3 * c + 3)
                            mix_free(STT(sl, ps[:, 0:n], 0.0, sl, ALU.max, ALU.add), ("z", h, j))
                            mix_freed(dve, ("z", h, j))
                            i = TT(sl[:, 0:P], sl[:, 0:P], strict, ALU.mult)
                            if j < NT - 1:
                                dve.wait_ge(sem("c_sp"), c)
                                i = TT(sl[:, P:], sl[:, P:], c_sp[h % 2][:, OFF[j + 1]:OFF[j + 1] + n - P], ALU.add)
                            i.then_inc(sem("c_sp"), 1)
                    if h % 2 == 0 and h:
                        i = h // 2 - 1
                        ps = mix_wait(dve, ("cpv", i))
                        dve.wait_ge(sem("c_ohi"), i + 1)
                        mix_free(TT(oL[:, i, :], ps[:, :], f32(oH[:, i, :]), ALU.subtract), ("cpv", i))
                gated("c")

                def exact_lo(key, src):
                    n = EXACT.index(key)
                    dve.wait_ge(sem("x_hi"), n + 1)
                    TT(oL[:, 4, :], src, f32(oH[:, 4, :]), ALU.subtract).then_inc(sem("x_lo"), 1)

                def rope(i, key, x, cos, sin, t1, t2, dsts, tag):
                    exact_lo(key, x)
                    ps = mix_wait(dve, key)
                    n = sem(f"{tag}_rp")
                    if i:
                        dve.wait_ge(sem(f"{tag}_rope"), i)
                    TT(t1, x, cos, ALU.mult).then_inc(n, 1)
                    mix_free(TT(t2, ps[:, :], sin, ALU.mult), key)
                    dve.wait_ge(n, i + 1)
                    mix_freed(dve, key)
                    for q, (r0, r1, dst, dil) in enumerate(dsts):
                        a, b_ = t1[r0:r1, :], t2[r0:r1, :]
                        if dil > 1:
                            dst = dst.rearrange("p (r l) -> p r l", r=dil)
                            a = a.rearrange("p (l r) -> p r l", r=dil)
                            b_ = b_.rearrange("p (l r) -> p r l", r=dil)
                        ins_ = TT(dst, a, b_, ALU.add)
                        if q == len(dsts) - 1:
                            ins_.then_inc(sem(f"{tag}_rope"), 1)

                dve.wait_ge(sem("tab"), 16)
                mix_freed(dve, ("cpv", 3))
                for i in range(4):
                    rope(i, ("drot", i), dX[:, i, :], dTab[:, TRC:TRC + S], dTab[:, TRS:TRS + S],
                         dY[:, 0, :], dY[:, 1, :], [(0, P, dQK[:, i, :], 1)], "d")
                for h in range(4):
                    for j in range(NT):
                        n = S - j * P
                        ps = mix_wait(dve, ("dz", h, j))
                        if h:
                            mix_wait(dve, ("dpv", h - 1))
                        else:
                            dve.wait_ge(sem("d_rope"), 4)
                        mix_free(TT(dP[:, j, 0:n], ps[:, 0:n], dTab[:, TD + S * h:TD + S * h + n], ALU.mult), ("dz", h, j))
                    exact_lo(("dn", h), dSq)
                    if h == 0:
                        for i in range(4):
                            big_freed(dve, ("dg", i))
                    if h:
                        o_lo_split("d", h - 1, dG[:, h - 1, :])
                    head_normed(h, dO, dSq, "d")
                    head_out(h, dO, LRN, dG[:, h, :], dG[:, h, :], "d")
                o_lo_split("d", 3, dG[:, 3, :])
                gated("d")
                dve.wait_ge(sem("tab"), 32)
                for i, (_, q, tl) in enumerate(WROPE):
                    dst = (bQ, bK)[q]
                    half = [(0, DH, dst[0:DH, tl, :], DIL[2 * tl // 3]), (DH, P, dst[DH:P, tl, :], DIL[min((2 * tl + 1) // 3, 2)])]
                    rope(i, ("brot", i), bX[:, i % 4, :], bTab[:, 0:S], bTab[:, S:2 * S],
                         bP[:, 0, :], bP[:, 1, :], half if tl < 4 else half[:1], "b")
                for i, (g, h, b0, nb, w) in enumerate(WU):
                    ps = mix_wait(dve, ("sc", i))
                    if i == 0:
                        dve.wait_ge(sem("b_rope"), 10)
                    if i >= 2:
                        mix_wait(dve, ("pt", i - 2))
                    if g == 0:
                        mask = consts[:, CMG0 + b0 * 128:CMG0 + b0 * 128 + 512].rearrange("p (b w) -> p b w", w=w)
                    else:
                        m0 = (CMG1, CMG2)[g - 1]
                        mask = consts[:, m0:m0 + P].unsqueeze(1).to_broadcast((P, 4, P))
                    pv = bP[:, i % 2, :].rearrange("p (b w) -> p b w", w=w)
                    mix_free(STT(pv, ps[:, :].rearrange("p (b w) -> p b w", w=w), DH ** -0.5, mask, ALU.mult, ALU.add), ("sc", i))
                    mix_freed(dve, ("sc", i))
                    V.reduce_max(w_m[:, g, b0:b0 + nb, h], pv, AX_X).then_inc(sem("b_max"), 1)
                    dve.wait_ge(sem("b_max"), i + 1)
                    TS(w_nm[:, g, b0:b0 + nb, h], w_m[:, g, b0:b0 + nb, h], -1.0, None, ALU.mult).then_inc(sem("b_nm"), 1)
                for n in range(2):
                    for g in range(3):
                        mix_freed(dve, ("st", n, g))
                fc = sem("b_fc")
                TT(bFS, bFM[:, 0, :], bFM[:, 1, :], ALU.max).then_inc(fc, 1)
                dve.wait_ge(fc, 1)
                TT(bFS, bFS, bFM[:, 2, :], ALU.max).then_inc(fc, 1)
                dve.wait_ge(fc, 2)
                for g in range(3):
                    TT(bFM[:, g, :], bFM[:, g, :], bFS, ALU.subtract).then_inc(sem("b_fac"), 1)
                dve.wait_ge(sem("b_fexp"), 1)
                TT(bFZ, bFZ, bFM, ALU.mult).then_inc(fc, 1)
                dve.wait_ge(fc, 3)
                TT(bFS, bFZ[:, 0, :], bFZ[:, 1, :], ALU.add).then_inc(fc, 1)
                dve.wait_ge(fc, 4)
                TT(bFS, bFS, bFZ[:, 2, :], ALU.add).then_inc(fc, 1)
                dve.wait_ge(fc, 5)
                V.reciprocal(bFS, bFS).then_inc(fc, 1)
                dve.wait_ge(fc, 6)
                for g in range(3):
                    TT(bFM[:, g, :], bFM[:, g, :], bFS, ALU.mult).then_inc(sem("b_share"), 1)
                for i in range(5):
                    r = P if i < 4 else DH
                    ps = mix_wait(dve, ("bf", i))
                    mix_free(TT(bQ[0:r, i, :], bQ[0:r, i, :], ps[0:r, :], ALU.mult), ("bf", i))
                    if i:
                        o_lo_split("b", i - 1, bQ[:, i - 1, :])
                o_lo_split("b", 4, bQ[0:DH, 4, :], DH)
                gated("b")
                mixed_lo(KT - 1)

                def y_weighted(jobs, hf, tag):
                    for t in range(NT):
                        ps = big_wait(dve, (f"{jobs}{hf}", t))
                        dve.wait_ge(sem(f"{tag}_ss"), NT * hf + t + 1)
                        big_free(TT(yhalf[hf][:, t, :], ps[:, :], postw[:, hf * 512:hf * 512 + 512], ALU.mult), (f"{jobs}{hf}", t))

                def residual(jobs, tag):
                    rstd(tag)
                    for t in range(NT):
                        for hf in range(2):
                            cs = slice(hf * 512, hf * 512 + 512)
                            big_freed(dve, (f"{jobs}{hf}", t))
                            STT(xv[:, t, cs], yhalf[hf][:, t, :], n_y[:, t:t + 1], xv[:, t, cs], ALU.mult, ALU.add).then_inc(sem(f"{tag}_x"), 1)

                dve.wait_ge(sem("postw"), 16)
                for hf in range(2):
                    y_weighted("o", hf, "n2")
                residual("o", "n2")
                pre("pre2", "n3", LN2)
                def f_lo(n):
                    u, q = n % 16, n % 4 * 2
                    dve.wait_ge(sem("f_hi"), n + 1)
                    TT(hL[:, q:q + 2, :], fT[:, 2 * u:2 * u + 2, :], f32(hH[:, q:q + 2, :]), ALU.subtract).then_inc(sem("f_lo"), 1)

                for g in range(8):
                    if g == 7:
                        for n in range(3):
                            f_lo(n)
                    for i in range(4):
                        k = 4 * g + i
                        ps = big_wait(dve, (f"up{g}", i))
                        dve.wait_ge(sem("f_relu"), k + 1)
                        big_free(STT(fT[:, k, :], ps[:, :], 0.0, fT[:, k, :], ALU.max, ALU.mult), (f"up{g}", i))
                for n in range(3, 32):
                    if n == 19:
                        dve.wait_ge(sem("postw"), 32)
                        y_weighted("dn", 0, "n4")
                    f_lo(n)
                y_weighted("dn", 1, "n4")
                residual("dn", "n4")
                dve.wait_ge(sem("n4_x"), 2 * NT)

            @block.tensor
            def _(pe):
                MM, TR = nc.tensor.matmul, nc.tensor.transpose
                state = {"u": 0}

                def unit(job, i):
                    u = state["u"]
                    assert UNITS[u][0] is job and UNITS[u][1] == i
                    slot = u % RING
                    r0, rows = job.units[i]
                    kts = [(r0 // P + k, min(P, rows - k * P)) for k in range(max(1, -(-rows // P)))]
                    pe.wait_ge(sem("w_ready"), u + 1)
                    sH, sL = (oH, oL) if job.src == "o" else (hH, hL)
                    last_unit = i == len(job.units) - 1
                    first = True
                    for t in range(job.tiles):
                        b, use = BIG[(job.name, t)]
                        if i == 0 and use > 1:
                            pe.wait_ge(sem(f"big_free{b}"), use - 1)
                        for k, (kt, rr) in enumerate(kts):
                            ks = (2 * (i % 4) + k) if job.src == "f" else kt
                            for m, (wt, xt) in enumerate(((rH, sH), (rL, sH), (rH, sL))):
                                if job.kind == "T":
                                    o_ = big[b][:, 0:S]
                                    a_, r_ = wt[0:rr, slot, k, t * P:(t + 1) * P], xt[0:rr, ks, :]
                                else:
                                    o_ = big[b][:, 0:job.n]
                                    d = DIL[job.perm]
                                    if job.perm == 0:
                                        a_ = xt[0:rr, ks, t * P:(t + 1) * P]
                                    else:
                                        a_ = xt[0:rr, ks, :].rearrange("p (l r) -> p r l", r=d)
                                        a_ = a_[:, t, :]
                                    r_ = wt[0:rr, slot, k, 0:job.n]
                                s0 = i == 0 and k == 0 and m == 0
                                s1 = last_unit and k == len(kts) - 1 and m == 2
                                ins_ = MM(o_, a_, r_, start=s0, stop=s1)
                                if s1:
                                    ins_.then_inc(sem(f"big_done{b}"), 1)
                                elif first and u > 0:
                                    ins_.then_inc(sem("w_used"), 1)
                                first = False
                    state["u"] += 1

                def do(name, need=None, between=None):
                    job = JOB[name]
                    for i in range(len(job.units)):
                        if need:
                            need(i)
                        unit(job, i)
                        if between:
                            between(i)

                fills = []

                def fill(n=1):
                    for _ in range(n):
                        if fills:
                            unit(*fills.pop(0))

                def set_fill(*names):
                    assert not fills
                    fills.extend((JOB[name], i) for name in names for i in range(4))

                order = iter(MIX)

                def tile_of(key):
                    assert next(order) == key, key
                    b, k = MIX[key]
                    if k > 1:
                        pe.wait_ge(sem(f"mix_free{b}"), k - 1)
                    return mxb[b]

                def done(ins_, key):
                    ins_.then_inc(sem(f"mix_done{MIX[key][0]}"), 1)

                def pre(tag):
                    for k in range(KT):
                        ps = tile_of((tag, k))
                        for part in ("h", "ha"):
                            pe.wait_ge(sem(f"{tag}_{part}"), 2 if k < KT // 2 else 4)
                        for t in range(NT):
                            i = TR(ps[:, t * P:(t + 1) * P], hn[:, t, k * P:(k + 1) * P], ident)
                        done(i, (tag, k))

                def pre_split(tag):
                    return lambda i: [mix_freed(pe, (tag, k)) for k in (2 * i, 2 * i + 1)]

                pe.wait_ge(consts_loaded, 16)
                pe.wait_ge(ones_ready, 1)
                pe.wait_ge(exact_ready, 2)
                pre("pre1")
                def l2_sums(*tiles):
                    for i in tiles:
                        ps = tile_of(("l2", i))
                        pe.wait_ge(sem("a_sq"), i + 1)
                        done(MM(ps[:, :], ones[:, :], g_sq[:, i % 2, :], start=True, stop=True), ("l2", i))

                def gates_by_token():
                    ps = tile_of("ab")
                    big_freed(pe, ("aab", 0))
                    for t in range(NT):
                        i = TR(ps[:, 8 * t:8 * t + 8], g_ab[:, t * P:(t + 1) * P], ident[0:8, 0:8])
                    done(i, "ab")

                do("aq", pre_split("pre1"))
                do("ak", between=lambda i: l2_sums(*((), (), (0, 1), (2, 3))[i]))
                do("aab")
                do("av", between=lambda i: l2_sums(*((), (4, 5), (6, 7), ())[i]))
                gates_by_token()
                set_fill("gatea0", "az")
                fill(1)
                pe.wait_ge(sem("a_g"), 2)
                ps = tile_of("gc")
                done(MM(ps[:, 0:16], triu, s_g.rearrange("p b h -> p (b h)"), start=True, stop=True), "gc")
                fill(1)
                pe.wait_ge(sem("a_l2"), 8)

                def per_head_tile(key, op):
                    ps = tile_of(key)
                    for h in range(GH):
                        i = op(ps[:, h * P:(h + 1) * P], h)
                    done(i, key)

                def tokens(t, h, b):
                    return t[:, h, b * P:(b + 1) * P]

                def MM1(o_, a_, b_):
                    return MM(o_, a_, b_, start=True, stop=True)

                def decays(b):
                    per_head_tile(("R", b), lambda o_, h: MM1(o_, s_g[:, b, h:h + 1].to_broadcast((P, P)), triu))
                    per_head_tile(("B", b), lambda o_, h: MM1(o_, s_be[:, b, h:h + 1].to_broadcast((P, P)), ident))

                def lower(b):
                    mix_freed(pe, ("B", b))
                    per_head_tile(("LT", b), lambda o_, h: MM1(o_, tokens(aK, h, b), g_kb[b % 2][:, h, :]))

                def scores_gdn(b):
                    per_head_tile(("att", b), lambda o_, h: MM1(o_, tokens(aK, h, b), tokens(aQ, h, b)))

                def natural_k_v(b):
                    per_head_tile(("kn", b), lambda o_, h: TR(o_, tokens(aK, h, b), ident))
                    per_head_tile(("vn", b), lambda o_, h: TR(o_, tokens(aV, h, b), ident))

                for b in range(2):
                    decays(b)
                    fill(1)
                    lower(b)
                    scores_gdn(b)
                pe.wait_ge(sem("a_silu"), 12)
                for b0 in (0, 2):
                    for e in range(2):
                        pe.wait_ge(sem(f"a_U{e}"), b0 // 2 + 1)
                        per_head_tile(("T0", b0 + e), lambda o_, h: TR(o_, g_U(e, h), ident))
                    natural_k_v(b0)
                    for n in range(1, LEVELS):
                        for e in range(2):
                            for c in range(2):
                                key = ("Y", b0 + e, n, c)
                                ps = tile_of(key)
                                pe.wait_ge(sem(f"a_LTm{e}"), LEVELS * (b0 // 2) + n + 1)
                                mix_freed(pe, ("T0", b0 + e) if n == 1 else ("X", b0 + e, n - 1, c))
                                for q in range(2):
                                    i = MM1(ps[:, q * P:(q + 1) * P], g_LTm[e][:, 2 * c + q, :], g_T(e, 2 * c + q))
                                done(i, key)
                        for e in range(2):
                            for c in range(2):
                                key = ("X", b0 + e, n, c)
                                ps = tile_of(key)
                                mix_freed(pe, ("Y", b0 + e, n, c))
                                hs = [(q, 2 * c + q) for q in range(2)]
                                if n < LEVELS - 1:
                                    for q, h in hs:
                                        MM1(ps[:, q * DH:(q + 1) * DH], g_U(e, h), level_half(g_Y[e][:, h, :], n, 0))
                                for q, h in hs:
                                    i = MM1(ps[:, P + q * DH:P + (q + 1) * DH], g_Y[e][:, h, :], level_half(g_U(e, h), n, 1))
                                done(i, key)
                    for b in (b0, b0 + 1):
                        e, ahead = b % 2, b + 2 < NT
                        if b > b0:
                            natural_k_v(b)
                            if ahead:
                                scores_gdn(b + 1)
                        if b:
                            mix_freed(pe, ("dS", b - 1))
                        else:
                            pe.wait_ge(sem("a_S0"), 1)
                        pe.wait_ge(sem("a_kbe"), b + 1)
                        per_head_tile(("ks", b), lambda o_, h: MM1(o_, g_kb[e][:, h, :], g_S[:, h, :]))
                        if ahead:
                            decays(b + 2)
                        else:
                            fill(1)
                        if b == 1:
                            fill(1)
                        mix_freed(pe, ("ks", b))
                        for c in range(2):
                            mix_freed(pe, ("X", b, LEVELS - 1, c))
                        per_head_tile(("new", b), lambda o_, h: MM1(o_, g_U(e, h), g_vb[:, h, :]))
                        if ahead:
                            lower(b + 2)
                        elif b == NT - 1:
                            fill(1)
                        pe.wait_ge(sem("a_qd"), b + 1)
                        mix_freed(pe, ("new", b))
                        mix_freed(pe, ("att", b))
                        ps = tile_of(("o", b))
                        for h in range(GH):
                            MM(ps[:, h * P:(h + 1) * P], g_S[:, h, :], tokens(aQ, h, b), start=True, stop=False)
                            i = MM(ps[:, h * P:(h + 1) * P], g_Y[e][:, h, :], g_att[e][:, h, :], start=False, stop=True)
                        done(i, ("o", b))
                        per_head_tile(("dS", b), lambda o_, h: MM1(o_, g_kd[:, h, :], g_Y[e][:, h, :]))
                    if b0 == 0:
                        scores_gdn(3)
                fill(8)

                def exact_product(key, matrix):
                    ps = tile_of(key)
                    pe.wait_ge(sem("x_lo"), EXACT.index(key) + 1)
                    MM(ps[:, :], matrix, oH[:, 4, :], start=True, stop=False)
                    done(MM(ps[:, :], matrix, oL[:, 4, :], start=False, stop=True), key)

                def head_means(*hs):
                    for h in hs:
                        ps = tile_of(("an", h))
                        pe.wait_ge(sem("an_sq"), h + 1)
                        done(MM(ps[:, :], ones[:, :], g_sq[:, h % 2, :], start=True, stop=True), ("an", h))

                do("gatea1", between=lambda i: head_means(*((0, 1), (), (2, 3), ())[i]))
                do("ya0", lambda i: pe.wait_ge(sem("a_olo"), 2 * i + 2))
                do("ya1")
                for n in ("cq", "ck", "cv"):
                    do(n)
                set_fill("gatec0", "gatec1")
                for n in ("cq", "ck", "cv"):
                    for i in range(4):
                        big_freed(pe, (n, i))
                pe.wait_ge(sem("c_bias"), 2)

                def hv(t, h):
                    return t[h % 2 * DH:h % 2 * DH + DH, h // 2, :]

                for h in range(SBH + 1):
                    if h < SBH:
                        for j in reversed(range(NT)):
                            n = S - j * P
                            ps = tile_of(("z", h, j))
                            done(MM(ps[:, 0:n], hv(cK, h)[:, j * P:(j + 1) * P], hv(cQ, h)[:, j * P:], start=True, stop=True), ("z", h, j))
                    if h < SBH:
                        fill(1)
                    if h >= 1:
                        g = h - 1
                        pe.wait_ge(sem("c_sp"), NT * h)
                        for j in range(NT):
                            n = S - j * P
                            ps = tile_of(("cs", g, j))
                            MM(ps[:, 0:n], hv(cK, g)[:, j * P:(j + 1) * P], hv(cQ, g)[:, j * P:], start=True, stop=False)
                            MM(ps[:, 0:P], idb[:, :], strictb[:, :], start=False, stop=False)
                            i = MM(ps[:, 0:n], consts[:, CNTL:CNTL + P], c_sp[g % 2][:, OFF[j]:OFF[j] + n], start=False, stop=j == NT - 1)
                            if j < NT - 1:
                                i = MM(ps[:, P:n], consts[:, CNTU:CNTU + P], c_sp[g % 2][:, OFF[j + 1]:OFF[j + 1] + n - P], start=False, stop=True)
                            done(i, ("cs", g, j))
                    if h % 2 == 0 and h:
                        i = h // 2 - 1
                        ps = tile_of(("cpv", i))
                        for j in range(NT):
                            for g in (h - 2, h - 1):
                                mix_freed(pe, ("cs", g, j))
                                r = MM(ps[g % 2 * DH:g % 2 * DH + DH, j * P:], cV[:, j, g * DH:(g + 1) * DH],
                                       c_A[g % 2][:, OFF[j]:OFF[j] + S - j * P], start=j == 0, stop=j == NT - 1)
                        done(r, ("cpv", i))
                fill(8)
                do("yc0", lambda i: [mix_freed(pe, ("cpv", q)) for q in (2 * i, 2 * i + 1)])
                do("yc1")
                do("dqk")

                def d_rotate(i):
                    exact_product(("drot", i), rot_r[:, P:2 * P])

                do("dv", between=d_rotate)
                do("dg")
                for i in range(4):
                    big_freed(pe, ("dv", i))
                set_fill("gated0", "gated1")
                pe.wait_ge(sem("d_rope"), 4)
                for h in range(4):
                    for j in range(NT):
                        n = S - j * P
                        ps = tile_of(("dz", h, j))
                        q, k = dQK[:, h // 2, :], dQK[:, 2 + h // 2, :]
                        r0 = h % 2 * DH
                        done(MM(ps[:, 0:n], k[r0:r0 + DH, j * P:(j + 1) * P], q[r0:r0 + DH, j * P:], start=True, stop=True), ("dz", h, j))
                    fill(1)
                    ps = tile_of(("dpv", h))
                    for j in range(NT):
                        mix_freed(pe, ("dz", h, j))
                        r = MM(ps[:, j * P:], dV[:, j, h * P:(h + 1) * P], dP[:, j, 0:S - j * P], start=j == 0, stop=j == NT - 1)
                    done(r, ("dpv", h))
                    fill(1)
                    exact_product(("dn", h), ones_r[:, :])
                do("yd0", lambda i: pe.wait_ge(sem("d_olo"), 2 * i + 2))
                do("yd1")
                def b_rotate(i):
                    exact_product(("brot", i), rot_r[:, 0:P])

                do("bq0")
                do("bk0", between=b_rotate)
                do("bq1")
                b_rotate(4)
                do("bk1")
                b_rotate(5)
                do("bv1", between=lambda i: b_rotate(6 + i))
                do("bv0")
                for g in range(2):
                    for i in range(4):
                        big_freed(pe, (f"bv{g}", i))
                set_fill("gateb0", "gateb1")
                pe.wait_ge(sem("b_rope"), 10)
                nexp = 0
                for i in range(len(WU) + 2):
                    if i < len(WU):
                        g, h, b0, nb, w = WU[i]
                        ps = tile_of(("sc", i))
                        hh = 3 * g + h
                        q, k = hv(bQ, hh), hv(bK, hh)
                        for b in range(nb):
                            bb = b0 + b
                            keys = slice(bb * P, (bb + 1) * P) if g else slice(max(bb - 1, 0) * P, max(bb - 1, 0) * P + 2 * P)
                            if g == 0 and bb == 0:
                                MM(ps[:, 0:P], q[:, 0:P], k[:, 0:P], start=True, stop=True)
                                r = MM(ps[:, P:2 * P], q[:, 0:P], k[:, 0:P], start=True, stop=True)
                            else:
                                r = MM(ps[:, b * w:(b + 1) * w], q[:, bb * P:(bb + 1) * P], k[:, keys], start=True, stop=True)
                        done(r, ("sc", i))
                    if 1 <= i <= len(WU):
                        nexp += WU[i - 1][3]
                        ps = tile_of(("pt", i - 1))
                        pe.wait_ge(sem("b_exp"), nexp)
                        for b in range(4):
                            r = TR(ps[:, b * P:(b + 1) * P], bP[:, (i - 1) % 2, b * P:(b + 1) * P], ident)
                        done(r, ("pt", i - 1))
                    if i in (0, 1, 3, 5, 8):
                        fill(1)
                    if i >= 2:
                        g, h, b0, nb, w = WU[i - 2]
                        hh = 3 * g + h
                        p0 = hh % 2 * DH
                        ps = tile_of(("wpv", i - 2))
                        mix_freed(pe, ("pt", i - 2))
                        pt = bPT[:, (i - 2) % 2, :]
                        vs = lambda b: bV[:, g, b, h * DH:(h + 1) * DH]
                        for b in range(nb):
                            o_ = ps[p0:p0 + DH, b * P:(b + 1) * P]
                            if g == 0:
                                MM(o_, vs(max(b0 + b - 1, 0)), pt[:, 2 * b * P:2 * b * P + P], start=True, stop=False)
                                r = MM(o_, vs(b0 + b), pt[:, 2 * b * P + P:2 * b * P + 2 * P], start=False, stop=True)
                            else:
                                r = MM(o_, vs(b), pt[:, b * P:(b + 1) * P], start=True, stop=True)
                        done(r, ("wpv", i - 2))
                for n in range(2):
                    for g in range(3):
                        ps = tile_of(("st", n, g))
                        for b in range(NT):
                            r = TR(ps[0:3, b * P:(b + 1) * P], (w_m, w_z)[n][:, g, b, :], ident)
                        done(r, ("st", n, g))
                fill(8)
                pe.wait_ge(sem("b_share"), 3)
                for t in range(5):
                    ps = tile_of(("bf", t))
                    for hh in (2 * t, 2 * t + 1):
                        if hh < 9:
                            g, h = hh // 3, hh % 3
                            r = MM(ps[hh % 2 * DH:hh % 2 * DH + DH, :], consts[0:3, CSEL + h * DH:CSEL + (h + 1) * DH], bFM[:, g, :], start=True, stop=True)
                    done(r, ("bf", t))
                do("yb0", lambda i: pe.wait_ge(sem("b_olo"), min(2 * i + 2, 5)))
                do("yb1")
                do("o0", lambda i: pe.wait_ge(sem("m_lo"), 2 * i + 2))
                do("o1")
                pre("pre2")
                for g in range(8):
                    do(f"up{g}", None if g else pre_split("pre2"))
                for hf in range(2):
                    job = JOB[f"dn{hf}"]
                    for i in range(16):
                        pe.wait_ge(sem("f_lo"), 16 * hf + i + 1)
                        unit(job, i)

        with nc.Fori(0, DEPTH) as l:
            with nc.Block() as block:
                build_layer(l, block)
            with nc.Block() as block:
                def clear(eng, part):
                    for s in list(sems.values())[part::5]:
                        eng.sem_clear(s)

                @block.sync
                def _(sp):
                    clear(sp, 0)

                @block.scalar
                def _(act):
                    clear(act, 1)

                @block.vector
                def _(dve):
                    clear(dve, 2)

                @block.tensor
                def _(pe):
                    clear(pe, 3)

                @block.gpsimd
                def _(pool):
                    clear(pool, 4)

        with nc.Block() as block:
            @block.sync
            def _(sp):
                sp.dma_start(out.rearrange("a (t p) d -> p (a t) d", p=P), xv).then_inc(stored, 16)
                sp.wait_ge(stored, 16)


_NAMES = ["x", "norm_pre_mix", "norm_post_mix", "norm_pre_mlp", "norm_post_mlp", "w_in", "conv_w", "a_log",
          "dt_bias", "gdn_norm", "ret_norm", "w_br_a", "w_br_b", "w_br_c", "w_br_d", "w_o", "w_mlp_in", "w_mlp_out"]


def small_weights(a):
    out = []
    for l in range(DEPTH):
        cols = lambda v: v.reshape(-1, P).T
        rows = lambda v: np.broadcast_to(v[None, :], (P, v.shape[0]))
        out.append(np.concatenate(
            [cols(a["norm_pre_mix"][l]), cols(a["norm_pre_mlp"][l]), cols(a["gdn_norm"][l]), cols(a["ret_norm"][l]),
             *[cols(a["conv_w"][l, tap]) for tap in range(4)], rows(a["a_log"][l]), rows(a["dt_bias"][l])], 1))
    return np.ascontiguousarray(np.stack(out))


def kernel(**inputs):
    import concourse.bacc as bacc
    from concourse.bass_utils import run_bass_kernel_spmd

    nc = bacc.Bacc("TRN2", target_bir_lowering=False, num_devices=1)
    arrays = {n: np.ascontiguousarray(inputs[n]) for n in _NAMES}
    arrays["small"] = small_weights(arrays)
    arrays["consts"] = shape_constants()
    arrays["tables"] = shape_tables()
    aps = {n: nc.dram_tensor(f"in_{n}", a.shape, mybir.dt.from_np(a.dtype), kind="ExternalInput").ap()
           for n, a in arrays.items()}
    out = nc.dram_tensor("out_0", (1, S, DM), F32, kind="ExternalOutput").ap()
    hybrid_kernel(nc, aps, out)
    r = run_bass_kernel_spmd(nc, [{f"in_{n}": a for n, a in arrays.items()}], core_ids=[0])
    return r.results[0]["out_0"]
```
